# Optimizing a Trainium2 kernel written in Bass

```python
import math
import jax, jax.numpy as jnp
from jax import lax
import numpy as np

D_MODEL = 1024
BATCH = 1
SEQ = 256
DEPTH = 2

GRID_W = 64
SSM_WIDTH = D_MODEL
SSM_GROUP = 16
SSM_GROUPS = SSM_WIDTH // SSM_GROUP
SSM_STATE = 64
SSM_DIRS = 2
LOG_STEP_MIN = math.log(1e-3)
LOG_STEP_MAX = math.log(1e-1)
N_HEADS = 16
N_KV_HEADS = 4
HEAD_DIM = D_MODEL // N_HEADS
Q_PER_KV = N_HEADS // N_KV_HEADS
ROPE_AXIS_DIM = HEAD_DIM // 2
ROPE_THETA = 10000.0
ATTN_BLOCK = 128
QKV_WIDTH = (N_HEADS + 2 * N_KV_HEADS) * HEAD_DIM
D_FF = ((8 * D_MODEL // 3 + 127) // 128) * 128
N_EXPERTS = 8
TOP_K = 2
D_FF_EXPERT = 7 * D_MODEL // 2
N_EVEN = (DEPTH + 1) // 2
N_ODD = DEPTH // 2
NORM_EPS = 1e-6

kernel_name = "hybrid_s5_axial_gqa_moe_encoder"

def rms_norm(x, gain):
    x32 = x.astype(jnp.float32)
    y = x32 * lax.rsqrt(jnp.mean(x32 * x32, axis=-1, keepdims=True) + NORM_EPS)
    return (y * gain.astype(jnp.float32)).astype(x.dtype)

def swiglu(h, w_gate, w_up, w_down):
    return (jax.nn.silu(h @ w_gate) * (h @ w_up)) @ w_down

def s5_mixer(h, w_in, lam_re, lam_im, log_step, b_re, b_im, c_re, c_im, d_skip, w_glu, w_out):
    bsz, seq, _ = h.shape
    u = h @ w_in
    uf = u.astype(jnp.float32).reshape(bsz, seq, SSM_GROUPS, SSM_GROUP)
    y = d_skip.astype(jnp.float32).reshape(SSM_GROUPS, SSM_GROUP) * uf

    def combine(e1, e2):
        a1r, a1i, b1r, b1i = e1
        a2r, a2i, b2r, b2i = e2
        return (a2r * a1r - a2i * a1i,
                a2r * a1i + a2i * a1r,
                a2r * b1r - a2i * b1i + b2r,
                a2r * b1i + a2i * b1r + b2i)

    for d in range(SSM_DIRS):
        lr = lam_re[d].astype(jnp.float32)
        li = lam_im[d].astype(jnp.float32)
        step = jnp.exp(log_step[d].astype(jnp.float32))[:, None]
        mag = jnp.exp(lr * step)
        ang = li * step
        ab_re = mag * jnp.cos(ang)
        ab_im = mag * jnp.sin(ang)
        nr, ni = ab_re - 1.0, ab_im
        den = lr * lr + li * li
        q_re = (nr * lr + ni * li) / den
        q_im = (ni * lr - nr * li) / den
        br = b_re[d].astype(jnp.float32)
        bi = b_im[d].astype(jnp.float32)
        bb_re = q_re[..., None] * br - q_im[..., None] * bi
        bb_im = q_re[..., None] * bi + q_im[..., None] * br
        bu_re = jnp.einsum('blgs,gps->blgp', uf, bb_re)
        bu_im = jnp.einsum('blgs,gps->blgp', uf, bb_im)
        a_re = jnp.broadcast_to(ab_re, bu_re.shape)
        a_im = jnp.broadcast_to(ab_im, bu_im.shape)
        _, _, xr, xi = lax.associative_scan(combine, (a_re, a_im, bu_re, bu_im),
                                            reverse=(d == 1), axis=1)
        y = y + (jnp.einsum('blgp,gsp->blgs', xr, c_re[d].astype(jnp.float32))
                 - jnp.einsum('blgp,gsp->blgs', xi, c_im[d].astype(jnp.float32)))
    y = y.reshape(bsz, seq, SSM_WIDTH).astype(h.dtype)
    g = jax.nn.gelu(y)
    g = g * jax.nn.sigmoid(g @ w_glu)
    return g @ w_out

def axial_rope_tables(seq):
    rows = seq // GRID_W
    freqs = ROPE_THETA ** (-jnp.arange(0, ROPE_AXIS_DIM, 2, dtype=jnp.float32) / ROPE_AXIS_DIM)
    n_f = freqs.shape[0]
    row_ang = jnp.arange(rows, dtype=jnp.float32)[:, None] * freqs
    col_ang = jnp.arange(GRID_W, dtype=jnp.float32)[:, None] * freqs
    ang = jnp.concatenate([
        jnp.broadcast_to(row_ang[:, None, :], (rows, GRID_W, n_f)),
        jnp.broadcast_to(col_ang[None, :, :], (rows, GRID_W, n_f))], axis=-1)
    ang = ang.reshape(seq, 2 * n_f)
    return jnp.cos(ang), jnp.sin(ang)

def apply_rope(x, cos, sin):
    x32 = x.astype(jnp.float32).reshape(*x.shape[:-1], HEAD_DIM // 2, 2)
    x1, x2 = x32[..., 0], x32[..., 1]
    c = cos[None, :, None, :]
    s = sin[None, :, None, :]
    out = jnp.stack([x1 * c - x2 * s, x1 * s + x2 * c], axis=-1)
    return out.reshape(x.shape).astype(x.dtype)

def axial_gqa_mixer(h, w_qkv, q_gain, k_gain, w_out):
    bsz, seq, _ = h.shape
    qkv = h @ w_qkv
    q = qkv[..., :N_HEADS * HEAD_DIM].reshape(bsz, seq, N_HEADS, HEAD_DIM)
    k = qkv[..., N_HEADS * HEAD_DIM:(N_HEADS + N_KV_HEADS) * HEAD_DIM].reshape(bsz, seq, N_KV_HEADS, HEAD_DIM)
    v = qkv[..., (N_HEADS + N_KV_HEADS) * HEAD_DIM:].reshape(bsz, seq, N_KV_HEADS, HEAD_DIM)
    q = rms_norm(q, q_gain)
    k = rms_norm(k, k_gain)
    cos, sin = axial_rope_tables(seq)
    q = apply_rope(q, cos, sin)
    k = apply_rope(k, cos, sin)
    n_blk = seq // ATTN_BLOCK
    qb = q.reshape(bsz, n_blk, ATTN_BLOCK, N_KV_HEADS, Q_PER_KV, HEAD_DIM).transpose(1, 0, 2, 3, 4, 5)
    scale = 1.0 / math.sqrt(HEAD_DIM)

    def attend(q_blk):
        s = jnp.einsum('bqkgd,bskd->bkgqs', q_blk, k, preferred_element_type=jnp.float32) * scale
        p = jax.nn.softmax(s, axis=-1).astype(v.dtype)
        return jnp.einsum('bkgqs,bskd->bqkgd', p, v)

    o = lax.map(attend, qb)
    o = o.transpose(1, 0, 2, 3, 4, 5).reshape(bsz, seq, N_HEADS * HEAD_DIM)
    return o @ w_out

def moe_swiglu(h, w_router, w_gate, w_up, w_down):
    bsz, seq, dm = h.shape
    hf = h.reshape(bsz * seq, dm)
    logits = (hf @ w_router).astype(jnp.float32)
    top_vals, top_idx = lax.top_k(logits, TOP_K)
    top_w = jax.nn.softmax(top_vals, axis=-1)
    gates = jnp.sum(jax.nn.one_hot(top_idx, N_EXPERTS, dtype=jnp.float32) * top_w[..., None], axis=1)
    gates = gates.astype(h.dtype)
    out = jnp.zeros_like(hf)
    for e in range(N_EXPERTS):
        out = out + gates[:, e:e + 1] * swiglu(hf, w_gate[e], w_up[e], w_down[e])
    return out.reshape(bsz, seq, dm)

def setup_inputs(seed: int = 0) -> dict:
    key = jax.random.key(seed)
    ks = iter(jax.random.split(key, 32))

    def nrm(shape, scale):
        return jax.random.normal(next(ks), shape, jnp.float32) * scale

    x = nrm((BATCH, SEQ, D_MODEL), 1.0)
    norm_gains = 1.0 + nrm((DEPTH, 4, D_MODEL), 0.1)
    ssm_w_in = nrm((N_EVEN, D_MODEL, SSM_WIDTH), D_MODEL ** -0.5)
    n_idx = jnp.arange(SSM_STATE, dtype=jnp.float32)
    ssm_lambda_re = -0.5 + nrm((N_EVEN, SSM_DIRS, SSM_GROUPS, SSM_STATE), 0.01)
    ssm_lambda_im = math.pi * n_idx + nrm((N_EVEN, SSM_DIRS, SSM_GROUPS, SSM_STATE), 0.01)
    ssm_log_step = jax.random.uniform(next(ks), (N_EVEN, SSM_DIRS, SSM_GROUPS), jnp.float32,
                                      LOG_STEP_MIN, LOG_STEP_MAX)
    b_scale = (2.0 * SSM_GROUP) ** -0.5
    c_scale = (2.0 * SSM_STATE) ** -0.5
    ssm_b_re = nrm((N_EVEN, SSM_DIRS, SSM_GROUPS, SSM_STATE, SSM_GROUP), b_scale)
    ssm_b_im = nrm((N_EVEN, SSM_DIRS, SSM_GROUPS, SSM_STATE, SSM_GROUP), b_scale)
    ssm_c_re = nrm((N_EVEN, SSM_DIRS, SSM_GROUPS, SSM_GROUP, SSM_STATE), c_scale)
    ssm_c_im = nrm((N_EVEN, SSM_DIRS, SSM_GROUPS, SSM_GROUP, SSM_STATE), c_scale)
    ssm_d = nrm((N_EVEN, SSM_WIDTH), 1.0)
    ssm_w_glu = nrm((N_EVEN, SSM_WIDTH, SSM_WIDTH), SSM_WIDTH ** -0.5)
    ssm_w_out = nrm((N_EVEN, SSM_WIDTH, D_MODEL), SSM_WIDTH ** -0.5)
    ffn_w_gate = nrm((N_EVEN, D_MODEL, D_FF), D_MODEL ** -0.5)
    ffn_w_up = nrm((N_EVEN, D_MODEL, D_FF), D_MODEL ** -0.5)
    ffn_w_down = nrm((N_EVEN, D_FF, D_MODEL), D_FF ** -0.5)
    attn_w_qkv = nrm((N_ODD, D_MODEL, QKV_WIDTH), D_MODEL ** -0.5)
    attn_q_gain = 1.0 + nrm((N_ODD, HEAD_DIM), 0.1)
    attn_k_gain = 1.0 + nrm((N_ODD, HEAD_DIM), 0.1)
    attn_w_out = nrm((N_ODD, N_HEADS * HEAD_DIM, D_MODEL), (N_HEADS * HEAD_DIM) ** -0.5)
    moe_w_router = nrm((N_ODD, D_MODEL, N_EXPERTS), D_MODEL ** -0.5)
    moe_w_gate = nrm((N_ODD, N_EXPERTS, D_MODEL, D_FF_EXPERT), D_MODEL ** -0.5)
    moe_w_up = nrm((N_ODD, N_EXPERTS, D_MODEL, D_FF_EXPERT), D_MODEL ** -0.5)
    moe_w_down = nrm((N_ODD, N_EXPERTS, D_FF_EXPERT, D_MODEL), D_FF_EXPERT ** -0.5)
    return {"x": x, "norm_gains": norm_gains,
            "ssm_w_in": ssm_w_in, "ssm_lambda_re": ssm_lambda_re, "ssm_lambda_im": ssm_lambda_im,
            "ssm_log_step": ssm_log_step, "ssm_b_re": ssm_b_re, "ssm_b_im": ssm_b_im,
            "ssm_c_re": ssm_c_re, "ssm_c_im": ssm_c_im, "ssm_d": ssm_d,
            "ssm_w_glu": ssm_w_glu, "ssm_w_out": ssm_w_out,
            "ffn_w_gate": ffn_w_gate, "ffn_w_up": ffn_w_up, "ffn_w_down": ffn_w_down,
            "attn_w_qkv": attn_w_qkv, "attn_q_gain": attn_q_gain, "attn_k_gain": attn_k_gain,
            "attn_w_out": attn_w_out,
            "moe_w_router": moe_w_router, "moe_w_gate": moe_w_gate, "moe_w_up": moe_w_up,
            "moe_w_down": moe_w_down}

def reference(x, norm_gains,
              ssm_w_in, ssm_lambda_re, ssm_lambda_im, ssm_log_step, ssm_b_re, ssm_b_im,
              ssm_c_re, ssm_c_im, ssm_d, ssm_w_glu, ssm_w_out,
              ffn_w_gate, ffn_w_up, ffn_w_down,
              attn_w_qkv, attn_q_gain, attn_k_gain, attn_w_out,
              moe_w_router, moe_w_gate, moe_w_up, moe_w_down):
    h = x
    for i in range(DEPTH):
        j = i // 2
        g = norm_gains[i]
        if i % 2 == 0:
            mix = s5_mixer(rms_norm(h, g[0]), ssm_w_in[j], ssm_lambda_re[j], ssm_lambda_im[j],
                           ssm_log_step[j], ssm_b_re[j], ssm_b_im[j], ssm_c_re[j], ssm_c_im[j],
                           ssm_d[j], ssm_w_glu[j], ssm_w_out[j])
            h = h + rms_norm(mix, g[1])
            ff = swiglu(rms_norm(h, g[2]), ffn_w_gate[j], ffn_w_up[j], ffn_w_down[j])
            h = h + rms_norm(ff, g[3])
        else:
            mix = axial_gqa_mixer(rms_norm(h, g[0]), attn_w_qkv[j], attn_q_gain[j],
                                  attn_k_gain[j], attn_w_out[j])
            h = h + rms_norm(mix, g[1])
            ff = moe_swiglu(rms_norm(h, g[2]), moe_w_router[j], moe_w_gate[j], moe_w_up[j],
                            moe_w_down[j])
            h = h + rms_norm(ff, g[3])
    return h


_drawn_inputs = setup_inputs


def setup_inputs(seed=0):
    import zlib

    import numpy as np

    out = dict(_drawn_inputs(seed))
    spreads = {}
    factors = {}
    for name, (base, spread) in spreads.items():
        noise = np.random.default_rng([zlib.crc32(name.encode()), seed]).standard_normal(out[name].shape)
        drawn = base * np.exp(spread * noise) if base else spread * noise
        out[name] = __import__('jax').numpy.asarray(drawn.astype(out[name].dtype))
    for name, factor in factors.items():
        out[name] = (out[name] * factor).astype(out[name].dtype)
    return out
```

```python
import concourse.bass as bass
from concourse import mybir
from contextlib import ExitStack

WIDTHS = (64, 96, 144, 256)


def hybrid_trunk(nc, x_in, norm_gains, ssm_w_in, ssm_lambda_re, ssm_lambda_im, ssm_log_step,
                 ssm_b_re, ssm_b_im, ssm_c_re, ssm_c_im, ssm_d, ssm_w_glu, ssm_w_out,
                 ffn_w_gate, ffn_w_up, ffn_w_down, attn_w_qkv, attn_q_gain, attn_k_gain,
                 attn_w_out, moe_w_router, moe_w_gate, moe_w_up, moe_w_down,
                 rope_cos, rope_sin, out):
    f32, i32 = mybir.dt.float32, mybir.dt.int32
    ALU, ACT, AX = mybir.AluOpType, mybir.ActivationFunctionType, mybir.AxisListType
    MUL, ADD, SUB = ALU.mult, ALU.add, ALU.subtract

    P = 128
    SEQ, D = x_in.shape[1], x_in.shape[2]
    NT, KD = SEQ // P, D // P
    DIRS, GROUPS, ST = ssm_lambda_re.shape[1:]
    GC = D // GROUPS
    CH = P // GC
    NC = SEQ // CH
    GP = GROUPS // 2
    DG = DIRS * GP
    NPOW = CH + 1
    SB = 4
    NB = DG // SB
    EPS = 1e-6
    IW = 256
    ITEM = KD * IW
    SLOTS = 21
    FF_STEPS = ffn_w_gate.shape[2] // IW
    EXP, EFF = moe_w_gate.shape[1], moe_w_gate.shape[3]
    EX_STEPS = EFF // IW
    HALF = EX_STEPS // 2
    QKV = attn_w_qkv.shape[2]
    NH, HD = D // attn_q_gain.shape[1], attn_q_gain.shape[1]
    NKV = (QKV // HD - NH) // 2
    HPK = NH // NKV
    QK = NH + NKV
    assert HALF * 3 == SLOTS and EX_STEPS == 2 * HALF and CH * GC == P and NC * CH == SEQ

    ctx = ExitStack()
    with ctx:
        def sb(name, shape, dt=f32):
            return ctx.enter_context(nc.sbuf_tensor(name, shape, dt))

        sems = {}

        def sg(name):
            if name not in sems:
                sems[name] = ctx.enter_context(nc.semaphore(name))
            return sems[name]

        BIGW = 53056
        big = sb("big", [P, BIGW])
        cnt_i = sb("cnt_i", [1, EXP], i32)
        ps = ctx.enter_context(nc.psum_tensor("ps", [P, 8, 512], f32))
        x_scr = nc.dram_tensor("x_scr", (P, NT * D), f32, kind="Internal").ap()
        k_scr = nc.dram_tensor("k_scr", (GROUPS, GC, 15 * GC), f32, kind="Internal").ap()

        def at(off, *shape):
            n = 1
            for s in shape:
                n *= s
            assert off + n <= BIGW
            v = big[:, off:off + n]
            if len(shape) == 1:
                return v
            names = "abcd"[:len(shape)]
            return v.rearrange(f"p ({' '.join(names)}) -> p {' '.join(names)}",
                               **{names[i]: shape[i] for i in range(len(shape) - 1)})

        TOP = BIGW - 448
        ident = at(TOP, P)
        gcol = at(TOP + 128, 64)
        ssq = at(TOP + 192, 2)
        msq = at(TOP + 194, 2)
        rstd = at(TOP + 196, 2)
        nhalf = at(TOP + 198, 48)
        hms = at(TOP + 246, 48)
        hrs = at(TOP + 294, 48)
        small = at(TOP + 342, 106)

        def slot(n):
            return at((n % SLOTS) * ITEM, KD, IW)

        def slot_down(n):
            return at((n % SLOTS) * ITEM, 2, D)

        RA, RDS, RC, REZ, RB = 0, 8192, 20480, 28672, 36864
        X_, HT, N1, R8_ = 45056, 47104, 49152, 51200
        x = at(X_, NT, D)
        hT = at(HT, KD, SEQ)
        nat = at(N1, NT, D)
        nat_flat = at(N1, NT * D)
        post_gain = at(R8_, D)
        w_in = at(RA, 4, KD, IW)
        xbd = at(RA, 2, DG, 2, NC)
        u_grp = at(RA, GROUPS, CH, GC)
        u_tok = at(RB, CH, D)
        w_glu = at(RB, 4, KD, IW)
        w_out0 = at(REZ, 4, KD, IW)
        bbar = at(RDS, 2, DG + 1, GC)
        cP = at(RDS + 2080, 2, DG, GC)
        S_ = at(RDS + 4128, 2, DG, NC)
        bP = at(RDS + 4128, 2, DG, GC)
        pw = at(RDS + 8224, 2, NPOW, DG)
        pd = at(RDS + 9376, 2, NPOW, DG)
        def tmp(n):
            assert n < 27
            return at(RDS + 10528 + 64 * n, DG)
        yg = at(RDS + 4128, GROUPS, NC)
        gT = at(RDS + 4128 + 2048, KD, SEQ)
        mT = hT
        wt = [at(RC + 1024 * i, 2, SB, P) for i in range(2)]
        wm = [at(RC + 2048 + 1024 * i, SB, 2, P) for i in range(2)]
        kall = at(RC, 2, 8, 15, GC)
        kzero = at(RC + 3840, 2, 8, GC)
        mtmp = [at(RC + 5800 + 576 * i, SB * NPOW * GC) for i in range(4)]
        toe = at(RC, GROUPS, P)
        g_tok = at(RC, CH, D)
        ec = at(REZ, 2, DG, NC)
        zz = at(REZ + 4096, 2, DG, NC)
        vv = [at(REZ + 4096 + 1152 * i, 2, SB, NPOW, GC) for i in range(2)]
        raw_b = at(RB, 2, P, GC)
        raw_c = at(RB + 4096, 2, GC, P)
        raw_l = at(REZ, 4, P)
        raw_g = at(REZ + 512, P)
        raw_s = at(REZ + 640, 2)
        raw_d = at(REZ + 704, GC)
        raw_dx = at(REZ + 768, CH, GC)
        uc = at(HT, GROUPS, NC)
        ud = at(N1, GROUPS, NC)
        tmp8 = at(N1, DG, NC)
        r8t = at(R8_, GP, NC)
        sig = at(N1, KD, SEQ)
        dcol = at(52224, GROUPS)

        sil = [at(43008 + 256 * i, SEQ) for i in range(2)]
        hid = [at(43520 + 256 * i, SEQ) for i in range(2)]
        qkv = at(43008, NT, QKV)
        kT = at(46080, NKV, SEQ)
        qT = hT
        k_dup = at(N1, NT, NKV, 2, HD)
        rope_m = [at(HT + 512 * i, NH, HD // 2) for i in range(4)]
        o_nat = qkv
        prob = [at(N1 + 512 * i, 2, SEQ) for i in range(2)]
        probT = [at(N1 + 1024 + 512 * i, 2, NT, P) for i in range(2)]
        rope_raw = at(52224, 2, NT, HD // 2)
        qk_gain = at(52352, 2, HD)
        rope_t = at(N1 + 1280, 2, 4, NT, HD // 2)
        nmax, psum_, prcp = (small[:, 32 * i:32 * i + 32] for i in range(3))
        UNITS = NT * NH // 2
        h_moe = nat
        acc = x
        xg = hT
        yT = hT
        y_lo = at(43008, D)
        y_hi = at(HT, D)
        sel_g = at(43008, NT, SEQ)
        sel = at(44032, NT, SEQ)
        sel_gT = at(44544, NT, NT, P)
        m_sil = [at(51200 + 256 * i, SEQ) for i in range(2)]
        m_hid = [at(51712 + 256 * i, SEQ) for i in range(2)]
        iota = at(52224, SEQ)
        iota_i = at(43700, SEQ).bitcast(i32)
        rank = at(52480, NT, EXP + 1)
        chosen = at(52498, NT, EXP + 1)
        gate = at(52516, NT, EXP + 1)
        w_router = gcol.rearrange("p (k e) -> p k e", k=KD)
        upper = at(43008, P)
        ones = at(43136, P)
        lower_e = at(43264, EXP, EXP)
        gt_ = at(43328, NT, EXP, EXP)
        eq_ = at(43456, NT, EXP, EXP)
        logit = at(43584, NT, EXP)
        lshift = at(43600, NT, EXP)
        wexp = at(43616, NT, EXP)
        beats = at(43632, NT, EXP)
        lmax = at(43648, NT)
        wsum = at(43650, NT)
        last_gain = at(((3 * FF_STEPS + QKV // IW + D // IW + EXP * 3 * EX_STEPS) % SLOTS) * ITEM, D)
        SEL_AT = 3
        CHUNKS = EFF // P
        EI = 3 * EX_STEPS

        block = ctx.enter_context(nc.Block())
        w_in_v = [w[0].rearrange("(k p) n -> p k n", p=P) for w in (ssm_w_in, ssm_w_glu, ssm_w_out)]

        def cols(w, j):
            return w.rearrange("(k p) n -> p k n", p=P)[:, :, j * IW:(j + 1) * IW]

        def rows(w, j):
            return w[j * IW:(j + 1) * IW, :].rearrange("(f p) n -> p f n", p=P)

        items = []
        for j in range(FF_STEPS):
            items += [cols(ffn_w_gate[0], j), cols(ffn_w_up[0], j), rows(ffn_w_down[0], j)]
        ITEM_QKV = len(items)
        items += [cols(attn_w_qkv[0], j) for j in range(QKV // IW)]
        ITEM_WO = len(items)
        items += [cols(attn_w_out[0], j) for j in range(D // IW)]
        ITEM_MOE = len(items)
        full = [f"item_in_slot{n}" for n in range(SLOTS)]

        def item_full(n):
            return sg(full[n % SLOTS]), 16 * (n // SLOTS + 1)

        def item_read(n):
            if n < ITEM_QKV:
                return sg("gu_done" if n % 3 < 2 else "down_done"), 2 * (n // 3) + 2
            return sg("proj_done"), n - ITEM_QKV + 1

        def moe_item_full(e, m):
            n = ITEM_MOE + m
            return sg(full[n % SLOTS]), 16 * (n // SLOTS + 1) + 32 * e

        @block.sync
        def _(sp):
            for t in range(NT):
                sp.dma_start(x[:, t, :], x_in[0, t * P:(t + 1) * P, :]).then_inc(sg(f"x_in{t}"), 16)
            lam_v = [w[0].rearrange("d (g a) p -> (d g) (a p)", a=2) for w in (ssm_lambda_re, ssm_lambda_im)]
            for i in range(2):
                sp.dma_start(raw_l[0:DG, i, :], lam_v[i]).then_inc(sg("lam_in"), 16)
            sp.dma_start(raw_s[0:DG, :], ssm_log_step[0].rearrange("d (g a) -> (d g) a", a=2)).then_inc(sg("lam_in"), 16)
            sp.dma_start(raw_g[0:64, :], norm_gains.rearrange("l n (k p) -> (l n k) p", p=P)).then_inc(sg("gain_in"), 16)
            sp.dma_start(raw_d[0:GROUPS, :], ssm_d[0].rearrange("(g s) -> g s", s=GC)).then_inc(sg("gain_in"), 16)
            for i, w in enumerate((ssm_b_re, ssm_b_im)):
                sp.dma_start(raw_b[0:DG, i, :, :], w[0].rearrange("d (g a) p s -> (d g) (a p) s", a=2)).then_inc(sg("b_in"), 16)
            for i, w in enumerate((ssm_c_re, ssm_c_im)):
                for a in range(2):
                    sp.dma_start(raw_c[0:DG, i, :, a * ST:(a + 1) * ST],
                                 w[0].rearrange("d (g a) s p -> a (d g) s p", a=2)[a]).then_inc(sg("c_in"), 16)
            for i in range(4):
                sp.dma_start(w_in[:, i, :, :], w_in_v[0][:, :, i * IW:(i + 1) * IW]).then_inc(sg(f"mix_w{i}"), 16)
            for t in range(NT):
                sp.wait_ge(sg("u_act"), t + 1)
                sp.wait_ge(sg("u_dve"), t + 1)
                for s in range(CH):
                    sp.dma_start(u_tok[16 * t:16 * t + 16, s, :], nat[s:P:CH, t, :]).then_inc(sg("u_tok_in"), 16)
            sp.wait_ge(sg("u_grp_ready"), 2)
            for i in range(4):
                sp.dma_start(w_glu[:, i, :, :], w_in_v[1][:, :, i * IW:(i + 1) * IW]).then_inc(sg(f"mix_w{i}"), 16)
            sp.wait_ge(sg("k_final"), 1)
            k_w = k_scr.rearrange("(q j a) s x -> j a s q x", j=SB, a=2)
            for j in range(SB):
                for a in range(2):
                    sp.dma_start(k_w[j, a], kall[32 * j:32 * j + GC, a, :, :, :].rearrange("p q t o -> p q (t o)")).then_inc(sg("k_stored"), 16)
            sp.wait_ge(sg("k_stored"), 16 * 2 * SB)
            sp.wait_ge(sg("y_state"), NB)
            for s in range(CH):
                sp.dma_start(toe[GC * s:GC * (s + 1), :, :],
                             k_scr.rearrange("g s x -> s g x")[:, :, (CH - 1 - s) * GC:(CH - 1 - s) * GC + P]).then_inc(sg("toe_in"), 16)
            for i in range(4):
                sp.dma_start(w_out0[:, i, :, :], w_in_v[2][:, :, i * IW:(i + 1) * IW]).then_inc(sg(f"mix_w{i}"), 16)
            sp.dma_start(post_gain[:, :], norm_gains[0, 1:2, :].to_broadcast([P, D])).then_inc(sg("post_gain_in"), 16)
            for n, src in enumerate(items):
                if n == 4:
                    sp.wait_ge(sg("m_ready"), 8)
                if n == 10:
                    sp.wait_ge(sg("gT_tr"), 4)
                if n == 14:
                    sp.wait_ge(sg("out0_done"), 1)
                if n >= SLOTS:
                    sp.wait_ge(*item_read(n - SLOTS))
                dst = slot_down(n) if (n < ITEM_QKV and n % 3 == 2) else slot(n)
                sp.dma_start(dst, src).then_inc(sg(full[n % SLOTS]), 16)
                if n == SLOTS - 1:
                    sp.wait_ge(sg("x_done"), 2)
                    sp.dma_start(post_gain[:, :], norm_gains[0, 3:4, :].to_broadcast([P, D])).then_inc(sg("post_gain_in"), 16)
                    for i, w in enumerate((rope_cos, rope_sin)):
                        sp.dma_start(rope_raw[:, i], w.rearrange("(t p) f -> p t f", p=P)).then_inc(sg("rope_in"), 16)
                    for i, w in enumerate((attn_q_gain, attn_k_gain)):
                        sp.dma_start(qk_gain[:, i], w[0:1, :].to_broadcast([P, HD])).then_inc(sg("rope_in"), 16)
            def moe_item(e, m):
                j, kind = divmod(m, 3)
                js = slice(j * IW, (j + 1) * IW)
                if kind < 2:
                    w = (moe_w_gate, moe_w_up)[kind][0, bass.ds(e, 1), :, js].rearrange("e (k p) n -> p (e k) n", p=P)
                    dst = slot(ITEM_MOE + m)
                else:
                    w = moe_w_down[0, bass.ds(e, 1), js, :].rearrange("e (f p) n -> p (e f) n", p=P)
                    dst = slot_down(ITEM_MOE + m)
                sp.dma_start(dst, w).then_inc(sg(full[(ITEM_MOE + m) % SLOTS]), 16)

            def moe_wait_read(e, m):
                prev = m - SLOTS + (EI if m < SLOTS else 0)
                expert = e - 1 if m < SLOTS else e
                sp.wait_ge(sg("moe_gu" if prev % 3 < 2 else "moe_down"), CHUNKS * expert + 2 * (prev // 3) + 2)

            sp.wait_ge(sg("x_done"), 4)
            sp.dma_start(x_scr[:, :], x.rearrange("p t d -> p (t d)")).then_inc(sg("x_stored"), 16)
            sp.dma_start(post_gain[:, :], norm_gains[1, 1:2, :].to_broadcast([P, D])).then_inc(sg("post_gain_in"), 16)
            qkv_m = ITEM_WO - (ITEM_MOE - SLOTS)
            for m in range(0, qkv_m):
                sp.wait_ge(*item_read(ITEM_MOE - SLOTS + m))
                moe_item(0, m)
            sp.wait_ge(sg("oT_tr"), 4)
            sp.wait_ge(sg("x_stored"), 16)
            sp.dma_start(x.rearrange("p t d -> p (t d)"), x_scr[:, :]).then_inc(sg("x_back"), 16)
            sp.dma_start(w_router, moe_w_router[0].rearrange("(k p) e -> p k e", p=P)).then_inc(sg("router_in"), 16)
            for m in range(qkv_m, SLOTS):
                sp.wait_ge(*item_read(ITEM_MOE - SLOTS + m))
                moe_item(0, m)
            sp.wait_ge(sg("x_done"), 6)
            sp.dma_start(post_gain[:, :], norm_gains[1, 2:3, :].to_broadcast([P, D])).then_inc(sg("post_gain_in"), 16)
            sp.dma_start(x_scr[:, :], x.rearrange("p t d -> p (t d)")).then_inc(sg("x_stored"), 16)
            for m in range(SLOTS, EI):
                moe_wait_read(0, m)
                moe_item(0, m)
            with sp.Fori(1, EXP) as e:
                for m in range(EI):
                    moe_wait_read(e, m)
                    moe_item(e, m)
            sp.wait_ge(sg("moe_gu"), CHUNKS * (EXP - 1) + 2 * HALF + 2)
            sp.dma_start(last_gain[:, :], norm_gains[1, 3:4, :].to_broadcast([P, D])).then_inc(sg("last_gain_in"), 16)
            sp.wait_ge(sg("gather_mm"), 4 * EXP)
            sp.wait_ge(sg("x_stored"), 32)
            sp.dma_start(nat.rearrange("p t d -> p (t d)"), x_scr[:, :]).then_inc(sg("x_back"), 16)
            for t in range(NT):
                sp.wait_ge(sg("y_final"), t + 1)
                sp.dma_start(out[0, t * P:(t + 1) * P, :], acc[:, t, :]).then_inc(sg("out_stored"), 16)
            sp.wait_ge(sg("out_stored"), 16 * NT)

        @block.gpsimd
        def _(pool):
            step = [0]

            def link(ins):
                step[0] += 1
                ins.then_inc(sg("pool_step"), 1)
                pool.wait_ge(sg("pool_step"), step[0])

            link(pool.memset(ident[:, :], 0.0))
            pool.affine_select(out=ident[:, :], in_=ident[:, :], compare_op=ALU.not_equal, fill=1.0,
                               base=0, pattern=[[-1, P]], channel_multiplier=1).then_inc(sg("ident_ready"), 1)
            pool.memset(bbar[:, :, DG, :], 0.0).then_inc(sg("bbar_pad"), 1)
            link(pool.memset(nhalf[:, :], -0.5))

            def rstd_of(n):
                pool.wait_ge(sg("ms_ready"), n + 1)
                pool.tensor_tensor(rstd[:, :], msq[:, :], nhalf[:, 0:2], ALU.pow).then_inc(sg("rstd_ready"), 1)

            rstd_of(0)
            pool.wait_ge(sg("bbar_ready"), 1)
            for b in range(NB):
                d, q = divmod(b, NB // 2)
                s = slice(SB * b, SB * (b + 1))
                pt = pd[:, :, 1:NPOW, s] if d == 0 else pw[:, :, 0:CH, s]
                if b >= 1:
                    pool.wait_ge(sg("wt_ready"), b)
                for i, (bi, ti) in enumerate(((0, 1), (1, 0))):
                    pool.tensor_tensor(mtmp[2 + i][:, 0:SB * P].rearrange("p (g s i) -> p g s i", g=SB, s=CH),
                                       bbar[:, bi, s, :].unsqueeze(2).to_broadcast([P, SB, CH, GC]),
                                       pt[:, ti].rearrange("p s g -> p g s").unsqueeze(3).to_broadcast([P, SB, CH, GC]),
                                       MUL).then_inc(sg("wt_pool"), 1)
            for b in range(NB):
                d, q = divmod(b, NB // 2)
                s = slice(SB * b, SB * (b + 1))
                pt = pw[:, :, :, s] if d == 0 else pd[:, :, :, s]
                pool.wait_ge(sg("wt_ready"), NB) if b == 0 else pool.wait_ge(sg("v_ready"), b)
                for i, (ci, ti) in enumerate(((0, 1), (1, 0))):
                    pool.tensor_tensor(mtmp[2 + i].rearrange("p (g s i) -> p g s i", g=SB, s=NPOW),
                                       cP[:, ci, s, :].unsqueeze(2).to_broadcast([P, SB, NPOW, GC]),
                                       pt[:, ti].rearrange("p s g -> p g s").unsqueeze(3).to_broadcast([P, SB, NPOW, GC]),
                                       MUL).then_inc(sg("v_pool"), 1)
            rstd_of(1)
            rstd_of(2)
            rstd_of(3)
            rstd_of(4)
            pool.wait_ge(sg("head_ms"), 1)
            pool.tensor_tensor(hrs[:, 0:NT * QK], hms[:, 0:NT * QK], nhalf[:, 0:NT * QK], ALU.pow).then_inc(sg("head_rstd"), 1)
            rstd_of(5)
            pool.wait_ge(sg("x_done"), 6)
            link(pool.memset(upper[:, :], 1.0))
            link(pool.affine_select(out=upper[:, :], in_=upper[:, :], compare_op=ALU.is_gt, fill=0.0,
                                    base=0, pattern=[[1, P]], channel_multiplier=-1))
            link(pool.memset(ones[:, :], 1.0))
            link(pool.memset(lower_e[:, :, :], 1.0))
            link(pool.affine_select(out=lower_e[:, :, :], in_=lower_e[:, :, :], compare_op=ALU.is_gt, fill=0.0,
                                    base=0, pattern=[[1, EXP], [-1, EXP]], channel_multiplier=0))
            for v in (rank, chosen, gate):
                link(pool.memset(v[:, :, EXP:EXP + 1], 0.0))
            link(pool.iota(iota_i, pattern=[[1, SEQ]], base=0, channel_multiplier=0))
            pool.tensor_copy(iota[:, :], iota_i).then_inc(sg("route_consts"), 1)
            rstd_of(6)
            pool.wait_ge(sg("x_stored"), 32)
            pool.wait_ge(sg("nat_ready"), 8)
            pool.wait_ge(sg("ssq_ready"), 14)
            pool.memset(acc[:, :, :], 0.0).then_inc(sg("acc_done"), 1)
            rstd_of(7)

        @block.scalar
        def _(act):
            step = [0]

            def link(ins):
                step[0] += 1
                ins.then_inc(sg("act_step"), 1)
                act.wait_ge(sg("act_step"), step[0])

            def nat_sq(t, src):
                return nat[:, t, :] if len(src.shape) == 2 else nat[:, t, :].rearrange("p (a b) -> p a b", a=2)

            def sum_squares_x(done):
                for t in range(NT):
                    act.wait_ge(sg("x_done"), done - 1 + t)
                    act.activation(nat[:, t, :], x[:, t, :], ACT.Square, accum_out=ssq[:, t:t + 1]).then_inc(sg("ssq_ready"), 1)

            def sum_squares(sources):
                for t, src in enumerate(sources):
                    ins = act.activation(nat_sq(t, src), src, ACT.Square, accum_out=ssq[:, t:t + 1])
                    ins.then_inc(sg("ssq_ready"), 1)

            def hT_half(n, gain):
                for b in (0, 2):
                    act.wait_ge(sg("tr_ready"), 4 * n + b + 1)
                    for k in (2 * b, 2 * b + 1):
                        ins = act.activation(hT[:, k, :], ps[:, b, (k % 2) * SEQ:(k % 2 + 1) * SEQ], ACT.Copy,
                                             scale=1.0 if gain is None else gcol[:, gain * 8 + k:gain * 8 + k + 1])
                    ins.then_inc(sg("hT_ready"), 1)

            for t in range(NT):
                act.wait_ge(sg(f"x_in{t}"), 16)
            sum_squares([x[:, t, :] for t in range(NT)])
            act.wait_ge(sg("lam_copied"), 1)
            act.activation(tmp(2), ps[:, 4, 128:192], ACT.Exp).then_inc(sg("step_ready"), 1)
            act.wait_ge(sg("ang_ready"), 1)
            act.activation(tmp(4), tmp(3), ACT.Exp).then_inc(sg("mag_ready"), 1)
            act.activation(tmp(7), tmp(5), ACT.Sin).then_inc(sg("mag_ready"), 1)
            act.activation(tmp(8), tmp(6), ACT.Sin).then_inc(sg("mag_ready"), 1)
            for i in range(2):
                act.wait_ge(sg("bc_tr"), 2 * i + 2)
                bank = 5 if i == 0 else 6
                for h in range(2):
                    act.activation(bP[:, i, :, 8 * h:8 * h + 8].rearrange("p g s -> p s g"),
                                   ps[:, 5 + h, :].rearrange("p (s g) -> p s g", g=DG), ACT.Copy).then_inc(sg("bc_out"), 1)
            for i in range(2):
                act.wait_ge(sg("bc_tr"), 4 + 2 * i + 2)
                for h in range(2):
                    act.activation(cP[:, i, :, 8 * h:8 * h + 8].rearrange("p g s -> p s g"),
                                   ps[:, 5 + h, :].rearrange("p (s g) -> p s g", g=DG), ACT.Copy).then_inc(sg("bc_out"), 1)
            act.wait_ge(sg("gain_tr"), 1)
            act.activation(gcol[:, :], ps[:, 7, 0:64], ACT.Copy).then_inc(sg("gcol_ready"), 1)
            act.wait_ge(sg("gcol_ready"), 1)
            hT_half(0, 0)
            act.wait_ge(sg("pw_ready"), 1)
            for k in range(NPOW):
                ins = act.activation(pd[:, :, k, :], pw[:, :, CH - k, :], ACT.Copy)
            ins.then_inc(sg("pd_ready"), 1)
            for t in range(NT):
                act.wait_ge(sg("u_mm"), t + 1)
                act.activation(nat[:, t, 0:512], ps[:, 2 * t, :], ACT.Copy).then_inc(sg("u_act"), 1)
            act.wait_ge(sg("u_tok_in"), 16 * NT * CH)
            GA = 28
            act.activation(u_grp[0:NC, 0:GA].rearrange("p g s i -> p s g i"),
                           u_tok[0:NC, :, 0:GA * GC].rearrange("p s (g i) -> p s g i", i=GC), ACT.Copy).then_inc(sg("u_grp_ready"), 1)
            for b in range(4):
                act.wait_ge(sg("uc_tr"), b + 1)
                act.activation(uc[:, 16 * b:16 * b + 16, :].rearrange("p g c -> p (g c)"), ps[:, b, :], ACT.Copy).then_inc(sg("uc_ready"), 1)
            for b in range(NB):
                if b >= 2:
                    act.wait_ge(sg("s_mm"), b - 1)
                for h in range(2):
                    act.wait_ge(sg("w_tr"), 2 * b + h + 1)
                    act.activation(wm[b % 2][:, 2 * h:2 * h + 2, :, :].rearrange("p g r q -> p (g r q)"),
                                   ps[:, 2 * (b % 2) + h, :], ACT.Copy).then_inc(sg("w_out_act"), 1)
                if b >= 1:
                    act.wait_ge(sg("s_mm"), b)
                    act.activation(S_[:, :, SB * (b - 1):SB * b, :].rearrange("p r g c -> p r (g c)"),
                                   ps[:, 4 + (b - 1) % 2, 0:256].rearrange("p (r x) -> p r x", r=2), ACT.Copy).then_inc(sg("s_out"), 1)
            act.wait_ge(sg("s_mm"), NB)
            act.activation(S_[:, :, SB * (NB - 1):SB * NB, :].rearrange("p r g c -> p r (g c)"),
                           ps[:, 4 + (NB - 1) % 2, 0:256].rearrange("p (r x) -> p r x", r=2), ACT.Copy).then_inc(sg("s_out"), 1)
            for b in range(NB):
                d, q = divmod(b, NB // 2)
                act.wait_ge(sg("k_mm"), b + 1)
                lo = CH - 1 if d == 0 else 0
                if d == 0:
                    ins = act.activation(kall[:, :, q, CH - 1:15, :],
                                         ps[:, 4 + 2 * (b % 2):6 + 2 * (b % 2), 0:P].rearrange("p a (t o) -> p a t o", o=GC), ACT.Copy)
                else:
                    ins = act.activation(kall[:, :, q, 0:CH - 1, :],
                                         ps[:, 4 + 2 * (b % 2):6 + 2 * (b % 2), 0:(CH - 1) * GC].rearrange("p a (t o) -> p a t o", o=GC), ACT.Copy)
                if d == 1:
                    ins = act.activation(kzero[:, :, q, :],
                                         ps[:, 4 + 2 * (b % 2):6 + 2 * (b % 2), (CH - 1) * GC:CH * GC], ACT.Copy)
                ins.then_inc(sg("k_out"), 1)
            for b in range(4):
                act.wait_ge(sg("y_sum"), b + 1)
                act.activation(yg[:, 16 * b:16 * b + 16, :], yg[:, 16 * b:16 * b + 16, :], ACT.Gelu_apprx_tanh).then_inc(sg("gelu"), 1)
            for r in range(0, 16, 2):
                act.wait_ge(sg("g_tr"), r + 1)
                act.activation(g_tok[0:NC, :, 64 * r:64 * r + 64].rearrange("c t (g o) -> c g t o", o=GC),
                               ps[0:NC, 4 + r % 4, :].rearrange("c (g t o) -> c g t o", g=4, t=CH), ACT.Copy).then_inc(sg("g_tok_act"), 1)
            for b in (0, 2):
                act.wait_ge(sg("gT_tr"), b + 1)
                act.activation(gT[:, 2 * b:2 * b + 2, :].rearrange("p k (c t) -> p k t c", t=CH),
                               ps[:, b, :].rearrange("p (k t c) -> p k t c", k=2, t=CH), ACT.Copy).then_inc(sg("gT_ready"), 1)
            for m in range(KD):
                act.wait_ge(sg("glu_mm"), m + 1)
                act.activation(sig[:, m, :], ps[:, 4 + m % 4, 0:SEQ], ACT.Sigmoid).then_inc(sg("sig_ready"), 1)
            act.wait_ge(sg("out0_done"), 1)
            sum_squares([ps[:, 2 * t:2 * t + 2, :] for t in range(NT)])
            sum_squares_x(2)
            hT_half(1, 2)
            for c in range(2 * FF_STEPS):
                act.wait_ge(sg("gu_done"), c + 1)
                if c >= 2:
                    act.wait_ge(sg("hid_ready"), c - 1)
                act.activation(sil[c % 2], ps[:, c % 2, 0:SEQ], ACT.Silu).then_inc(sg("sil_ready"), 1)
            act.wait_ge(sg("down_done"), 2 * FF_STEPS)
            sum_squares([ps[:, 2 + 2 * t:4 + 2 * t, :] for t in range(NT)])
            sum_squares_x(4)
            hT_half(2, 4)
            act.wait_ge(sg("proj_done"), QKV // IW)
            act.wait_ge(sg("x_stored"), 16)
            act.activation(qkv[:, 0, :].rearrange("p (b n) -> p b n", b=3), ps[:, 0:3, :], ACT.Copy).then_inc(sg("qkv_act"), 1)
            act.wait_ge(sg("qkv_act"), 1)
            act.activation(nat_flat[:, 0:QK * HD], qkv[:, 0, 0:QK * HD], ACT.Square).then_inc(sg("head_sq"), 1)
            act.wait_ge(sg("qkv_dve"), 1)
            act.wait_ge(sg("head_sum"), 1)
            act.activation(nat_flat[:, 0:QK * HD], qkv[:, 1, 0:QK * HD], ACT.Square).then_inc(sg("head_sq"), 1)
            for b in (0, 2):
                act.wait_ge(sg("q_tr"), b + 1)
                act.activation(qT[:, 2 * b:2 * b + 2, :], ps[:, b, :].rearrange("p (k n) -> p k n", k=2), ACT.Copy).then_inc(sg("qT_ready"), 1)
            act.wait_ge(sg("k_tr"), 1)
            act.activation(kT[:, 0:2, :], ps[:, 4, :].rearrange("p (k n) -> p k n", k=2), ACT.Copy).then_inc(sg("qT_ready"), 1)
            for u in range(UNITS):
                act.wait_ge(sg("smax_ready"), u + 1)
                if u >= 2:
                    act.wait_ge(sg("p_tr"), u - 1)
                for h in range(2):
                    act.activation(prob[u % 2][:, h, :], ps[:, 2 * (u % 2) + h, 0:SEQ], ACT.Exp, bias=nmax[:, 2 * u + h:2 * u + h + 1],
                                   scale=HD ** -0.5, accum_out=psum_[:, 2 * u + h:2 * u + h + 1]).then_inc(sg("probs_ready"), 1)
            for b in (0, 2):
                act.wait_ge(sg("oT_tr"), b + 1)
                act.activation(hT[:, 2 * b:2 * b + 2, :], ps[:, b, :].rearrange("p (k n) -> p k n", k=2), ACT.Copy).then_inc(sg("hT_ready"), 1)
            act.wait_ge(sg("proj_done"), QKV // IW + D // IW)
            sum_squares([ps[:, 4 + 2 * t:6 + 2 * t, :] for t in range(NT)])
            sum_squares_x(6)
            hT_half(3, None)
            act.wait_ge(sg("logits_shifted"), 1)
            act.activation(wexp, lshift, ACT.Exp).then_inc(sg("logits_exp"), 1)
            with act.Fori(0, EXP) as e:
                for b in (0, 2):
                    act.wait_ge(sg("gather_mm"), 4 * e + b + 1)
                    act.activation(xg[:, 2 * b:2 * b + 2, :], ps[:, 2 + b, :].rearrange("p (k n) -> p k n", k=2), ACT.Copy).then_inc(sg("xg_ready"), 1)
                for c in range(CHUNKS):
                    act.wait_ge(sg("moe_gu"), CHUNKS * e + c + 1)
                    if c >= 2:
                        act.wait_ge(sg("moe_hid"), CHUNKS * e + c - 1)
                    act.activation(m_sil[c % 2], ps[:, c % 2, 0:SEQ], ACT.Silu).then_inc(sg("moe_sil"), 1)
                    if c == SEL_AT + 4:
                        act.wait_ge(sg("selg_tr"), e + 1)
                        act.activation(sel_gT.rearrange("p a b n -> p (a b n)"), ps[:, 6, :], ACT.Copy).then_inc(sg("selgT_ready"), 1)
                act.wait_ge(sg("moe_down"), CHUNKS * (e + 1))
                for b in (0, 2):
                    act.activation(yT[:, 2 * b:2 * b + 2, :], ps[:, 2 + b, :].rearrange("p (k n) -> p k n", k=2), ACT.Copy).then_inc(sg("yT_ready"), 1)
                act.wait_ge(sg("y_tr"), 2 * e + 1)
                act.activation(y_lo[:, 0:512], ps[:, 6, :], ACT.Copy).then_inc(sg("y_ready"), 1)
                act.wait_ge(sg("y_tr"), 2 * e + 2)
                act.activation(y_hi[:, 0:512], ps[:, 0, :], ACT.Copy).then_inc(sg("y_ready"), 1)
            act.wait_ge(sg("scatter_mm"), 4 * EXP)
            for t in range(NT):
                act.wait_ge(sg("acc_done"), 4 * (EXP - 1) + 2 * t + 3)
                act.activation(hT.rearrange("p k n -> p (k n)")[:, t * D:(t + 1) * D], acc[:, t, :], ACT.Square,
                               accum_out=ssq[:, t:t + 1]).then_inc(sg("ssq_ready"), 1)

        @block.vector
        def _(dve):
            step = [0]

            def link(ins):
                step[0] += 1
                ins.then_inc(sg("dve_step"), 1)
                dve.wait_ge(sg("dve_step"), step[0])

            def tt(o, a, b, op):
                link(dve.tensor_tensor(o, a, b, op))

            def mean_square(n):
                dve.wait_ge(sg("ssq_ready"), 2 * (n + 1))
                dve.tensor_scalar(msq[:, :], ssq[:, :], 1.0 / D, EPS, MUL, ADD).then_inc(sg("ms_ready"), 1)

            def pre_norm(n):
                mean_square(n)
                dve.wait_ge(sg("rstd_ready"), n + 1)
                for t in range(NT):
                    dve.tensor_scalar(nat[:, t, :], x[:, t, :], rstd[:, t:t + 1], None, MUL).then_inc(sg("nat_ready"), 1)

            def hT_half(n, gain):
                for b in (1, 3):
                    dve.wait_ge(sg("tr_ready"), 4 * n + b + 1)
                    for k in (2 * b, 2 * b + 1):
                        ins = dve.tensor_scalar(hT[:, k, :], ps[:, b, (k % 2) * SEQ:(k % 2 + 1) * SEQ],
                                                1.0 if gain is None else gcol[:, gain * 8 + k:gain * 8 + k + 1], None, MUL)
                    ins.then_inc(sg("hT_ready"), 1)

            def post_norm(n, bank):
                mean_square(n)
                dve.wait_ge(sg("rstd_ready"), n + 1)
                dve.wait_ge(sg("post_gain_in"), 16 * (n + 1) // 2)
                for t in range(NT):
                    link(dve.scalar_tensor_tensor(nat[:, t, :], ps[:, bank + 2 * t:bank + 2 * t + 2, :].rearrange("p a b -> p (a b)"),
                                                  rstd[:, t:t + 1], post_gain[:, :], MUL, MUL))
                    dve.tensor_tensor(x[:, t, :], x[:, t, :], nat[:, t, :], ADD).then_inc(sg("x_done"), 1)

            dve.wait_ge(sg("lam_in"), 48)
            dve.tensor_copy(raw_l[0:DG, 2, :].rearrange("g (a p) -> g a p", a=2),
                            raw_s[0:DG, :].unsqueeze(2).to_broadcast([DG, 2, ST])).then_inc(sg("lstep_spread"), 1)
            pre_norm(0)
            dve.wait_ge(sg("gain_in"), 32)
            dve.tensor_copy(raw_dx[0:GROUPS, :, :], raw_d[0:GROUPS, :].unsqueeze(1).to_broadcast([GROUPS, CH, GC])).then_inc(sg("d_spread"), 1)
            lr, li, st, ea, mag, rs, rc_, sn, cs = (tmp(i) for i in range(9))
            dve.wait_ge(sg("lam_tr"), 1)
            dve.tensor_copy(lr, ps[:, 4, 0:64])
            dve.tensor_copy(li, ps[:, 4, 64:128]).then_inc(sg("lam_copied"), 1)
            dve.wait_ge(sg("step_ready"), 1)
            tt(ea, lr, st, MUL)
            tt(rs, li, st, MUL)
            n_, t_ = tmp(9), tmp(10)
            MAGIC = 12582912.0
            link(dve.tensor_scalar(n_, rs, 0.15915494309189535, MAGIC, MUL, ADD))
            link(dve.tensor_scalar(n_, n_, -MAGIC, None, ADD))
            for c in (6.28125, 1.9350051879882812e-3, 3.019915981956753e-7):
                link(dve.scalar_tensor_tensor(rs, n_, -c, rs, MUL, ADD))
            PI = 3.1415925
            link(dve.tensor_scalar(rs, rs, PI, -PI, ALU.min, ALU.max))
            link(dve.tensor_scalar(t_, rs, -1.0, None, MUL))
            tt(t_, t_, rs, ALU.max)
            dve.tensor_scalar(rc_, t_, -1.0, 1.5707963267948966, MUL, ADD).then_inc(sg("ang_ready"), 1)
            dve.wait_ge(sg("mag_ready"), 3)
            dve.memset(pw[:, 0, 0, :], 1.0)
            dve.memset(pw[:, 1, 0, :], 0.0)
            tt(pw[:, 0, 1, :], mag, cs, MUL)
            tt(pw[:, 1, 1, :], mag, sn, MUL)

            def cmul(o_re, o_im, a, b, shape, t1, t2):
                tt(t1, a[0], b[0], MUL)
                tt(t2, a[1], b[1], MUL)
                link(dve.tensor_tensor(o_re, t1, t2, SUB))
                tt(t1, a[0], b[1], MUL)
                tt(t2, a[1], b[0], MUL)
                link(dve.tensor_tensor(o_im, t1, t2, ADD))

            q1, q2 = tmp(11), tmp(12)
            cmul(pw[:, 0, 2, :], pw[:, 1, 2, :], (pw[:, 0, 1, :],) + (pw[:, 1, 1, :],), (pw[:, 0, 1, :], pw[:, 1, 1, :]), None, q1, q2)
            w1 = mtmp[0][:, 0:2 * DG].rearrange("p (k g) -> p k g", k=2)
            w2 = mtmp[1][:, 0:2 * DG].rearrange("p (k g) -> p k g", k=2)
            b2 = [pw[:, r, 2:3, :].to_broadcast([P, 2, DG]) for r in range(2)]
            cmul(pw[:, 0, 3:5, :], pw[:, 1, 3:5, :], (pw[:, 0, 1:3, :], pw[:, 1, 1:3, :]), b2, None, w1, w2)
            w1 = mtmp[0][:, 0:4 * DG].rearrange("p (k g) -> p k g", k=4)
            w2 = mtmp[1][:, 0:4 * DG].rearrange("p (k g) -> p k g", k=4)
            b4 = [pw[:, r, 4:5, :].to_broadcast([P, 4, DG]) for r in range(2)]
            cmul(pw[:, 0, 5:9, :], pw[:, 1, 5:9, :], (pw[:, 0, 1:5, :], pw[:, 1, 1:5, :]), b4, None, w1, w2)
            dve.memset(tmp(26), 0.0).then_inc(sg("pw_ready"), 1)
            den, nr, qr, qi = tmp(13), tmp(14), tmp(15), tmp(16)
            tt(q1, lr, lr, MUL)
            tt(q2, li, li, MUL)
            tt(den, q1, q2, ADD)
            link(dve.reciprocal(den, den))
            link(dve.tensor_scalar(nr, pw[:, 0, 1, :], -1.0, None, ADD))
            tt(q1, nr, lr, MUL)
            tt(q2, pw[:, 1, 1, :], li, MUL)
            tt(q1, q1, q2, ADD)
            tt(qr, q1, den, MUL)
            tt(q1, pw[:, 1, 1, :], lr, MUL)
            tt(q2, nr, li, MUL)
            tt(q1, q1, q2, SUB)
            tt(qi, q1, den, MUL)
            dve.wait_ge(sg("bc_out"), 4)
            m1 = at(REZ + 4096, DG, GC)
            m2 = at(REZ + 4096 + 1024, DG, GC)
            qb = [v.unsqueeze(2).to_broadcast([P, DG, GC]) for v in (qr, qi)]
            tt(m1, bP[:, 0], qb[0], MUL)
            tt(m2, bP[:, 1], qb[1], MUL)
            tt(bbar[:, 0, 0:DG, :], m1, m2, SUB)
            tt(m1, bP[:, 1], qb[0], MUL)
            tt(m2, bP[:, 0], qb[1], MUL)
            dve.wait_ge(sg("bbar_pad"), 1)
            dve.wait_ge(sg("pd_ready"), 1)
            dve.tensor_tensor(bbar[:, 1, 0:DG, :], m1, m2, ADD).then_inc(sg("bbar_ready"), 1)
            dve.wait_ge(sg("gcol_ready"), 1)
            hT_half(0, 0)
            dve.wait_ge(sg("bbar_ready"), 1)
            e1 = (tmp(17), tmp(18))
            cur = (cs, sn)
            for i in range(3):
                nxt = e1 if i % 2 == 0 else (tmp(19), tmp(20))
                cmul(nxt[0], nxt[1], cur, cur, None, q1, q2)
                tt(q1, nxt[0], nxt[0], MUL)
                tt(q2, nxt[1], nxt[1], MUL)
                tt(q1, q1, q2, ADD)
                link(dve.tensor_scalar(q1, q1, -0.5, 1.5, MUL, ADD))
                tt(nxt[0], nxt[0], q1, MUL)
                tt(nxt[1], nxt[1], q1, MUL)
                cur = nxt
            dve.wait_ge(sg("d_tr"), 1)
            link(dve.tensor_copy(dcol[:, :], ps[:, 7, 64:128]))
            link(dve.memset(ec[:, 0, :, 0:1], 1.0))
            link(dve.memset(ec[:, 1, :, 0:1], 0.0))
            n = 1
            while n < NC:
                bb = [v.unsqueeze(2).to_broadcast([P, DG, n]) for v in cur]
                t1 = at(REZ + 4096, DG, n)
                t2 = at(REZ + 4096 + 1024, DG, n)
                cmul(ec[:, 0, :, n:2 * n], ec[:, 1, :, n:2 * n], (ec[:, 0, :, 0:n], ec[:, 1, :, 0:n]), bb, None, t1, t2)
                if 2 * n < NC:
                    nxt = (tmp(21), tmp(22)) if cur[0] is not None and n in (1, 4, 16) else (tmp(23), tmp(24))
                    cmul(nxt[0], nxt[1], cur, cur, None, q1, q2)
                    cur = nxt
                n *= 2
            for t in range(NT):
                dve.wait_ge(sg("u_mm"), t + 1)
                dve.tensor_copy(nat[:, t, 512:1024], ps[:, 2 * t + 1, :]).then_inc(sg("u_dve"), 1)

            def build_wt(b):
                d = b // (NB // 2)
                s = slice(SB * b, SB * (b + 1))
                pt = pd[:, :, 1:NPOW, s] if d == 0 else pw[:, :, 0:CH, s]
                v4 = [m[:, 0:SB * P].rearrange("p (g s i) -> p g s i", g=SB, s=CH) for m in mtmp]
                for i in range(2):
                    ins = dve.tensor_tensor(v4[i], bbar[:, i, s, :].unsqueeze(2).to_broadcast([P, SB, CH, GC]),
                                            pt[:, i].rearrange("p s g -> p g s").unsqueeze(3).to_broadcast([P, SB, CH, GC]), MUL)
                link(ins)
                if b >= 2:
                    dve.wait_ge(sg("w_tr"), 2 * (b - 1))
                link(dve.tensor_tensor(wt[b % 2][:, 0].rearrange("p g x -> p (g x)"), mtmp[0][:, 0:SB * P], mtmp[1][:, 0:SB * P], SUB))
                dve.wait_ge(sg("wt_pool"), 2 * (b + 1))
                dve.tensor_tensor(wt[b % 2][:, 1].rearrange("p g x -> p (g x)"), mtmp[2][:, 0:SB * P], mtmp[3][:, 0:SB * P], ADD).then_inc(sg("wt_ready"), 1)

            build_wt(0)
            build_wt(1)
            dve.wait_ge(sg("u_tok_in"), 16 * NT * CH)
            GA = 28
            for s in range(CH):
                ins = dve.tensor_copy(u_grp[0:NC, GA:, s, :], u_tok[0:NC, s, GA * GC:].rearrange("p (g i) -> p g i", i=GC))
            ins.then_inc(sg("u_grp_ready"), 1)
            for b in range(2, NB):
                build_wt(b)
            dve.wait_ge(sg("uc_tr"), 4)
            link(dve.memset(xbd[:, :, :, :, :], 0.0))
            m2_, m4_, m8_ = tmp(21), tmp(22), tmp(25)
            tt(m2_, mag, mag, MUL)
            tt(m4_, m2_, m2_, MUL)
            tt(m8_, m4_, m4_, MUL)
            dve.wait_ge(sg("s_out"), NB)
            tt(zz[:, 0], S_[:, 0], ec[:, 0], MUL)
            tt(tmp8, S_[:, 1], ec[:, 1], MUL)
            tt(zz[:, 0], zz[:, 0], tmp8, ADD)
            tt(zz[:, 1], S_[:, 1], ec[:, 0], MUL)
            tt(tmp8, S_[:, 0], ec[:, 1], MUL)
            tt(zz[:, 1], zz[:, 1], tmp8, SUB)
            for d in range(DIRS):
                gsl = slice(GP * d, GP * (d + 1))
                link(dve.tensor_copy(r8t[:, :, :], m8_[:, gsl].unsqueeze(2).to_broadcast([P, GP, NC])))
                link(dve.memset(r8t[:, :, 0:1], 0.0))
                for r in range(2):
                    ins = dve.tensor_tensor_scan(S_[:, r, gsl, :].rearrange("p g c -> p (g c)"), r8t[:, :, :].rearrange("p g c -> p (g c)"),
                                                 zz[:, r, gsl, :].rearrange("p g c -> p (g c)"), 0.0, MUL, ADD)
                link(ins)
            for r, (ea_, eb_, op) in enumerate(((0, 1, SUB), (1, 0, ADD))):
                tt(zz[:, 0], S_[:, 0], ec[:, ea_], MUL)
                tt(tmp8, S_[:, 1], ec[:, eb_], MUL)
                for a in range(2):
                    h = slice(64 * a, 64 * a + 64)
                    ins = dve.tensor_tensor(xbd[h, r, :, a, 1:NC], zz[h, 0, :, 0:NC - 1], tmp8[h, :, 0:NC - 1], op)
                link(ins)
            dve.memset(tmp(26), 0.0).then_inc(sg("x_ready"), 1)
            for b in range(NB):
                d = b // (NB // 2)
                s = slice(SB * b, SB * (b + 1))
                pt = pw[:, :, :, s] if d == 0 else pd[:, :, :, s]
                v4 = [m.rearrange("p (g s i) -> p g s i", g=SB, s=NPOW) for m in mtmp]
                for i in range(2):
                    ins = dve.tensor_tensor(v4[i], cP[:, i, s, :].unsqueeze(2).to_broadcast([P, SB, NPOW, GC]),
                                            pt[:, i].rearrange("p s g -> p g s").unsqueeze(3).to_broadcast([P, SB, NPOW, GC]), MUL)
                link(ins)
                if b >= 2:
                    dve.wait_ge(sg("y_state"), b - 1)
                v = vv[b % 2]
                link(dve.tensor_tensor(v[:, 0].rearrange("p g s i -> p (g s i)"), mtmp[0], mtmp[1], SUB))
                dve.wait_ge(sg("v_pool"), 2 * (b + 1))
                dve.scalar_tensor_tensor(v[:, 1].rearrange("p g s i -> p (g s i)"), mtmp[2], -1.0, mtmp[3], MUL, SUB).then_inc(sg("v_ready"), 1)
            dve.wait_ge(sg("k_out"), NB)
            dve.tensor_tensor(kall[:, :, :, CH - 1, :], kall[:, :, :, CH - 1, :], kzero[:, :, :, :], ADD).then_inc(sg("k_final"), 1)
            tt(ud[:, :, :], uc[:, :, :], dcol[:, :].unsqueeze(2).to_broadcast([P, GROUPS, NC]), MUL)
            for b in range(4):
                dve.wait_ge(sg("y_mm"), b + 1)
                dve.tensor_tensor(yg[:, 16 * b:16 * b + 16, :].rearrange("p g c -> p (g c)"), ps[:, b, :],
                                  ud[:, 16 * b:16 * b + 16, :].rearrange("p g c -> p (g c)"), ADD).then_inc(sg("y_sum"), 1)
            for r in range(1, 16, 2):
                dve.wait_ge(sg("g_tr"), r + 1)
                dve.tensor_copy(g_tok[0:NC, :, 64 * r:64 * r + 64].rearrange("c t (g o) -> c g t o", o=GC),
                                ps[0:NC, 4 + r % 4, :].rearrange("c (g t o) -> c g t o", g=4, t=CH)).then_inc(sg("g_tok_dve"), 1)
            for b in (1, 3):
                dve.wait_ge(sg("gT_tr"), b + 1)
                dve.tensor_copy(gT[:, 2 * b:2 * b + 2, :].rearrange("p k (c t) -> p k t c", t=CH),
                                ps[:, b, :].rearrange("p (k t c) -> p k t c", k=2, t=CH)).then_inc(sg("gT_ready"), 1)
            for m in range(KD):
                dve.wait_ge(sg("sig_ready"), m + 1)
                dve.tensor_tensor(mT[:, m, :], sig[:, m, :], gT[:, m, :], MUL).then_inc(sg("m_ready"), 1)
            post_norm(1, 0)
            dve.wait_ge(sg("x_done"), 2)
            pre_norm(2)
            hT_half(1, 2)
            for c in range(2 * FF_STEPS):
                dve.wait_ge(sg("sil_ready"), c + 1)
                if c >= 2:
                    dve.wait_ge(sg("down_done"), c - 1)
                dve.tensor_tensor(hid[c % 2], sil[c % 2], ps[:, c % 2, SEQ:2 * SEQ], MUL).then_inc(sg("hid_ready"), 1)
            post_norm(3, 2)
            dve.wait_ge(sg("x_done"), 4)
            pre_norm(4)
            hT_half(2, 4)
            dve.wait_ge(sg("proj_done"), QKV // IW)
            dve.wait_ge(sg("x_stored"), 16)
            dve.tensor_copy(qkv[:, 1, :].rearrange("p (b n) -> p b n", b=3), ps[:, 3:6, :]).then_inc(sg("qkv_dve"), 1)
            dve.wait_ge(sg("rope_in"), 64)
            for w in range(2):
                for i, (cs_, par) in enumerate(((0, 0), (1, 1), (1, 0), (0, 1))):
                    ins = dve.tensor_tensor(rope_t[:, w, i], rope_raw[:, cs_],
                                            qk_gain[:, w, par::2].unsqueeze(1).to_broadcast([P, NT, HD // 2]), MUL)
            link(ins)
            for t in range(NT):
                dve.wait_ge(sg("head_sq"), t + 1)
                dve.tensor_reduce(hms[:, t * QK:(t + 1) * QK], nat_flat[:, 0:QK * HD].rearrange("p (h d) -> p h d", d=HD), AX.X, ADD).then_inc(sg("head_sum"), 1)
            dve.wait_ge(sg("head_sum"), NT)
            dve.tensor_scalar(hms[:, 0:NT * QK], hms[:, 0:NT * QK], 1.0 / HD, EPS, MUL, ADD).then_inc(sg("head_ms"), 1)
            dve.wait_ge(sg("head_rstd"), 1)
            dve.wait_ge(sg("qkv_act"), 1)
            dve.wait_ge(sg("qkv_dve"), 1)
            def finish_heads(q):
                t, h0 = divmod(q, 2)
                dve.wait_ge(sg("probs_ready"), 8 * (q + 1))
                dve.wait_ge(sg("pv_done"), 4 * (q + 1))
                link(dve.reciprocal(prcp[:, 8 * q:8 * q + 8], psum_[:, 8 * q:8 * q + 8]))
                dve.tensor_tensor(o_nat[:, t, h0 * 512:(h0 + 1) * 512].rearrange("p (h d) -> p h d", d=HD),
                                  ps[:, 6 + q % 2, :].rearrange("p (h d) -> p h d", d=HD),
                                  prcp[:, 8 * q:8 * q + 8].unsqueeze(2).to_broadcast([P, 8, HD]), MUL).then_inc(sg("o_ready"), 1)

            for t in range(NT):
                v = qkv[:, t, 0:QK * HD].rearrange("p (h d) -> p h d", d=HD)
                tt(v, v, hrs[:, t * QK:(t + 1) * QK].unsqueeze(2).to_broadcast([P, QK, HD]), MUL)
                for w in range(2):
                    hs = slice(0, NH) if w == 0 else slice(NH, QK)
                    nh = NH if w == 0 else NKV
                    for i in range(4):
                        ins = dve.tensor_tensor(rope_m[i][:, 0:nh], v[:, hs, (i % 2)::2],
                                                rope_t[:, w, i, t].unsqueeze(1).to_broadcast([P, nh, HD // 2]), MUL)
                    link(ins)
                    if w == 0:
                        dve.tensor_tensor(v[:, hs, 0::2], rope_m[0], rope_m[1], SUB)
                        link(dve.tensor_tensor(v[:, hs, 1::2], rope_m[2], rope_m[3], ADD))
                    else:
                        for c in range(2):
                            dve.tensor_tensor(k_dup[:, t, :, c, 0::2], rope_m[0][:, 0:nh], rope_m[1][:, 0:nh], SUB)
                            ins = dve.tensor_tensor(k_dup[:, t, :, c, 1::2], rope_m[2][:, 0:nh], rope_m[3][:, 0:nh], ADD)
                        ins.then_inc(sg("rope_done"), 1)
                        dve.wait_ge(sg("rope_done"), t + 1)
            for b in (1, 3):
                dve.wait_ge(sg("q_tr"), b + 1)
                dve.tensor_copy(qT[:, 2 * b:2 * b + 2, :], ps[:, b, :].rearrange("p (k n) -> p k n", k=2)).then_inc(sg("qT_ready"), 1)
            dve.wait_ge(sg("k_tr"), 2)
            dve.tensor_copy(kT[:, 2:4, :], ps[:, 5, :].rearrange("p (k n) -> p k n", k=2)).then_inc(sg("qT_ready"), 1)

            def score_max(u):
                dve.wait_ge(sg("scores_ready"), u + 1)
                link(dve.tensor_reduce(nmax[:, 2 * u:2 * u + 2], ps[:, 2 * (u % 2):2 * (u % 2) + 2, 0:SEQ], AX.X, ALU.max))
                dve.tensor_scalar(nmax[:, 2 * u:2 * u + 2], nmax[:, 2 * u:2 * u + 2], -HD ** -0.5, None, MUL).then_inc(sg("smax_ready"), 1)

            score_max(0)
            for u in range(UNITS):
                if u + 1 < UNITS:
                    score_max(u + 1)
                dve.wait_ge(sg("p_tr"), u + 1)
                if u >= 2:
                    dve.wait_ge(sg("pv_done"), u - 1)
                dve.tensor_copy(probT[u % 2], ps[:, 4 + u % 2, :].rearrange("p (a b n) -> p a b n", a=2, b=NT)).then_inc(sg("probT_ready"), 1)
                if u % 4 == 0 and u >= 4:
                    finish_heads(u // 4 - 1)
            finish_heads(UNITS // 4 - 1)
            for b in (1, 3):
                dve.wait_ge(sg("oT_tr"), b + 1)
                dve.tensor_copy(hT[:, 2 * b:2 * b + 2, :], ps[:, b, :].rearrange("p (k n) -> p k n", k=2)).then_inc(sg("hT_ready"), 1)
            dve.wait_ge(sg("x_back"), 16)
            post_norm(5, 4)
            mean_square(6)
            dve.wait_ge(sg("rstd_ready"), 7)
            dve.wait_ge(sg("post_gain_in"), 64)
            dve.wait_ge(sg("x_done"), 6)
            for t in range(NT):
                dve.scalar_tensor_tensor(h_moe[:, t, :], x[:, t, :], rstd[:, t:t + 1], post_gain[:, :], MUL, MUL).then_inc(sg("nat_ready"), 1)
            hT_half(3, None)
            dve.wait_ge(sg("route_consts"), 1)
            dve.wait_ge(sg("logits_mm"), 1)
            link(dve.tensor_copy(logit[:, :, :], ps[:, 4, 0:NT * EXP].rearrange("p (t e) -> p t e", t=NT)))
            link(dve.tensor_reduce(lmax, logit, AX.X, ALU.max))
            dve.tensor_tensor(lshift, logit, lmax.unsqueeze(2).to_broadcast([P, NT, EXP]), SUB).then_inc(sg("logits_shifted"), 1)
            lj = logit.unsqueeze(2).to_broadcast([P, NT, EXP, EXP])
            li_ = logit.unsqueeze(3).to_broadcast([P, NT, EXP, EXP])
            dve.tensor_tensor(gt_, lj, li_, ALU.is_gt)
            tt(eq_, lj, li_, ALU.is_equal)
            tt(eq_, eq_, lower_e.unsqueeze(1).to_broadcast([P, NT, EXP, EXP]), MUL)
            tt(gt_, gt_, eq_, ADD)
            link(dve.tensor_reduce(beats, gt_, AX.X, ADD))
            dve.tensor_scalar(chosen[:, :, 0:EXP], beats, 1.5, None, ALU.is_lt).then_inc(sg("chosen_ready"), 1)
            dve.wait_ge(sg("chosen_ready"), 1)
            dve.wait_ge(sg("logits_exp"), 1)
            tt(wexp, wexp, chosen[:, :, 0:EXP], MUL)
            link(dve.tensor_reduce(wsum, wexp, AX.X, ADD))
            link(dve.reciprocal(wsum, wsum))
            tt(gate[:, :, 0:EXP], wexp, wsum.unsqueeze(2).to_broadcast([P, NT, EXP]), MUL)
            dve.wait_ge(sg("rank_mm"), 1)
            link(dve.tensor_copy(rank[:, :, 0:EXP], ps[:, 5, 0:NT * EXP].rearrange("p (t e) -> p t e", t=NT)))
            dve.tensor_copy(cnt_i[0:1, :], ps[0:1, 6, 0:EXP]).then_inc(sg("counts_ready"), 1)

            def selection(dst, weight, e, sem):
                for t in range(NT):
                    dve.tensor_scalar(dst[:, t, :], iota[:, :], rank[:, t, bass.ds(e, 1)], weight[:, t, bass.ds(e, 1)],
                                      ALU.is_equal, MUL).then_inc(sg(sem), 1)

            selection(sel, chosen, 0, "sel_ready")
            with dve.Fori(0, EXP) as e:
                for b in (1, 3):
                    dve.wait_ge(sg("gather_mm"), 4 * e + b + 1)
                    dve.tensor_copy(xg[:, 2 * b:2 * b + 2, :], ps[:, 2 + b, :].rearrange("p (k n) -> p k n", k=2)).then_inc(sg("xg_ready"), 1)
                for c in range(CHUNKS):
                    dve.wait_ge(sg("moe_sil"), CHUNKS * e + c + 1)
                    if c >= 2:
                        dve.wait_ge(sg("moe_down"), CHUNKS * e + c - 1)
                    dve.tensor_tensor(m_hid[c % 2], m_sil[c % 2], ps[:, c % 2, SEQ:2 * SEQ], MUL).then_inc(sg("moe_hid"), 1)
                    if c == SEL_AT:
                        dve.wait_ge(sg("acc_done"), 4 * e + 1)
                        selection(sel_g, gate, e, "selg_ready")
                        selection(sel, chosen, e + 1, "sel_ready")
                dve.wait_ge(sg("moe_down"), CHUNKS * (e + 1))
                for b in (1, 3):
                    dve.tensor_copy(yT[:, 2 * b:2 * b + 2, :], ps[:, 2 + b, :].rearrange("p (k n) -> p k n", k=2)).then_inc(sg("yT_ready"), 1)
                dve.wait_ge(sg("y_tr"), 2 * e + 1)
                dve.tensor_copy(y_lo[:, 512:1024], ps[:, 7, :]).then_inc(sg("y_ready"), 1)
                dve.wait_ge(sg("y_tr"), 2 * e + 2)
                dve.tensor_copy(y_hi[:, 512:1024], ps[:, 1, :]).then_inc(sg("y_ready"), 1)
                for b in range(4):
                    dve.wait_ge(sg("scatter_mm"), 4 * e + b + 1)
                    av = acc[:, b // 2, (b % 2) * 512:(b % 2 + 1) * 512]
                    dve.wait_ge(sg("acc_done"), 4 * e + 1)
                    dve.tensor_tensor(av, av, ps[:, 2 + b, :], ADD).then_inc(sg("acc_done"), 1)
            mean_square(7)
            dve.wait_ge(sg("rstd_ready"), 8)
            dve.wait_ge(sg("last_gain_in"), 16)
            dve.wait_ge(sg("x_back"), 32)
            dve.wait_ge(sg("acc_done"), 4 * EXP + 1)
            for t in range(NT):
                link(dve.scalar_tensor_tensor(acc[:, t, :], acc[:, t, :], rstd[:, t:t + 1], last_gain[:, :], MUL, MUL))
                dve.tensor_tensor(acc[:, t, :], acc[:, t, :], nat[:, t, :], ADD).then_inc(sg("y_final"), 1)

        @block.tensor
        def _(pe):
            def transposed_nat(n):
                pe.wait_ge(sg("nat_ready"), 2 * (n + 1))
                for b in range(4):
                    for k in (2 * b, 2 * b + 1):
                        for t in range(NT):
                            m = pe.transpose(ps[:, b, (k % 2) * SEQ + t * P:(k % 2) * SEQ + (t + 1) * P],
                                             nat[:, t, k * P:(k + 1) * P], ident[:, :])
                    m.then_inc(sg("tr_ready"), 1)

            id64 = ident[0:64, 0:64]
            pe.wait_ge(sg("ident_ready"), 1)
            pe.wait_ge(sg("lam_in"), 48)
            pe.wait_ge(sg("lstep_spread"), 1)
            for i in range(3):
                m = pe.transpose(ps[:, 4, 64 * i:64 * i + 64], raw_l[0:DG, i, :], id64)
            m.then_inc(sg("lam_tr"), 1)
            pe.wait_ge(sg("b_in"), 32)
            pe.wait_ge(sg("c_in"), 64)
            for r in range(4):
                if r >= 1:
                    pe.wait_ge(sg("bc_out"), 2 * r)
                for h in range(2):
                    for s in range(8):
                        src = raw_b[0:DG, r, :, 8 * h + s] if r < 2 else raw_c[0:DG, r - 2, 8 * h + s, :]
                        m = pe.transpose(ps[:, 5 + h, 64 * s:64 * s + 64], src, id64)
                    m.then_inc(sg("bc_tr"), 1)
            pe.wait_ge(sg("gain_in"), 32)
            pe.transpose(ps[:, 7, 0:64], raw_g[0:64, :], id64).then_inc(sg("gain_tr"), 1)
            pe.wait_ge(sg("d_spread"), 1)
            pe.wait_ge(sg("gcol_ready"), 1)
            pe.transpose(ps[:, 7, 64:128], raw_dx[0:GROUPS, :, :].rearrange("g t o -> g (t o)"), id64).then_inc(sg("d_tr"), 1)
            transposed_nat(0)
            pe.wait_ge(sg("hT_ready"), 4)
            for t in range(NT):
                for i in range(4):
                    if t == 0:
                        pe.wait_ge(sg(f"mix_w{i}"), 16)
                    for k in range(KD):
                        m = pe.matmul(ps[:, 2 * t + i // 2, (i % 2) * IW:(i % 2 + 1) * IW], hT[:, k, t * P:(t + 1) * P],
                                      w_in[:, i, k, :], start=k == 0, stop=k == KD - 1)
                m.then_inc(sg("u_mm"), 1)
            pe.wait_ge(sg("u_grp_ready"), 2)
            pe.wait_ge(sg("u_act"), 2)
            pe.wait_ge(sg("u_dve"), 2)
            for b in range(4):
                for g in range(16 * b, 16 * b + 16):
                    m = pe.transpose(ps[:, b, (g % 16) * NC:(g % 16 + 1) * NC],
                                     u_grp[0:NC, g, :, :].rearrange("c s i -> c (s i)"), ident[0:NC, 0:NC])
                m.then_inc(sg("uc_tr"), 1)

            def w_transposes(b):
                pe.wait_ge(sg("wt_ready"), b + 1)
                if b >= 2:
                    pe.wait_ge(sg("w_out_act"), 2 * (b - 1))
                if b == 0:
                    pe.wait_ge(sg("uc_ready"), 4)
                for g in range(SB):
                    for r in range(2):
                        n = 2 * g + r
                        m = pe.transpose(ps[:, 2 * (b % 2) + n // 4, (n % 4) * P:(n % 4 + 1) * P], wt[b % 2][:, r, g, :], ident[:, :])
                    if g % 2 == 1:
                        m.then_inc(sg("w_tr"), 1)

            def s_matmuls(b):
                pe.wait_ge(sg("w_out_act"), 2 * (b + 1))
                if b >= 2:
                    pe.wait_ge(sg("s_out"), b - 1)
                d = b // (NB // 2)
                for g in range(SB):
                    gp = (SB * b + g) % GP
                    for a in range(2):
                        rhs = uc[:, 2 * gp + a, :] if d == 0 else uc[:, 2 * gp + a, ::-1]
                        for r in range(2):
                            m = pe.matmul(ps[64 * a:64 * a + 64, 4 + b % 2, r * P + g * NC:r * P + (g + 1) * NC],
                                          wm[b % 2][:, g, r, 64 * a:64 * a + 64], rhs, start=True, stop=True)
                m.then_inc(sg("s_mm"), 1)

            for b in range(NB):
                w_transposes(b)
                if b >= 1:
                    s_matmuls(b - 1)
            s_matmuls(NB - 1)
            pe.wait_ge(sg("s_out"), NB)
            pe.wait_ge(sg("x_ready"), 1)
            for b in range(NB):
                d = b // (NB // 2)
                pe.wait_ge(sg("v_ready"), b + 1)
                v = vv[b % 2]
                if b >= 2:
                    pe.wait_ge(sg("k_out"), b - 1)
                k0 = 0 if d == 0 else 1
                for a in range(2):
                    for g in range(SB):
                        dg = SB * b + g
                        for r in range(2):
                            m = pe.matmul(ps[32 * g:32 * g + 32, 4 + 2 * (b % 2) + a, 0:P],
                                          bbar[64 * a:64 * a + 64, r, dg:dg + 2, :].rearrange("p g i -> p (g i)"),
                                          v[64 * a:64 * a + 64, r, g, k0:k0 + CH, :].rearrange("p t o -> p (t o)"),
                                          start=r == 0, stop=r == 1)
                m.then_inc(sg("k_mm"), 1)
                y0 = 1 if d == 0 else 0
                for g in range(SB):
                    dg = SB * b + g
                    gp = dg % GP
                    for r in range(2):
                        rhs = xbd[:, r, dg, :, :] if d == 0 else xbd[:, r, dg, :, ::-1]
                        m = pe.matmul(ps[:, gp // 8, (gp % 8) * 64:(gp % 8 + 1) * 64],
                                      v[:, r, g, y0:y0 + CH, :].rearrange("p t o -> p (t o)"), rhs,
                                      start=(d == 0 and gp % 8 == 0 and r == 0), stop=False, skip_group_check=True)
                m.then_inc(sg("y_state"), 1)
            pe.wait_ge(sg("toe_in"), 16 * CH)
            for g in range(GROUPS):
                m = pe.matmul(ps[:, g // 16, (g % 16) * NC:(g % 16 + 1) * NC], toe[:, g, :], uc[:, g, :],
                              start=False, stop=True, skip_group_check=True)
                if g % 16 == 15:
                    m.then_inc(sg("y_mm"), 1)
            for r in range(16):
                pe.wait_ge(sg("gelu"), r // 4 + 1)
                if r >= 4:
                    pe.wait_ge(sg("g_tok_act" if r % 2 == 0 else "g_tok_dve"), (r - 4) // 2 + 1)
                for g in range(4 * r, 4 * r + 4):
                    m = pe.transpose(ps[0:NC, 4 + r % 4, (g % 4) * P:(g % 4 + 1) * P], yg[:, g, :], ident[:, :])
                m.then_inc(sg("g_tr"), 1)
            pe.wait_ge(sg("g_tok_act"), 8)
            pe.wait_ge(sg("g_tok_dve"), 8)
            for b in range(4):
                for k in (2 * b, 2 * b + 1):
                    for t in range(CH):
                        m = pe.transpose(ps[:, b, (k % 2) * SEQ + t * NC:(k % 2) * SEQ + (t + 1) * NC],
                                         g_tok[0:NC, t, k * P:(k + 1) * P], ident[0:NC, 0:NC])
                m.then_inc(sg("gT_tr"), 1)
            pe.wait_ge(sg("gT_ready"), 4)
            for m_ in range(KD):
                if m_ % 2 == 0:
                    pe.wait_ge(sg(f"mix_w{m_ // 2}"), 32)
                if m_ >= 4:
                    pe.wait_ge(sg("m_ready"), m_ - 3)
                for k in range(KD):
                    m = pe.matmul(ps[:, 4 + m_ % 4, 0:SEQ], w_glu[:, m_ // 2, k, (m_ % 2) * P:(m_ % 2 + 1) * P],
                                  gT[:, k, :], start=k == 0, stop=k == KD - 1)
                m.then_inc(sg("glu_mm"), 1)
            pe.wait_ge(sg("m_ready"), 8)
            for t in range(NT):
                for i in range(4):
                    if t == 0:
                        pe.wait_ge(sg(f"mix_w{i}"), 48)
                    for k in range(KD):
                        m = pe.matmul(ps[:, 2 * t + i // 2, (i % 2) * IW:(i % 2 + 1) * IW], mT[:, k, t * P:(t + 1) * P],
                                      w_out0[:, i, k, :], start=k == 0, stop=k == KD - 1)
            m.then_inc(sg("out0_done"), 1)
            transposed_nat(1)
            pe.wait_ge(sg("hT_ready"), 8)

            def ffn_down(c):
                n = 3 * (c // 2) + 2
                pe.wait_ge(*item_full(n))
                pe.wait_ge(sg("hid_ready"), c + 1)
                for t in range(NT):
                    for h in range(2):
                        m = pe.matmul(ps[:, 2 + 2 * t + h, :], hid[c % 2][:, t * P:(t + 1) * P],
                                      slot_down(n)[:, c % 2, h * 512:(h + 1) * 512], start=c == 0, stop=c == 2 * FF_STEPS - 1)
                m.then_inc(sg("down_done"), 1)

            for c in range(2 * FF_STEPS):
                if c >= 2:
                    pe.wait_ge(sg("hid_ready"), c - 1)
                for i in range(2):
                    n = 3 * (c // 2) + i
                    pe.wait_ge(*item_full(n))
                    for k in range(KD):
                        m = pe.matmul(ps[:, c % 2, i * SEQ:(i + 1) * SEQ], slot(n)[:, k, (c % 2) * P:(c % 2 + 1) * P],
                                      hT[:, k, :], start=k == 0, stop=k == KD - 1)
                m.then_inc(sg("gu_done"), 1)
                if c >= 1:
                    ffn_down(c - 1)
            ffn_down(2 * FF_STEPS - 1)
            transposed_nat(2)
            pe.wait_ge(sg("hT_ready"), 12)
            for i in range(QKV // IW):
                pe.wait_ge(*item_full(ITEM_QKV + i))
                for t in range(NT):
                    for k in range(KD):
                        m = pe.matmul(ps[:, 3 * t + i // 2, (i % 2) * IW:(i % 2 + 1) * IW], hT[:, k, t * P:(t + 1) * P],
                                      slot(ITEM_QKV + i)[:, k, :], start=k == 0, stop=k == KD - 1)
                m.then_inc(sg("proj_done"), 1)
            pe.wait_ge(sg("rope_done"), NT)
            for b in range(4):
                for k in (2 * b, 2 * b + 1):
                    for t in range(NT):
                        m = pe.transpose(ps[:, b, (k % 2) * SEQ + t * P:(k % 2) * SEQ + (t + 1) * P],
                                         qkv[:, t, k * P:(k + 1) * P], ident[:, :])
                m.then_inc(sg("q_tr"), 1)
            for b in range(2):
                for k in (2 * b, 2 * b + 1):
                    for t in range(NT):
                        m = pe.transpose(ps[:, 4 + b, (k % 2) * SEQ + t * P:(k % 2) * SEQ + (t + 1) * P],
                                         k_dup[:, t, k].rearrange("p c d -> p (c d)"), ident[:, :])
                m.then_inc(sg("k_tr"), 1)
            pe.wait_ge(sg("qT_ready"), 6)

            def scores(u):
                t, hp = divmod(u, NH // 2)
                if u >= 2:
                    pe.wait_ge(sg("probs_ready"), 2 * (u - 1))
                for h in range(2):
                    m = pe.matmul(ps[:, 2 * (u % 2) + h, 0:SEQ], qT[64 * h:64 * h + 64, hp, t * P:(t + 1) * P],
                                  kT[64 * h:64 * h + 64, 2 * hp // HPK, :], start=True, stop=True)
                m.then_inc(sg("scores_ready"), 1)

            def prob_transposes(u):
                pe.wait_ge(sg("probs_ready"), 2 * (u + 1))
                if u >= 2:
                    pe.wait_ge(sg("probT_ready"), u - 1)
                for h in range(2):
                    for c in range(NT):
                        m = pe.transpose(ps[:, 4 + u % 2, (2 * h + c) * P:(2 * h + c + 1) * P], prob[u % 2][:, h, c * P:(c + 1) * P], ident[:, :])
                m.then_inc(sg("p_tr"), 1)

            def prob_values(u):
                t, hp = divmod(u, NH // 2)
                pe.wait_ge(sg("probT_ready"), u + 1)
                if u % 4 == 0 and u >= 8:
                    pe.wait_ge(sg("o_ready"), u // 4 - 1)
                kv = 2 * hp // HPK
                for h in range(2):
                    for c in range(NT):
                        m = pe.matmul(ps[:, 6 + (u // 4) % 2, (2 * (u % 4) + h) * HD:(2 * (u % 4) + h + 1) * HD], probT[u % 2][:, h, c, :],
                                      qkv[:, c, (QK + kv) * HD:(QK + kv + 1) * HD], start=c == 0, stop=c == NT - 1)
                m.then_inc(sg("pv_done"), 1)

            for u in range(UNITS + 2):
                if u < UNITS:
                    scores(u)
                if 1 <= u <= UNITS:
                    prob_transposes(u - 1)
                if u >= 2:
                    prob_values(u - 2)
            pe.wait_ge(sg("o_ready"), 4)
            for b in range(4):
                for k in (2 * b, 2 * b + 1):
                    for t in range(NT):
                        m = pe.transpose(ps[:, b, (k % 2) * SEQ + t * P:(k % 2) * SEQ + (t + 1) * P],
                                         o_nat[:, t, k * P:(k + 1) * P], ident[:, :])
                m.then_inc(sg("oT_tr"), 1)
            pe.wait_ge(sg("hT_ready"), 16)
            for i in range(D // IW):
                pe.wait_ge(*item_full(ITEM_WO + i))
                for t in range(NT):
                    for k in range(KD):
                        m = pe.matmul(ps[:, 4 + 2 * t + i // 2, (i % 2) * IW:(i % 2 + 1) * IW], hT[:, k, t * P:(t + 1) * P],
                                      slot(ITEM_WO + i)[:, k, :], start=k == 0, stop=k == KD - 1)
                m.then_inc(sg("proj_done"), 1)
            transposed_nat(3)
            pe.wait_ge(sg("hT_ready"), 20)
            pe.wait_ge(sg("router_in"), 16)
            for t in range(NT):
                for k in range(KD):
                    m = pe.matmul(ps[:, 4, t * EXP:(t + 1) * EXP], hT[:, k, t * P:(t + 1) * P], w_router[:, k, :],
                                  start=k == 0, stop=k == KD - 1)
            m.then_inc(sg("logits_mm"), 1)
            pe.wait_ge(sg("chosen_ready"), 1)
            pe.matmul(ps[:, 5, 0:EXP], upper[:, :], chosen[:, 0, 0:EXP], start=True, stop=True)
            pe.matmul(ps[:, 5, EXP:2 * EXP], ones[:, :], chosen[:, 0, 0:EXP], start=True, stop=False)
            pe.matmul(ps[:, 5, EXP:2 * EXP], upper[:, :], chosen[:, 1, 0:EXP], start=False, stop=True)
            for t in range(NT):
                m = pe.matmul(ps[0:1, 6, 0:EXP], ones[:, 0:1], chosen[:, t, 0:EXP], start=t == 0, stop=t == NT - 1)
            m.then_inc(sg("rank_mm"), 1)
            pe.wait_ge(sg("counts_ready"), 1)

            def expert(e, V):
                pe.wait_ge(sg("sel_ready"), NT * (e + 1))
                for b in range(4):
                    pe.wait_ge(sg("acc_done"), 4 * e + 1)
                    for k in (2 * b, 2 * b + 1):
                        for t in range(NT):
                            m = pe.matmul(ps[:, 2 + b, (k % 2) * SEQ:(k % 2) * SEQ + V], h_moe[:, t, k * P:(k + 1) * P],
                                          sel[:, t, 0:V], start=t == 0, stop=t == NT - 1)
                    m.then_inc(sg("gather_mm"), 1)
                pe.wait_ge(sg("xg_ready"), 4 * (e + 1))

                def down(c):
                    n = ITEM_MOE + 3 * (c // 2) + 2
                    pe.wait_ge(*moe_item_full(e, n - ITEM_MOE))
                    pe.wait_ge(sg("moe_hid"), CHUNKS * e + c + 1)
                    for k in range(KD):
                        m = pe.matmul(ps[:, 2 + k // 2, (k % 2) * SEQ:(k % 2) * SEQ + V], slot_down(n)[:, c % 2, k * P:(k + 1) * P],
                                      m_hid[c % 2][:, 0:V], start=(c == 0 and k % 2 == 0), stop=c == CHUNKS - 1, skip_group_check=True)
                    m.then_inc(sg("moe_down"), 1)

                for c in range(CHUNKS):
                    if c >= 2:
                        pe.wait_ge(sg("moe_hid"), CHUNKS * e + c - 1)
                    for i in range(2):
                        n = ITEM_MOE + 3 * (c // 2) + i
                        pe.wait_ge(*moe_item_full(e, n - ITEM_MOE))
                        for k in range(KD):
                            m = pe.matmul(ps[:, c % 2, i * SEQ:i * SEQ + V], slot(n)[:, k, (c % 2) * P:(c % 2 + 1) * P],
                                          xg[:, k, 0:V], start=k == 0, stop=k == KD - 1)
                    m.then_inc(sg("moe_gu"), 1)
                    if c >= 1:
                        down(c - 1)
                    if c == SEL_AT + 3:
                        pe.wait_ge(sg("selg_ready"), NT * (e + 1))
                        for ct in range(NT):
                            for t in range(NT):
                                m = pe.transpose(ps[:, 6, (NT * ct + t) * P:(NT * ct + t + 1) * P], sel_g[:, t, ct * P:(ct + 1) * P], ident[:, :])
                        m.then_inc(sg("selg_tr"), 1)
                down(CHUNKS - 1)
                pe.wait_ge(sg("yT_ready"), 4 * (e + 1))
                tiles = 1 if V <= P else 2
                for ct in range(tiles):
                    for k in range(KD):
                        m = pe.transpose(ps[:, (6 if ct == 0 else 0) + k // 4, (k % 4) * P:(k % 4 + 1) * P],
                                         yT[:, k, ct * P:(ct + 1) * P], ident[:, :])
                    m.then_inc(sg("y_tr"), 1 if tiles == 2 else 2)
                pe.wait_ge(sg("selgT_ready"), e + 1)
                pe.wait_ge(sg("y_ready"), 4 * (e + 1))
                for b in range(4):
                    for ct in range(tiles):
                        kk = min(V - ct * P, P)
                        m = pe.matmul(ps[:, 2 + b, :], sel_gT[0:kk, ct, b // 2, :],
                                      (y_lo if ct == 0 else y_hi)[0:kk, (b % 2) * 512:(b % 2 + 1) * 512],
                                      start=ct == 0, stop=ct == tiles - 1)
                    m.then_inc(sg("scatter_mm"), 1)

            with pe.Fori(0, EXP) as e:
                n = pe.value_load(cnt_i[0:1, bass.ds(e, 1)], min_val=0, max_val=SEQ)
                with pe.If(n > WIDTHS[1]):
                    with pe.If(n > WIDTHS[2]):
                        expert(e, WIDTHS[3])
                    with pe.Else():
                        expert(e, WIDTHS[2])
                with pe.Else():
                    with pe.If(n > WIDTHS[0]):
                        expert(e, WIDTHS[1])
                    with pe.Else():
                        expert(e, WIDTHS[0])
            pe.wait_ge(sg("sel_ready"), NT * (EXP + 1))


_INS = ("x", "norm_gains", "ssm_w_in", "ssm_lambda_re", "ssm_lambda_im", "ssm_log_step", "ssm_b_re", "ssm_b_im",
        "ssm_c_re", "ssm_c_im", "ssm_d", "ssm_w_glu", "ssm_w_out", "ffn_w_gate", "ffn_w_up", "ffn_w_down",
        "attn_w_qkv", "attn_q_gain", "attn_k_gain", "attn_w_out", "moe_w_router", "moe_w_gate", "moe_w_up",
        "moe_w_down")


def rope_tables(seq, axis_dim, grid_w=64, theta=10000.0):
    import numpy as np
    freqs = np.float32(theta) ** (-np.arange(0, axis_dim, 2, dtype=np.float32) / np.float32(axis_dim))
    token = np.arange(seq)
    ang = np.concatenate([(token // grid_w).astype(np.float32)[:, None] * freqs,
                          (token % grid_w).astype(np.float32)[:, None] * freqs], axis=1).astype(np.float32)
    return np.cos(ang).astype(np.float32), np.sin(ang).astype(np.float32)


def build(nc, inputs):
    import numpy as np
    arrays = {f"in_{n}": np.ascontiguousarray(inputs[n]) for n in _INS}
    seq, head = arrays["in_x"].shape[1], arrays["in_attn_q_gain"].shape[1]
    arrays["rope_cos"], arrays["rope_sin"] = rope_tables(seq, head // 2)
    args = [nc.dram_tensor(n, a.shape, mybir.dt.from_np(a.dtype), kind="ExternalInput").ap() for n, a in arrays.items()]
    out = nc.dram_tensor("out", arrays["in_x"].shape, mybir.dt.float32, kind="ExternalOutput").ap()
    hybrid_trunk(nc, *args, out)
    return arrays, out


def kernel(**inputs):
    import concourse.bacc as bacc
    from concourse.bass_utils import run_bass_kernel_spmd
    nc = bacc.Bacc("TRN2", target_bir_lowering=False, num_devices=1)
    arrays, _ = build(nc, inputs)
    return run_bass_kernel_spmd(nc, [arrays], core_ids=[0]).results[0]["out"]
```

```python
import concourse.bass as bass
from concourse import mybir
from contextlib import ExitStack

WIDE = (144, 256)


def hybrid_trunk(nc, x_in, norm_gains, ssm_w_in, ssm_lambda_re, ssm_lambda_im, ssm_log_step,
                 ssm_b_re, ssm_b_im, ssm_c_re, ssm_c_im, ssm_d, ssm_w_glu, ssm_w_out,
                 ffn_w_gate, ffn_w_up, ffn_w_down, attn_w_qkv, attn_q_gain, attn_k_gain,
                 attn_w_out, moe_w_router, moe_w_gate, moe_w_up, moe_w_down,
                 rope_cos, rope_sin, out):
    f32, i32 = mybir.dt.float32, mybir.dt.int32
    ALU, ACT, AX = mybir.AluOpType, mybir.ActivationFunctionType, mybir.AxisListType
    MUL, ADD, SUB = ALU.mult, ALU.add, ALU.subtract

    P = 128
    SEQ, D = x_in.shape[1], x_in.shape[2]
    NT, KD = SEQ // P, D // P
    DIRS, GROUPS, ST = ssm_lambda_re.shape[1:]
    GC = D // GROUPS
    CH = P // GC
    NC = SEQ // CH
    GP = GROUPS // 2
    DG = DIRS * GP
    NPOW = CH + 1
    SB = 4
    NB = DG // SB
    EPS = 1e-6
    IW = 256
    ITEM = KD * IW
    SLOTS = 21
    FF_STEPS = ffn_w_gate.shape[2] // IW
    EXP, EFF = moe_w_gate.shape[1], moe_w_gate.shape[3]
    EX_STEPS = EFF // IW
    HALF = EX_STEPS // 2
    QKV = attn_w_qkv.shape[2]
    NH, HD = D // attn_q_gain.shape[1], attn_q_gain.shape[1]
    NKV = (QKV // HD - NH) // 2
    HPK = NH // NKV
    QK = NH + NKV
    assert HALF * 3 == SLOTS and EX_STEPS == 2 * HALF and CH * GC == P and NC * CH == SEQ

    ctx = ExitStack()
    with ctx:
        def sb(name, shape, dt=f32):
            return ctx.enter_context(nc.sbuf_tensor(name, shape, dt))

        sems = {}

        def sg(name):
            if name not in sems:
                sems[name] = ctx.enter_context(nc.semaphore(name))
            return sems[name]

        BIGW = 53056
        big = sb("big", [P, BIGW])
        cnt_i = sb("cnt_i", [1, EXP], i32)
        ps = ctx.enter_context(nc.psum_tensor("ps", [P, 8, 512], f32))
        x_scr = nc.dram_tensor("x_scr", (P, NT * D), f32, kind="Internal").ap()
        k_scr = nc.dram_tensor("k_scr", (GROUPS, GC, 15 * GC), f32, kind="Internal").ap()

        def at(off, *shape):
            n = 1
            for s in shape:
                n *= s
            assert off + n <= BIGW
            v = big[:, off:off + n]
            if len(shape) == 1:
                return v
            names = "abcd"[:len(shape)]
            return v.rearrange(f"p ({' '.join(names)}) -> p {' '.join(names)}",
                               **{names[i]: shape[i] for i in range(len(shape) - 1)})

        TOP = BIGW - 448
        ident = at(TOP, P)
        gcol = at(TOP + 128, 64)
        ssq = at(TOP + 192, 2)
        msq = at(TOP + 194, 2)
        rstd = at(TOP + 196, 2)
        nhalf = at(TOP + 198, 48)
        hms = at(TOP + 246, 48)
        hrs = at(TOP + 294, 48)
        small = at(TOP + 342, 106)

        def slot(n):
            return at((n % SLOTS) * ITEM, KD, IW)

        def slot_down(n):
            return at((n % SLOTS) * ITEM, 2, D)

        RA, RDS, RC, REZ, RB = 0, 8192, 20480, 28672, 36864
        X_, HT, N1, R8_ = 45056, 47104, 49152, 51200
        x = at(X_, NT, D)
        hT = at(HT, KD, SEQ)
        nat = at(N1, NT, D)
        nat_flat = at(N1, NT * D)
        post_gain = at(R8_, D)
        w_in = at(RA, 4, KD, IW)
        xbd = at(RA, 2, DG, 2, NC)
        u_grp = at(RA, GROUPS, CH, GC)
        u_tok = at(RB, CH, D)
        w_glu = at(RB, 4, KD, IW)
        w_out0 = at(REZ, 4, KD, IW)
        bbar = at(RDS, 2, DG + 1, GC)
        cP = at(RDS + 2080, 2, DG, GC)
        S_ = at(RDS + 4128, 2, DG, NC)
        bP = at(RDS + 4128, 2, DG, GC)
        pw = at(RDS + 8224, 2, NPOW, DG)
        pd = at(RDS + 9376, 2, NPOW, DG)
        def tmp(n):
            assert n < 27
            return at(RDS + 10528 + 64 * n, DG)
        yg = at(RDS + 4128, GROUPS, NC)
        gT = at(RDS + 4128 + 2048, KD, SEQ)
        mT = hT
        wt = [at(RC + 1024 * i, 2, SB, P) for i in range(2)]
        wm = [at(RC + 2048 + 1024 * i, SB, 2, P) for i in range(2)]
        kall = at(RC, 2, 8, 15, GC)
        kzero = at(RC + 3840, 2, 8, GC)
        mtmp = [at(RC + 5800 + 576 * i, SB * NPOW * GC) for i in range(4)]
        ptmp = [mtmp[2:4], [at(RC + 4100 + 576 * i, SB * NPOW * GC) for i in range(2)]]
        toe = [at(REZ, GROUPS // 2, P), at(RC + 4096, GROUPS // 2, P)]
        g_tok = at(RA, CH, D)
        ec = at(REZ, 2, DG, NC)
        zz = at(REZ + 4096, 2, DG, NC)
        vv = [at(i, 2, SB, NPOW, GC) for i in (N1 + 1024, RB + 3 * ITEM)]
        raw_b = at(RB, 2, P, GC)
        raw_c = at(RB + 4096, 2, GC, P)
        raw_l = at(REZ, 4, P)
        raw_g = at(REZ + 512, P)
        raw_s = at(REZ + 640, 2)
        raw_d = at(REZ + 704, GC)
        raw_dx = at(REZ + 768, CH, GC)
        uc = at(HT, GROUPS, NC)
        ud = at(N1, GROUPS, NC)
        tmp8 = at(N1, GP, NC)
        r8t = at(N1 + 1024 + 1152, GP, NC)
        sig = at(N1, KD, SEQ)
        dcol = at(52352, GROUPS)

        sil = [at(43008 + 256 * i, SEQ) for i in range(2)]
        hid = [at(43520 + 256 * i, SEQ) for i in range(2)]
        qkv = at(43008, NT, QKV)
        kT = at(46080, NKV, SEQ)
        qT = hT
        k_dup = at(N1, NT, NKV, 2, HD)
        rope_m = [at(HT + 512 * i, NH, HD // 2) for i in range(4)]
        o_nat = qkv
        prob = [at(N1 + 512 * i, 2, SEQ) for i in range(2)]
        probT = [at(N1 + 1024 + 512 * i, 2, NT, P) for i in range(2)]
        rope_raw = at(52224, 2, NT, HD // 2)
        qk_gain = at(52352, 2, HD)
        rope_t = at(N1 + 1280, 2, 4, NT, HD // 2)
        nmax, psum_, prcp = (small[:, 32 * i:32 * i + 32] for i in range(3))
        UNITS = NT * NH // 2
        h_moe = nat
        acc = x
        xg = hT
        yT = hT
        moe_gain = at(44032, D)
        y_lo = at(43008, D)
        y_hi = at(HT, D)
        sel_g = at(43008, NT, SEQ)
        sel = at(44032, NT, SEQ)
        sel_gT = at(44544, NT, NT, P)
        m_hidT = [at(43520 + 256 * i, SEQ) for i in range(2)]
        m_sil = [at(51200 + 256 * i, SEQ) for i in range(2)]
        m_hid = [at(51712 + 256 * i, SEQ) for i in range(2)]
        iota = at(52224, SEQ)
        iota_i = at(43700, SEQ).bitcast(i32)
        rank = at(52480, NT, EXP + 1)
        chosen = at(52498, NT, EXP + 1)
        gate = at(52516, NT, EXP + 1)
        w_router = gcol.rearrange("p (k e) -> p k e", k=KD)
        upper = at(43008, P)
        ones = at(43136, P)
        lower_e = at(43264, EXP, EXP)
        gt_ = at(43328, NT, EXP, EXP)
        eq_ = at(43456, NT, EXP, EXP)
        logit = at(43584, NT, EXP)
        lshift = at(43600, NT, EXP)
        wexp = at(43616, NT, EXP)
        beats = at(43632, NT, EXP)
        lmax = at(43648, NT)
        wsum = at(43650, NT)
        last_gain = at(((3 * FF_STEPS + QKV // IW + D // IW + EXP * 3 * EX_STEPS) % SLOTS) * ITEM, D)
        SEL_AT = 3
        CHUNKS = EFF // P
        EI = 3 * EX_STEPS

        block = ctx.enter_context(nc.Block())
        w_in_v = [w[0].rearrange("(k p) n -> p k n", p=P) for w in (ssm_w_in, ssm_w_glu, ssm_w_out)]

        def cols(w, j):
            return w.rearrange("(k p) n -> p k n", p=P)[:, :, j * IW:(j + 1) * IW]

        def rows(w, j):
            return w[j * IW:(j + 1) * IW, :].rearrange("(f p) n -> p f n", p=P)

        items = []
        for j in range(FF_STEPS):
            items += [cols(ffn_w_gate[0], j), cols(ffn_w_up[0], j), rows(ffn_w_down[0], j)]
        ITEM_QKV = len(items)
        items += [cols(attn_w_qkv[0], j) for j in range(QKV // IW)]
        ITEM_WO = len(items)
        items += [cols(attn_w_out[0], j) for j in range(D // IW)]
        ITEM_MOE = len(items)
        full = [f"item_in_slot{n}" for n in range(SLOTS)]

        def item_full(n):
            return sg(full[n % SLOTS]), 16 * (n // SLOTS + 1)

        TR_BANKS = ((0, 1, 2, 3), (4, 5, 6, 7), (0, 1, 6, 7), (0, 1, 2, 3))

        def item_read(n):
            if n == ITEM_QKV - 1:
                return sg("mix_done"), 2 * NT
            if n >= ITEM_WO:
                return sg("mix_done"), 3 * NT
            if n < ITEM_QKV:
                return sg("gu_done" if n % 3 < 2 else "down_done"), 2 * (n // 3) + 2
            return sg("proj_done"), n - ITEM_QKV + 1

        def moe_item_full(e, m):
            n = ITEM_MOE + m
            return sg(full[n % SLOTS]), 16 * (n // SLOTS + 1) + 32 * e

        @block.sync
        def _(sp):
            for t in range(NT):
                sp.dma_start(x[:, t, :], x_in[0, t * P:(t + 1) * P, :]).then_inc(sg(f"x_in{t}"), 16)
            lam_v = [w[0].rearrange("d (g a) p -> (d g) (a p)", a=2) for w in (ssm_lambda_re, ssm_lambda_im)]
            for i in range(2):
                sp.dma_start(raw_l[0:DG, i, :], lam_v[i]).then_inc(sg("lam_in"), 16)
            sp.dma_start(raw_s[0:DG, :], ssm_log_step[0].rearrange("d (g a) -> (d g) a", a=2)).then_inc(sg("lam_in"), 16)
            sp.dma_start(raw_g[0:64, :], norm_gains.rearrange("l n (k p) -> (l n k) p", p=P)).then_inc(sg("gain_in"), 16)
            sp.dma_start(raw_d[0:GROUPS, :], ssm_d[0].rearrange("(g s) -> g s", s=GC)).then_inc(sg("gain_in"), 16)
            for i, w in enumerate((ssm_b_re, ssm_b_im)):
                sp.dma_start(raw_b[0:DG, i, :, :], w[0].rearrange("d (g a) p s -> (d g) (a p) s", a=2)).then_inc(sg("b_in"), 16)
            for i, w in enumerate((ssm_c_re, ssm_c_im)):
                for a in range(2):
                    sp.dma_start(raw_c[0:DG, i, :, a * ST:(a + 1) * ST],
                                 w[0].rearrange("d (g a) s p -> a (d g) s p", a=2)[a]).then_inc(sg("c_in"), 16)
            for i in range(4):
                sp.dma_start(w_in[:, i, :, :], w_in_v[0][:, :, i * IW:(i + 1) * IW]).then_inc(sg(f"mix_w{i}"), 16)
            for t in range(NT):
                sp.wait_ge(sg("u_act"), t + 1)
                sp.wait_ge(sg("u_dve"), t + 1)
                for s in range(CH):
                    sp.dma_start(u_tok[16 * t:16 * t + 16, s, :], nat[s:P:CH, t, :]).then_inc(sg("u_tok_in"), 16)
            sp.wait_ge(sg("u_grp_ready"), 2)
            for i in range(3):
                sp.dma_start(w_glu[:, i, :, :], w_in_v[1][:, :, i * IW:(i + 1) * IW]).then_inc(sg(f"mix_w{i}"), 16)
            k_w = k_scr.rearrange("(q j a) s x -> j a s q x", j=SB, a=2)
            for hf in range(2):
                qs = slice(4 * hf, 4 * hf + 4)
                sp.wait_ge(sg("k_final"), hf + 1)
                for j in range(SB):
                    for a in range(2):
                        sp.dma_start(k_w[j, a, :, qs], kall[32 * j:32 * j + GC, a, qs, :, :].rearrange("p q t o -> p q (t o)")).then_inc(sg("k_stored"), 16)
                sp.wait_ge(sg("k_stored"), 16 * 2 * SB * (hf + 1))
                if hf == 0:
                    sp.wait_ge(sg("x_ready"), 8)
                else:
                    sp.wait_ge(sg("y_state"), NB)
                for s in range(CH):
                    sp.dma_start(toe[hf][GC * s:GC * (s + 1), :, :],
                                 k_scr[32 * hf:32 * hf + 32].rearrange("g s x -> s g x")[:, :, (CH - 1 - s) * GC:(CH - 1 - s) * GC + P]).then_inc(sg(f"toe_in{hf}"), 16)
            sp.dma_start(w_glu[:, 3, :, :], w_in_v[1][:, :, 3 * IW:4 * IW]).then_inc(sg("glu_w3"), 16)
            for i in (2, 3, 0, 1):
                if i == 0:
                    sp.wait_ge(sg("y_mm"), 2)
                sp.dma_start(w_out0[:, i, :, :], w_in_v[2][:, :, i * IW:(i + 1) * IW]).then_inc(sg(f"mix_w{i}"), 16)
            sp.dma_start(post_gain[:, :], norm_gains[0, 1:2, :].to_broadcast([P, D])).then_inc(sg("post_gain_in"), 16)
            for n, src in enumerate(items):
                if n == 0:
                    sp.wait_ge(sg("gT_tr"), 4)
                if n == 4:
                    sp.wait_ge(sg("m_ready"), 8)
                if n == 14:
                    sp.wait_ge(sg("mix_done"), NT)
                if n >= SLOTS:
                    sp.wait_ge(*item_read(n - SLOTS))
                dst = slot_down(n) if (n < ITEM_QKV and n % 3 == 2) else slot(n)
                sp.dma_start(dst, src).then_inc(sg(full[n % SLOTS]), 16)
                if n == SLOTS - 1:
                    sp.wait_ge(sg("x_done"), 2)
                    sp.dma_start(post_gain[:, :], norm_gains[0, 3:4, :].to_broadcast([P, D])).then_inc(sg("post_gain_in"), 16)
                    for i, w in enumerate((rope_cos, rope_sin)):
                        sp.dma_start(rope_raw[:, i], w.rearrange("(t p) f -> p t f", p=P)).then_inc(sg("rope_in"), 16)
                    for i, w in enumerate((attn_q_gain, attn_k_gain)):
                        sp.dma_start(qk_gain[:, i], w[0:1, :].to_broadcast([P, HD])).then_inc(sg("rope_in"), 16)
            def moe_item(e, m):
                j, kind = divmod(m, 3)
                js = slice(j * IW, (j + 1) * IW)
                if kind < 2:
                    w = (moe_w_gate, moe_w_up)[kind][0, bass.ds(e, 1), :, js].rearrange("e (k p) n -> p (e k) n", p=P)
                    dst = slot(ITEM_MOE + m)
                else:
                    w = moe_w_down[0, bass.ds(e, 1), js, :].rearrange("e (f p) n -> p (e f) n", p=P)
                    dst = slot_down(ITEM_MOE + m)
                sp.dma_start(dst, w).then_inc(sg(full[(ITEM_MOE + m) % SLOTS]), 16)

            def moe_wait_read(e, m):
                prev = m - SLOTS + (EI if m < SLOTS else 0)
                expert = e - 1 if m < SLOTS else e
                sp.wait_ge(sg("moe_gu" if prev % 3 < 2 else "moe_down"), CHUNKS * expert + 2 * (prev // 3) + 2)

            sp.wait_ge(sg("x_done"), 4)
            sp.dma_start(x_scr[:, :], x.rearrange("p t d -> p (t d)")).then_inc(sg("x_stored"), 16)
            sp.dma_start(post_gain[:, :], norm_gains[1, 1:2, :].to_broadcast([P, D])).then_inc(sg("post_gain_in"), 16)
            qkv_m = ITEM_WO - (ITEM_MOE - SLOTS)
            for m in range(0, qkv_m):
                sp.wait_ge(*item_read(ITEM_MOE - SLOTS + m))
                moe_item(0, m)
            sp.wait_ge(sg("oT_tr"), 4)
            sp.wait_ge(sg("x_stored"), 16)
            sp.dma_start(x.rearrange("p t d -> p (t d)"), x_scr[:, :]).then_inc(sg("x_back"), 16)
            sp.dma_start(moe_gain[:, :], norm_gains[1, 2:3, :].to_broadcast([P, D])).then_inc(sg("moe_gain_in"), 16)
            sp.dma_start(w_router, moe_w_router[0].rearrange("(k p) e -> p k e", p=P)).then_inc(sg("router_in"), 16)
            for m in range(qkv_m, SLOTS):
                sp.wait_ge(*item_read(ITEM_MOE - SLOTS + m))
                moe_item(0, m)
            sp.wait_ge(sg("x_done"), 6)
            sp.dma_start(x_scr[:, :], x.rearrange("p t d -> p (t d)")).then_inc(sg("x_stored"), 16)
            for m in range(SLOTS, EI):
                moe_wait_read(0, m)
                moe_item(0, m)
            with sp.Fori(1, EXP) as e:
                for m in range(EI):
                    moe_wait_read(e, m)
                    moe_item(e, m)
            sp.wait_ge(sg("moe_gu"), CHUNKS * (EXP - 1) + 2 * HALF + 2)
            sp.dma_start(last_gain[:, :], norm_gains[1, 3:4, :].to_broadcast([P, D])).then_inc(sg("last_gain_in"), 16)
            sp.wait_ge(sg("gather_mm"), 4 * EXP)
            sp.wait_ge(sg("x_stored"), 32)
            sp.dma_start(nat.rearrange("p t d -> p (t d)"), x_scr[:, :]).then_inc(sg("x_back"), 16)
            for t in range(NT):
                sp.wait_ge(sg("y_final"), t + 1)
                sp.dma_start(out[0, t * P:(t + 1) * P, :], acc[:, t, :]).then_inc(sg("out_stored"), 16)
            sp.wait_ge(sg("out_stored"), 16 * NT)

        @block.gpsimd
        def _(pool):
            step = [0]

            def link(ins):
                step[0] += 1
                ins.then_inc(sg("pool_step"), 1)
                pool.wait_ge(sg("pool_step"), step[0])

            link(pool.memset(ident[:, :], 0.0))
            pool.affine_select(out=ident[:, :], in_=ident[:, :], compare_op=ALU.not_equal, fill=1.0,
                               base=0, pattern=[[-1, P]], channel_multiplier=1).then_inc(sg("ident_ready"), 1)
            pool.memset(bbar[:, :, DG, :], 0.0).then_inc(sg("bbar_pad"), 1)
            link(pool.memset(nhalf[:, :], -0.5))

            def rstd_of(n):
                for t in range(NT):
                    pool.wait_ge(sg("ms_ready"), NT * n + t + 1)
                    pool.tensor_tensor(rstd[:, t:t + 1], msq[:, t:t + 1], nhalf[:, 0:1], ALU.pow).then_inc(sg("rstd_ready"), 1)

            def rstd_pair(n):
                for t in range(NT):
                    for i in range(2):
                        pool.wait_ge(sg("ms_ready"), NT * n + 2 * t + i + 1)
                        pool.tensor_tensor(rstd[:, t:t + 1], msq[:, t:t + 1], nhalf[:, 0:1], ALU.pow).then_inc(sg("rstd_ready"), 1)

            rstd_of(0)
            pool.wait_ge(sg("bbar_ready"), 1)
            for b in range(NB):
                d, q = divmod(b, NB // 2)
                s = slice(SB * b, SB * (b + 1))
                pt = pd[:, :, 1:NPOW, s] if d == 0 else pw[:, :, 0:CH, s]
                if b >= 2:
                    pool.wait_ge(sg("wt_ready"), b - 1)
                for i, (bi, ti) in enumerate(((0, 1), (1, 0))):
                    pool.tensor_tensor(ptmp[b % 2][i][:, 0:SB * P].rearrange("p (g s i) -> p g s i", g=SB, s=CH),
                                       bbar[:, bi, s, :].unsqueeze(2).to_broadcast([P, SB, CH, GC]),
                                       pt[:, ti].rearrange("p s g -> p g s").unsqueeze(3).to_broadcast([P, SB, CH, GC]),
                                       MUL).then_inc(sg("wt_pool"), 1)
                if b >= NB - 8:
                    if b == NB - 8:
                        pool.wait_ge(sg("uc_tr"), 4)
                    z = b - (NB - 8)
                    pool.memset(xbd.rearrange("p r g a c -> p (r g a c)")[:, z * 1024:(z + 1) * 1024], 0.0).then_inc(sg("xbd_zero"), 1)
            for b in range(NB):
                d, q = divmod(b, NB // 2)
                s = slice(SB * b, SB * (b + 1))
                pt = pw[:, :, :, s] if d == 0 else pd[:, :, :, s]
                pool.wait_ge(sg("wt_ready"), NB - 1 + b) if b < 2 else pool.wait_ge(sg("v_ready"), b - 1)
                for i, (ci, ti) in enumerate(((0, 1), (1, 0))):
                    pool.tensor_tensor(ptmp[b % 2][i].rearrange("p (g s i) -> p g s i", g=SB, s=NPOW),
                                       cP[:, ci, s, :].unsqueeze(2).to_broadcast([P, SB, NPOW, GC]),
                                       pt[:, ti].rearrange("p s g -> p g s").unsqueeze(3).to_broadcast([P, SB, NPOW, GC]),
                                       MUL).then_inc(sg("v_pool"), 1)
            rstd_pair(1)
            rstd_pair(3)
            pool.wait_ge(sg("head_ms"), 1)
            pool.tensor_tensor(hrs[:, 0:NT * QK], hms[:, 0:NT * QK], nhalf[:, 0:NT * QK], ALU.pow).then_inc(sg("head_rstd"), 1)
            pool.wait_ge(sg("oT_tr"), 4)
            link(pool.memset(upper[:, :], 1.0))
            link(pool.affine_select(out=upper[:, :], in_=upper[:, :], compare_op=ALU.is_gt, fill=0.0,
                                    base=0, pattern=[[1, P]], channel_multiplier=-1))
            link(pool.memset(ones[:, :], 1.0))
            link(pool.memset(lower_e[:, :, :], 1.0))
            link(pool.affine_select(out=lower_e[:, :, :], in_=lower_e[:, :, :], compare_op=ALU.is_gt, fill=0.0,
                                    base=0, pattern=[[1, EXP], [-1, EXP]], channel_multiplier=0))
            for v in (rank, chosen, gate):
                link(pool.memset(v[:, :, EXP:EXP + 1], 0.0))
            link(pool.iota(iota_i, pattern=[[1, SEQ]], base=0, channel_multiplier=0))
            pool.tensor_copy(iota[:, :], iota_i).then_inc(sg("route_consts"), 1)
            rstd_pair(5)
            pool.wait_ge(sg("x_stored"), 32)
            pool.wait_ge(sg("nat_ready"), 8)
            pool.wait_ge(sg("ssq_ready"), 14)
            pool.memset(acc[:, :, :], 0.0).then_inc(sg("acc_done"), 1)
            rstd_of(7)

        @block.scalar
        def _(act):
            step = [0]

            def link(ins):
                step[0] += 1
                ins.then_inc(sg("act_step"), 1)
                act.wait_ge(sg("act_step"), step[0])

            def nat_sq(t, src):
                return nat[:, t, :] if len(src.shape) == 2 else nat[:, t, :].rearrange("p (a b) -> p a b", a=2)

            def sum_squares(t, src):
                act.activation(nat_sq(t, src), src, ACT.Square, accum_out=ssq[:, t:t + 1]).then_inc(sg("ssq_ready"), 1)

            def norm_sums(n, bank):
                for t in range(NT):
                    act.wait_ge(sg("mix_done"), NT * n + t + 1)
                    sum_squares(t, ps[:, bank + 2 * t:bank + 2 * t + 2, :])
                    act.wait_ge(sg("x_done"), NT * n + t + 1)
                    sum_squares(t, x[:, t, :])

            def hT_half(n, gain):
                for b in (0, 2):
                    act.wait_ge(sg("tr_ready"), 4 * n + b + 1)
                    for k in (2 * b, 2 * b + 1):
                        ins = act.activation(hT[:, k, :], ps[:, TR_BANKS[n][b], (k % 2) * SEQ:(k % 2 + 1) * SEQ], ACT.Copy,
                                             scale=1.0 if gain is None else gcol[:, gain * 8 + k:gain * 8 + k + 1])
                    ins.then_inc(sg("hT_ready"), 1)

            for t in range(NT):
                act.wait_ge(sg(f"x_in{t}"), 16)
                sum_squares(t, x[:, t, :])
            act.wait_ge(sg("lam_copied"), 1)
            act.activation(tmp(2), ps[:, 4, 128:192], ACT.Exp).then_inc(sg("step_ready"), 1)
            act.wait_ge(sg("ang_ready"), 1)
            act.activation(tmp(4), tmp(3), ACT.Exp).then_inc(sg("mag_ready"), 1)
            act.activation(tmp(7), tmp(5), ACT.Sin).then_inc(sg("mag_ready"), 1)
            act.activation(tmp(8), tmp(6), ACT.Sin).then_inc(sg("mag_ready"), 1)
            for i in range(2):
                act.wait_ge(sg("bc_tr"), 2 * i + 2)
                bank = 5 if i == 0 else 6
                for h in range(2):
                    act.activation(bP[:, i, :, 8 * h:8 * h + 8].rearrange("p g s -> p s g"),
                                   ps[:, 5 + h, :].rearrange("p (s g) -> p s g", g=DG), ACT.Copy).then_inc(sg("bc_out"), 1)
            for i in range(2):
                act.wait_ge(sg("bc_tr"), 4 + 2 * i + 2)
                for h in range(2):
                    act.activation(cP[:, i, :, 8 * h:8 * h + 8].rearrange("p g s -> p s g"),
                                   ps[:, 5 + h, :].rearrange("p (s g) -> p s g", g=DG), ACT.Copy).then_inc(sg("bc_out"), 1)
            act.wait_ge(sg("gain_tr"), 1)
            act.activation(gcol[:, :], ps[:, 7, 0:64], ACT.Copy).then_inc(sg("gcol_ready"), 1)
            act.wait_ge(sg("gcol_ready"), 1)
            hT_half(0, 0)
            act.wait_ge(sg("pw_ready"), 1)
            for k in range(NPOW):
                ins = act.activation(pd[:, :, k, :], pw[:, :, CH - k, :], ACT.Copy)
            ins.then_inc(sg("pd_ready"), 1)
            for t in range(NT):
                act.wait_ge(sg("u_mm"), t + 1)
                act.activation(nat[:, t, 0:512], ps[:, 2 * t, :], ACT.Copy).then_inc(sg("u_act"), 1)
            act.wait_ge(sg("u_tok_in"), 16 * NT * CH)
            GA = 28
            act.activation(u_grp[0:NC, 0:GA].rearrange("p g s i -> p s g i"),
                           u_tok[0:NC, :, 0:GA * GC].rearrange("p s (g i) -> p s g i", i=GC), ACT.Copy).then_inc(sg("u_grp_ready"), 1)
            for b in range(4):
                act.wait_ge(sg("uc_tr"), b + 1)
                act.activation(uc[:, 16 * b:16 * b + 16, :].rearrange("p g c -> p (g c)"), ps[:, b, :], ACT.Copy).then_inc(sg("uc_ready"), 1)
            for b in range(NB):
                if b >= 2:
                    act.wait_ge(sg("s_mm"), b - 1)
                for h in range(2):
                    act.wait_ge(sg("w_tr"), 2 * b + h + 1)
                    act.activation(wm[b % 2][:, 2 * h:2 * h + 2, :, :].rearrange("p g r q -> p (g r q)"),
                                   ps[:, 2 * (b % 2) + h, :], ACT.Copy).then_inc(sg("w_out_act"), 1)
                if b >= 1:
                    act.wait_ge(sg("s_mm"), b)
                    act.activation(S_[:, :, SB * (b - 1):SB * b, :].rearrange("p r g c -> p r (g c)"),
                                   ps[:, 4 + (b - 1) % 2, 0:256].rearrange("p (r x) -> p r x", r=2), ACT.Copy).then_inc(sg("s_out"), 1)
            act.wait_ge(sg("s_mm"), NB)
            act.activation(S_[:, :, SB * (NB - 1):SB * NB, :].rearrange("p r g c -> p r (g c)"),
                           ps[:, 4 + (NB - 1) % 2, 0:256].rearrange("p (r x) -> p r x", r=2), ACT.Copy).then_inc(sg("s_out"), 1)
            def states_placed(d):
                g = slice(GP * d, GP * (d + 1))
                for r in range(2):
                    act.wait_ge(sg("x_nat"), 2 * d + r + 1)
                    for a in range(2):
                        h = slice(64 * a, 64 * a + 64)
                        act.activation(xbd[h, r, g, a, 1:NC], zz[h, r, g, 0:NC - 1], ACT.Copy).then_inc(sg("x_ready"), 1)

            act.wait_ge(sg("xbd_zero"), 8)
            states_placed(0)
            for b in range(NB):
                d, q = divmod(b, NB // 2)
                act.wait_ge(sg("k_mm"), b + 1)
                lo = CH - 1 if d == 0 else 0
                if d == 0:
                    ins = act.activation(kall[:, :, q, CH - 1:15, :],
                                         ps[:, 4 + 2 * (b % 2):6 + 2 * (b % 2), 0:P].rearrange("p a (t o) -> p a t o", o=GC), ACT.Copy)
                else:
                    ins = act.activation(kall[:, :, q, 0:CH - 1, :],
                                         ps[:, 4 + 2 * (b % 2):6 + 2 * (b % 2), 0:(CH - 1) * GC].rearrange("p a (t o) -> p a t o", o=GC), ACT.Copy)
                if d == 1:
                    ins = act.activation(kzero[:, :, q, :],
                                         ps[:, 4 + 2 * (b % 2):6 + 2 * (b % 2), (CH - 1) * GC:CH * GC], ACT.Copy)
                ins.then_inc(sg("k_out"), 1)
                if b == NB // 2 - 1:
                    states_placed(1)
            for b in range(5):
                if b < 4:
                    act.wait_ge(sg("y_sum"), b + 1)
                    act.activation(yg[:, 16 * b:16 * b + 16, :], yg[:, 16 * b:16 * b + 16, :], ACT.Gelu_apprx_tanh).then_inc(sg("gelu"), 1)
                if b >= 1:
                    for r in range(4 * (b - 1), 4 * b, 2):
                        act.wait_ge(sg("g_tr"), r + 1)
                        act.activation(g_tok[0:NC, :, 64 * r:64 * r + 64].rearrange("c t (g o) -> c g t o", o=GC),
                                       ps[0:NC, 4 + r % 4, :].rearrange("c (g t o) -> c g t o", g=4, t=CH), ACT.Copy).then_inc(sg("g_tok_act"), 1)
            for b in (0, 2):
                act.wait_ge(sg("gT_tr"), b + 1)
                act.activation(gT[:, 2 * b:2 * b + 2, :].rearrange("p k (c t) -> p k t c", t=CH),
                               ps[:, b, :].rearrange("p (k t c) -> p k t c", k=2, t=CH), ACT.Copy).then_inc(sg("gT_ready"), 1)
            for m in range(KD):
                act.wait_ge(sg("glu_mm"), m + 1)
                act.activation(sig[:, m, :], ps[:, 4 + m % 4, 0:SEQ], ACT.Sigmoid).then_inc(sg("sig_ready"), 1)
            norm_sums(0, 0)
            hT_half(1, 2)
            for c in range(2 * FF_STEPS):
                act.wait_ge(sg("gu_done"), c + 1)
                if c >= 2:
                    act.wait_ge(sg("hid_ready"), c - 1)
                act.activation(sil[c % 2], ps[:, c % 2, 0:SEQ], ACT.Silu).then_inc(sg("sil_ready"), 1)
            norm_sums(1, 2)
            hT_half(2, 4)
            act.wait_ge(sg("proj_done"), QKV // IW)
            act.wait_ge(sg("x_stored"), 16)
            act.activation(qkv[:, 0, :].rearrange("p (b n) -> p b n", b=3), ps[:, 0:3, :], ACT.Copy).then_inc(sg("qkv_act"), 1)
            act.wait_ge(sg("qkv_act"), 1)
            act.activation(nat_flat[:, 0:QK * HD], qkv[:, 0, 0:QK * HD], ACT.Square).then_inc(sg("head_sq"), 1)
            act.wait_ge(sg("qkv_dve"), 1)
            act.wait_ge(sg("head_sum"), 1)
            act.activation(nat_flat[:, 0:QK * HD], qkv[:, 1, 0:QK * HD], ACT.Square).then_inc(sg("head_sq"), 1)
            for b in (0, 2):
                act.wait_ge(sg("q_tr"), b + 1)
                act.activation(qT[:, 2 * b:2 * b + 2, :], ps[:, b, :].rearrange("p (k n) -> p k n", k=2), ACT.Copy).then_inc(sg("qT_ready"), 1)
            act.wait_ge(sg("k_tr"), 1)
            act.activation(kT[:, 0:2, :], ps[:, 4, :].rearrange("p (k n) -> p k n", k=2), ACT.Copy).then_inc(sg("qT_ready"), 1)
            for u in range(UNITS):
                act.wait_ge(sg("smax_ready"), u + 1)
                if u >= 2:
                    act.wait_ge(sg("p_tr"), u - 1)
                for h in range(2):
                    act.activation(prob[u % 2][:, h, :], ps[:, 2 * (u % 2) + h, 0:SEQ], ACT.Exp, bias=nmax[:, 2 * u + h:2 * u + h + 1],
                                   scale=HD ** -0.5, accum_out=psum_[:, 2 * u + h:2 * u + h + 1]).then_inc(sg("probs_ready"), 1)
            for b in (0, 2):
                act.wait_ge(sg("oT_tr"), b + 1)
                act.activation(hT[:, 2 * b:2 * b + 2, :], ps[:, b, :].rearrange("p (k n) -> p k n", k=2), ACT.Copy).then_inc(sg("hT_ready"), 1)
            norm_sums(2, 4)
            hT_half(3, None)
            act.wait_ge(sg("logits_shifted"), 1)
            act.activation(wexp, lshift, ACT.Exp).then_inc(sg("logits_exp"), 1)
            act.wait_ge(sg("counts_ready"), 1)

            def gathered(e, other, count):
                for b in (0, 2):
                    act.wait_ge(sg("gather_mm"), 4 * e + b + 1)
                    ins = act.activation(xg[:, 2 * b:2 * b + 2, :], ps[:, b, :].rearrange("p (k n) -> p k n", k=2), ACT.Copy)
                    if b == 2:
                        ins.then_inc(sg("xg_ready"), 2)
                    else:
                        ins.then_inc(sg(other), count)

            def selection_transposed(e):
                act.wait_ge(sg("selg_tr"), e + 1)
                act.activation(sel_gT.rearrange("p a b n -> p (a b n)"), ps[:, 6, :], ACT.Copy).then_inc(sg("selgT_ready"), 1)

            def expert_narrow(e):
                gathered(e, "yT_ready", 4)
                for s in range(EX_STEPS + 1):
                    if s < EX_STEPS:
                        act.wait_ge(sg("moe_gu"), CHUNKS * e + 2 * s + 2)
                        if s >= 2:
                            act.wait_ge(sg("moe_hid"), CHUNKS * e + 2 * (s - 1))
                        act.activation(m_sil[s % 2], ps[:, s % 2, 0:SEQ], ACT.Silu).then_inc(sg("moe_sil"), 2)
                    if s >= 1:
                        act.wait_ge(sg("hid_tr"), EX_STEPS * e + s)
                        if s >= 3:
                            act.wait_ge(sg("moe_down"), CHUNKS * e + 2 * (s - 2))
                        act.activation(m_hidT[(s - 1) % 2], ps[:, 4 + (s - 1) % 2, 0:SEQ], ACT.Copy).then_inc(sg("hidT_ready"), 1)
                    if s == SEL_AT + 1:
                        selection_transposed(e)
                act.wait_ge(sg("moe_down"), CHUNKS * (e + 1))
                act.activation(y_lo[:, 0:512], ps[:, 2, :], ACT.Copy).then_inc(sg("y_ready"), 2)

            def expert_wide(e):
                gathered(e, "hidT_ready", EX_STEPS)
                for c in range(CHUNKS):
                    act.wait_ge(sg("moe_gu"), CHUNKS * e + c + 1)
                    if c >= 2:
                        act.wait_ge(sg("moe_hid"), CHUNKS * e + c - 1)
                    act.activation(m_sil[c % 2], ps[:, c % 2, 0:SEQ], ACT.Silu).then_inc(sg("moe_sil"), 1)
                    if c == SEL_AT + 4:
                        selection_transposed(e)
                act.wait_ge(sg("moe_down"), CHUNKS * (e + 1))
                for b in (0, 2):
                    act.activation(yT[:, 2 * b:2 * b + 2, :], ps[:, 2 + b, :].rearrange("p (k n) -> p k n", k=2), ACT.Copy).then_inc(sg("yT_ready"), 1)
                act.wait_ge(sg("y_tr"), 2 * e + 1)
                act.activation(y_lo[:, 0:512], ps[:, 6, :], ACT.Copy).then_inc(sg("y_ready"), 1)
                act.wait_ge(sg("y_tr"), 2 * e + 2)
                act.activation(y_hi[:, 0:512], ps[:, 0, :], ACT.Copy).then_inc(sg("y_ready"), 1)

            with act.Fori(0, EXP) as e:
                n = act.value_load(cnt_i[0:1, bass.ds(e, 1)], min_val=0, max_val=SEQ)
                with act.If(n > P):
                    expert_wide(e)
                with act.Else():
                    expert_narrow(e)
            act.wait_ge(sg("scatter_mm"), 4 * EXP)
            for t in range(NT):
                act.wait_ge(sg("acc_done"), 4 * EXP + 1)
                act.activation(hT.rearrange("p k n -> p (k n)")[:, t * D:(t + 1) * D], acc[:, t, :], ACT.Square,
                               accum_out=ssq[:, t:t + 1]).then_inc(sg("ssq_ready"), 1)

        @block.vector
        def _(dve):
            step = [0]

            def link(ins):
                step[0] += 1
                ins.then_inc(sg("dve_step"), 1)
                dve.wait_ge(sg("dve_step"), step[0])

            def tt(o, a, b, op):
                link(dve.tensor_tensor(o, a, b, op))

            def mean_square(n, t):
                dve.wait_ge(sg("ssq_ready"), n + 1)
                dve.tensor_scalar(msq[:, t:t + 1], ssq[:, t:t + 1], 1.0 / D, EPS, MUL, ADD).then_inc(sg("ms_ready"), 1)
                dve.wait_ge(sg("rstd_ready"), n + 1)

            def pre_norm(n, t, gain_row=None):
                mean_square(n, t)
                if gain_row is None:
                    dve.tensor_scalar(nat[:, t, :], x[:, t, :], rstd[:, t:t + 1], None, MUL).then_inc(sg("nat_ready"), 1)
                else:
                    dve.scalar_tensor_tensor(nat[:, t, :], x[:, t, :], rstd[:, t:t + 1], gain_row, MUL, MUL).then_inc(sg("nat_ready"), 1)

            def norms(n, bank, gain_row=None):
                for t in range(NT):
                    mean_square(NT + 2 * NT * n + 2 * t, t)
                    dve.wait_ge(sg("post_gain_in"), 16 * (n + 1))
                    link(dve.scalar_tensor_tensor(nat[:, t, :], ps[:, bank + 2 * t:bank + 2 * t + 2, :].rearrange("p a b -> p (a b)"),
                                                  rstd[:, t:t + 1], post_gain[:, :], MUL, MUL))
                    dve.tensor_tensor(x[:, t, :], x[:, t, :], nat[:, t, :], ADD).then_inc(sg("x_done"), 1)
                    dve.wait_ge(sg("x_done"), NT * n + t + 1)
                    pre_norm(NT + 2 * NT * n + 2 * t + 1, t, gain_row)

            def hT_half(n, gain):
                for b in (1, 3):
                    dve.wait_ge(sg("tr_ready"), 4 * n + b + 1)
                    for k in (2 * b, 2 * b + 1):
                        ins = dve.tensor_scalar(hT[:, k, :], ps[:, TR_BANKS[n][b], (k % 2) * SEQ:(k % 2 + 1) * SEQ],
                                                1.0 if gain is None else gcol[:, gain * 8 + k:gain * 8 + k + 1], None, MUL)
                    ins.then_inc(sg("hT_ready"), 1)

            dve.wait_ge(sg("lam_in"), 48)
            dve.tensor_copy(raw_l[0:DG, 2, :].rearrange("g (a p) -> g a p", a=2),
                            raw_s[0:DG, :].unsqueeze(2).to_broadcast([DG, 2, ST])).then_inc(sg("lstep_spread"), 1)
            for t in range(NT):
                pre_norm(t, t)
            dve.wait_ge(sg("gain_in"), 32)
            dve.tensor_copy(raw_dx[0:GROUPS, :, :], raw_d[0:GROUPS, :].unsqueeze(1).to_broadcast([GROUPS, CH, GC])).then_inc(sg("d_spread"), 1)
            lr, li, st, ea, mag, rs, rc_, sn, cs = (tmp(i) for i in range(9))
            dve.wait_ge(sg("lam_tr"), 1)
            dve.tensor_copy(lr, ps[:, 4, 0:64])
            dve.tensor_copy(li, ps[:, 4, 64:128]).then_inc(sg("lam_copied"), 1)
            dve.wait_ge(sg("step_ready"), 1)
            tt(ea, lr, st, MUL)
            tt(rs, li, st, MUL)
            n_, t_ = tmp(9), tmp(10)
            MAGIC = 12582912.0
            link(dve.tensor_scalar(n_, rs, 0.15915494309189535, MAGIC, MUL, ADD))
            link(dve.tensor_scalar(n_, n_, -MAGIC, None, ADD))
            for c in (6.28125, 1.9350051879882812e-3, 3.019915981956753e-7):
                link(dve.scalar_tensor_tensor(rs, n_, -c, rs, MUL, ADD))
            PI = 3.1415925
            link(dve.tensor_scalar(rs, rs, PI, -PI, ALU.min, ALU.max))
            link(dve.tensor_scalar(t_, rs, -1.0, None, MUL))
            tt(t_, t_, rs, ALU.max)
            dve.tensor_scalar(rc_, t_, -1.0, 1.5707963267948966, MUL, ADD).then_inc(sg("ang_ready"), 1)
            dve.wait_ge(sg("mag_ready"), 3)
            dve.memset(pw[:, 0, 0, :], 1.0)
            dve.memset(pw[:, 1, 0, :], 0.0)
            tt(pw[:, 0, 1, :], mag, cs, MUL)
            tt(pw[:, 1, 1, :], mag, sn, MUL)

            def cmul(o_re, o_im, a, b, shape, t1, t2):
                tt(t1, a[0], b[0], MUL)
                tt(t2, a[1], b[1], MUL)
                link(dve.tensor_tensor(o_re, t1, t2, SUB))
                tt(t1, a[0], b[1], MUL)
                tt(t2, a[1], b[0], MUL)
                link(dve.tensor_tensor(o_im, t1, t2, ADD))

            q1, q2 = tmp(11), tmp(12)
            cmul(pw[:, 0, 2, :], pw[:, 1, 2, :], (pw[:, 0, 1, :],) + (pw[:, 1, 1, :],), (pw[:, 0, 1, :], pw[:, 1, 1, :]), None, q1, q2)
            w1 = mtmp[0][:, 0:2 * DG].rearrange("p (k g) -> p k g", k=2)
            w2 = mtmp[1][:, 0:2 * DG].rearrange("p (k g) -> p k g", k=2)
            b2 = [pw[:, r, 2:3, :].to_broadcast([P, 2, DG]) for r in range(2)]
            cmul(pw[:, 0, 3:5, :], pw[:, 1, 3:5, :], (pw[:, 0, 1:3, :], pw[:, 1, 1:3, :]), b2, None, w1, w2)
            w1 = mtmp[0][:, 0:4 * DG].rearrange("p (k g) -> p k g", k=4)
            w2 = mtmp[1][:, 0:4 * DG].rearrange("p (k g) -> p k g", k=4)
            b4 = [pw[:, r, 4:5, :].to_broadcast([P, 4, DG]) for r in range(2)]
            cmul(pw[:, 0, 5:9, :], pw[:, 1, 5:9, :], (pw[:, 0, 1:5, :], pw[:, 1, 1:5, :]), b4, None, w1, w2)
            dve.memset(tmp(26), 0.0).then_inc(sg("pw_ready"), 1)
            den, nr, qr, qi = tmp(13), tmp(14), tmp(15), tmp(16)
            tt(q1, lr, lr, MUL)
            tt(q2, li, li, MUL)
            tt(den, q1, q2, ADD)
            link(dve.reciprocal(den, den))
            link(dve.tensor_scalar(nr, pw[:, 0, 1, :], -1.0, None, ADD))
            tt(q1, nr, lr, MUL)
            tt(q2, pw[:, 1, 1, :], li, MUL)
            tt(q1, q1, q2, ADD)
            tt(qr, q1, den, MUL)
            tt(q1, pw[:, 1, 1, :], lr, MUL)
            tt(q2, nr, li, MUL)
            tt(q1, q1, q2, SUB)
            tt(qi, q1, den, MUL)
            dve.wait_ge(sg("bc_out"), 4)
            m1 = at(REZ + 4096, DG, GC)
            m2 = at(REZ + 4096 + 1024, DG, GC)
            qb = [v.unsqueeze(2).to_broadcast([P, DG, GC]) for v in (qr, qi)]
            tt(m1, bP[:, 0], qb[0], MUL)
            tt(m2, bP[:, 1], qb[1], MUL)
            tt(bbar[:, 0, 0:DG, :], m1, m2, SUB)
            tt(m1, bP[:, 1], qb[0], MUL)
            tt(m2, bP[:, 0], qb[1], MUL)
            dve.wait_ge(sg("bbar_pad"), 1)
            dve.wait_ge(sg("pd_ready"), 1)
            dve.tensor_tensor(bbar[:, 1, 0:DG, :], m1, m2, ADD).then_inc(sg("bbar_ready"), 1)
            dve.wait_ge(sg("gcol_ready"), 1)
            hT_half(0, 0)
            dve.wait_ge(sg("bbar_ready"), 1)
            e1 = (tmp(17), tmp(18))
            cur = (cs, sn)
            for i in range(3):
                nxt = e1 if i % 2 == 0 else (tmp(19), tmp(20))
                cmul(nxt[0], nxt[1], cur, cur, None, q1, q2)
                tt(q1, nxt[0], nxt[0], MUL)
                tt(q2, nxt[1], nxt[1], MUL)
                tt(q1, q1, q2, ADD)
                link(dve.tensor_scalar(q1, q1, -0.5, 1.5, MUL, ADD))
                tt(nxt[0], nxt[0], q1, MUL)
                tt(nxt[1], nxt[1], q1, MUL)
                cur = nxt
            dve.wait_ge(sg("d_tr"), 1)
            link(dve.tensor_copy(dcol[:, :], ps[:, 7, 64:128]))
            link(dve.memset(ec[:, 0, :, 0:1], 1.0))
            link(dve.memset(ec[:, 1, :, 0:1], 0.0))
            n = 1
            while n < NC:
                bb = [v.unsqueeze(2).to_broadcast([P, DG, n]) for v in cur]
                t1 = at(REZ + 4096, DG, n)
                t2 = at(REZ + 4096 + 1024, DG, n)
                cmul(ec[:, 0, :, n:2 * n], ec[:, 1, :, n:2 * n], (ec[:, 0, :, 0:n], ec[:, 1, :, 0:n]), bb, None, t1, t2)
                if 2 * n < NC:
                    nxt = (tmp(21), tmp(22)) if cur[0] is not None and n in (1, 4, 16) else (tmp(23), tmp(24))
                    cmul(nxt[0], nxt[1], cur, cur, None, q1, q2)
                    cur = nxt
                n *= 2
            for t in range(NT):
                dve.wait_ge(sg("u_mm"), t + 1)
                dve.tensor_copy(nat[:, t, 512:1024], ps[:, 2 * t + 1, :]).then_inc(sg("u_dve"), 1)

            def build_wt(b):
                d = b // (NB // 2)
                s = slice(SB * b, SB * (b + 1))
                pt = pd[:, :, 1:NPOW, s] if d == 0 else pw[:, :, 0:CH, s]
                v4 = [m[:, 0:SB * P].rearrange("p (g s i) -> p g s i", g=SB, s=CH) for m in mtmp]
                for i in range(2):
                    ins = dve.tensor_tensor(v4[i], bbar[:, i, s, :].unsqueeze(2).to_broadcast([P, SB, CH, GC]),
                                            pt[:, i].rearrange("p s g -> p g s").unsqueeze(3).to_broadcast([P, SB, CH, GC]), MUL)
                link(ins)
                if b >= 2:
                    dve.wait_ge(sg("w_tr"), 2 * (b - 1))
                link(dve.tensor_tensor(wt[b % 2][:, 0].rearrange("p g x -> p (g x)"), mtmp[0][:, 0:SB * P], mtmp[1][:, 0:SB * P], SUB))
                dve.wait_ge(sg("wt_pool"), 2 * (b + 1))
                dve.tensor_tensor(wt[b % 2][:, 1].rearrange("p g x -> p (g x)"), ptmp[b % 2][0][:, 0:SB * P], ptmp[b % 2][1][:, 0:SB * P], ADD).then_inc(sg("wt_ready"), 1)

            build_wt(0)
            build_wt(1)
            dve.wait_ge(sg("u_tok_in"), 16 * NT * CH)
            GA = 28
            for s in range(CH):
                ins = dve.tensor_copy(u_grp[0:NC, GA:, s, :], u_tok[0:NC, s, GA * GC:].rearrange("p (g i) -> p g i", i=GC))
            ins.then_inc(sg("u_grp_ready"), 1)
            for b in range(2, NB):
                build_wt(b)
            m2_, m4_, m8_ = tmp(21), tmp(22), tmp(25)
            tt(m2_, mag, mag, MUL)
            tt(m4_, m2_, m2_, MUL)
            tt(m8_, m4_, m4_, MUL)

            def chunk_scan(d, step):
                g = slice(GP * d, GP * (d + 1))
                z0, z1, t8 = zz[:, 0, g], zz[:, 1, g], tmp8[:, :]
                s0, s1, c0, c1 = S_[:, 0, g], S_[:, 1, g], ec[:, 0, g], ec[:, 1, g]
                if step == 0:
                    dve.wait_ge(sg("s_out"), NB // 2 * (d + 1))
                    dve.tensor_tensor(z0, s0, c0, MUL)
                    tt(t8, s1, c1, MUL)
                    tt(z0, z0, t8, ADD)
                elif step == 1:
                    dve.tensor_tensor(z1, s1, c0, MUL)
                    tt(t8, s0, c1, MUL)
                    tt(z1, z1, t8, SUB)
                elif step == 2:
                    link(dve.tensor_copy(r8t[:, :, :], m8_[:, g].unsqueeze(2).to_broadcast([P, GP, NC])))
                    link(dve.memset(r8t[:, :, 0:1], 0.0))
                elif step < 5:
                    r = step - 3
                    link(dve.tensor_tensor_scan(S_[:, r, g, :].rearrange("p g c -> p (g c)"), r8t[:, :, :].rearrange("p g c -> p (g c)"),
                                                zz[:, r, g, :].rearrange("p g c -> p (g c)"), 0.0, MUL, ADD))
                elif step == 5:
                    dve.tensor_tensor(z0, s0, c0, MUL)
                    tt(t8, s1, c1, MUL)
                elif step == 6:
                    dve.tensor_tensor(z0, z0, t8, SUB).then_inc(sg("x_nat"), 1)
                    dve.wait_ge(sg("x_nat"), 2 * d + 1)
                    dve.tensor_tensor(z1, s1, c0, MUL)
                    tt(t8, s0, c1, MUL)
                else:
                    dve.tensor_tensor(z1, z1, t8, ADD).then_inc(sg("x_nat"), 1)

            for step_ in range(8):
                chunk_scan(0, step_)
            def k_zero(hf):
                dve.wait_ge(sg("k_out"), NB // 2 + 4 * (hf + 1))
                v = kall[:, :, 4 * hf:4 * hf + 4, CH - 1, :]
                dve.tensor_tensor(v, v, kzero[:, :, 4 * hf:4 * hf + 4, :], ADD).then_inc(sg("k_final"), 1)

            for b in range(NB):
                d = b // (NB // 2)
                s = slice(SB * b, SB * (b + 1))
                pt = pw[:, :, :, s] if d == 0 else pd[:, :, :, s]
                v4 = [m.rearrange("p (g s i) -> p g s i", g=SB, s=NPOW) for m in mtmp]
                for i in range(2):
                    ins = dve.tensor_tensor(v4[i], cP[:, i, s, :].unsqueeze(2).to_broadcast([P, SB, NPOW, GC]),
                                            pt[:, i].rearrange("p s g -> p g s").unsqueeze(3).to_broadcast([P, SB, NPOW, GC]), MUL)
                link(ins)
                if b >= 2:
                    dve.wait_ge(sg("y_state"), b - 1)
                v = vv[b % 2]
                link(dve.tensor_tensor(v[:, 0].rearrange("p g s i -> p (g s i)"), mtmp[0], mtmp[1], SUB))
                dve.wait_ge(sg("v_pool"), 2 * (b + 1))
                dve.scalar_tensor_tensor(v[:, 1].rearrange("p g s i -> p (g s i)"), ptmp[b % 2][0], -1.0, ptmp[b % 2][1], MUL, SUB).then_inc(sg("v_ready"), 1)
                if b < 8:
                    chunk_scan(1, b)
                if b == 13:
                    k_zero(0)
            k_zero(1)
            dve.wait_ge(sg("y_state"), NB)
            tt(ud[:, :, :], uc[:, :, :], dcol[:, :].unsqueeze(2).to_broadcast([P, GROUPS, NC]), MUL)
            for b in range(5):
                if b < 4:
                    dve.wait_ge(sg("y_mm"), b + 1)
                    dve.tensor_tensor(yg[:, 16 * b:16 * b + 16, :].rearrange("p g c -> p (g c)"), ps[:, b, :],
                                      ud[:, 16 * b:16 * b + 16, :].rearrange("p g c -> p (g c)"), ADD).then_inc(sg("y_sum"), 1)
                if b >= 1:
                    for r in range(4 * (b - 1) + 1, 4 * b, 2):
                        dve.wait_ge(sg("g_tr"), r + 1)
                        dve.tensor_copy(g_tok[0:NC, :, 64 * r:64 * r + 64].rearrange("c t (g o) -> c g t o", o=GC),
                                        ps[0:NC, 4 + r % 4, :].rearrange("c (g t o) -> c g t o", g=4, t=CH)).then_inc(sg("g_tok_dve"), 1)
            for b in (1, 3):
                dve.wait_ge(sg("gT_tr"), b + 1)
                dve.tensor_copy(gT[:, 2 * b:2 * b + 2, :].rearrange("p k (c t) -> p k t c", t=CH),
                                ps[:, b, :].rearrange("p (k t c) -> p k t c", k=2, t=CH)).then_inc(sg("gT_ready"), 1)
            for m in range(KD):
                dve.wait_ge(sg("sig_ready"), m + 1)
                dve.tensor_tensor(mT[:, m, :], sig[:, m, :], gT[:, m, :], MUL).then_inc(sg("m_ready"), 1)
            norms(0, 0)
            hT_half(1, 2)
            for c in range(2 * FF_STEPS):
                dve.wait_ge(sg("sil_ready"), c + 1)
                if c >= 2:
                    dve.wait_ge(sg("down_done"), c - 1)
                dve.tensor_tensor(hid[c % 2], sil[c % 2], ps[:, c % 2, SEQ:2 * SEQ], MUL).then_inc(sg("hid_ready"), 1)
            norms(1, 2)
            hT_half(2, 4)
            dve.wait_ge(sg("proj_done"), QKV // IW)
            dve.wait_ge(sg("x_stored"), 16)
            dve.tensor_copy(qkv[:, 1, :].rearrange("p (b n) -> p b n", b=3), ps[:, 3:6, :]).then_inc(sg("qkv_dve"), 1)
            dve.wait_ge(sg("rope_in"), 64)
            for w in range(2):
                for i, (cs_, par) in enumerate(((0, 0), (1, 1), (1, 0), (0, 1))):
                    ins = dve.tensor_tensor(rope_t[:, w, i], rope_raw[:, cs_],
                                            qk_gain[:, w, par::2].unsqueeze(1).to_broadcast([P, NT, HD // 2]), MUL)
            link(ins)
            for t in range(NT):
                dve.wait_ge(sg("head_sq"), t + 1)
                dve.tensor_reduce(hms[:, t * QK:(t + 1) * QK], nat_flat[:, 0:QK * HD].rearrange("p (h d) -> p h d", d=HD), AX.X, ADD).then_inc(sg("head_sum"), 1)
            dve.wait_ge(sg("head_sum"), NT)
            dve.tensor_scalar(hms[:, 0:NT * QK], hms[:, 0:NT * QK], 1.0 / HD, EPS, MUL, ADD).then_inc(sg("head_ms"), 1)
            dve.wait_ge(sg("head_rstd"), 1)
            dve.wait_ge(sg("qkv_act"), 1)
            dve.wait_ge(sg("qkv_dve"), 1)
            def finish_heads(q):
                t, h0 = divmod(q, 2)
                dve.wait_ge(sg("probs_ready"), 8 * (q + 1))
                dve.wait_ge(sg("pv_done"), 4 * (q + 1))
                link(dve.reciprocal(prcp[:, 8 * q:8 * q + 8], psum_[:, 8 * q:8 * q + 8]))
                dve.tensor_tensor(o_nat[:, t, h0 * 512:(h0 + 1) * 512].rearrange("p (h d) -> p h d", d=HD),
                                  ps[:, 6 + q % 2, :].rearrange("p (h d) -> p h d", d=HD),
                                  prcp[:, 8 * q:8 * q + 8].unsqueeze(2).to_broadcast([P, 8, HD]), MUL).then_inc(sg("o_ready"), 1)

            for t in range(NT):
                v = qkv[:, t, 0:QK * HD].rearrange("p (h d) -> p h d", d=HD)
                tt(v, v, hrs[:, t * QK:(t + 1) * QK].unsqueeze(2).to_broadcast([P, QK, HD]), MUL)
                for w in range(2):
                    hs = slice(0, NH) if w == 0 else slice(NH, QK)
                    nh = NH if w == 0 else NKV
                    for i in range(4):
                        ins = dve.tensor_tensor(rope_m[i][:, 0:nh], v[:, hs, (i % 2)::2],
                                                rope_t[:, w, i, t].unsqueeze(1).to_broadcast([P, nh, HD // 2]), MUL)
                    link(ins)
                    if w == 0:
                        dve.tensor_tensor(v[:, hs, 0::2], rope_m[0], rope_m[1], SUB)
                        link(dve.tensor_tensor(v[:, hs, 1::2], rope_m[2], rope_m[3], ADD))
                    else:
                        for c in range(2):
                            dve.tensor_tensor(k_dup[:, t, :, c, 0::2], rope_m[0][:, 0:nh], rope_m[1][:, 0:nh], SUB)
                            ins = dve.tensor_tensor(k_dup[:, t, :, c, 1::2], rope_m[2][:, 0:nh], rope_m[3][:, 0:nh], ADD)
                        ins.then_inc(sg("rope_done"), 1)
                        dve.wait_ge(sg("rope_done"), t + 1)
            for b in (1, 3):
                dve.wait_ge(sg("q_tr"), b + 1)
                dve.tensor_copy(qT[:, 2 * b:2 * b + 2, :], ps[:, b, :].rearrange("p (k n) -> p k n", k=2)).then_inc(sg("qT_ready"), 1)
            dve.wait_ge(sg("k_tr"), 2)
            dve.tensor_copy(kT[:, 2:4, :], ps[:, 5, :].rearrange("p (k n) -> p k n", k=2)).then_inc(sg("qT_ready"), 1)

            def score_max(u):
                dve.wait_ge(sg("scores_ready"), u + 1)
                link(dve.tensor_reduce(nmax[:, 2 * u:2 * u + 2], ps[:, 2 * (u % 2):2 * (u % 2) + 2, 0:SEQ], AX.X, ALU.max))
                dve.tensor_scalar(nmax[:, 2 * u:2 * u + 2], nmax[:, 2 * u:2 * u + 2], -HD ** -0.5, None, MUL).then_inc(sg("smax_ready"), 1)

            score_max(0)
            for u in range(UNITS):
                if u + 1 < UNITS:
                    score_max(u + 1)
                dve.wait_ge(sg("p_tr"), u + 1)
                if u >= 2:
                    dve.wait_ge(sg("pv_done"), u - 1)
                dve.tensor_copy(probT[u % 2], ps[:, 4 + u % 2, :].rearrange("p (a b n) -> p a b n", a=2, b=NT)).then_inc(sg("probT_ready"), 1)
                if u % 4 == 0 and u >= 4:
                    finish_heads(u // 4 - 1)
            finish_heads(UNITS // 4 - 1)
            for b in (1, 3):
                dve.wait_ge(sg("oT_tr"), b + 1)
                dve.tensor_copy(hT[:, 2 * b:2 * b + 2, :], ps[:, b, :].rearrange("p (k n) -> p k n", k=2)).then_inc(sg("hT_ready"), 1)
            dve.wait_ge(sg("x_back"), 16)
            dve.wait_ge(sg("moe_gain_in"), 16)
            norms(2, 4, moe_gain)
            hT_half(3, None)
            dve.wait_ge(sg("route_consts"), 1)
            dve.wait_ge(sg("logits_mm"), 1)
            link(dve.tensor_copy(logit[:, :, :], ps[:, 4, 0:NT * EXP].rearrange("p (t e) -> p t e", t=NT)))
            link(dve.tensor_reduce(lmax, logit, AX.X, ALU.max))
            dve.tensor_tensor(lshift, logit, lmax.unsqueeze(2).to_broadcast([P, NT, EXP]), SUB).then_inc(sg("logits_shifted"), 1)
            lj = logit.unsqueeze(2).to_broadcast([P, NT, EXP, EXP])
            li_ = logit.unsqueeze(3).to_broadcast([P, NT, EXP, EXP])
            dve.tensor_tensor(gt_, lj, li_, ALU.is_gt)
            tt(eq_, lj, li_, ALU.is_equal)
            tt(eq_, eq_, lower_e.unsqueeze(1).to_broadcast([P, NT, EXP, EXP]), MUL)
            tt(gt_, gt_, eq_, ADD)
            link(dve.tensor_reduce(beats, gt_, AX.X, ADD))
            dve.tensor_scalar(chosen[:, :, 0:EXP], beats, 1.5, None, ALU.is_lt).then_inc(sg("chosen_ready"), 1)
            dve.wait_ge(sg("chosen_ready"), 1)
            dve.wait_ge(sg("logits_exp"), 1)
            tt(wexp, wexp, chosen[:, :, 0:EXP], MUL)
            link(dve.tensor_reduce(wsum, wexp, AX.X, ADD))
            link(dve.reciprocal(wsum, wsum))
            tt(gate[:, :, 0:EXP], wexp, wsum.unsqueeze(2).to_broadcast([P, NT, EXP]), MUL)
            dve.wait_ge(sg("rank_mm"), 1)
            link(dve.tensor_copy(rank[:, :, 0:EXP], ps[:, 5, 0:NT * EXP].rearrange("p (t e) -> p t e", t=NT)))
            dve.tensor_copy(cnt_i[0:1, :], ps[0:1, 6, 0:EXP]).then_inc(sg("counts_ready"), 1)

            def selection(dst, weight, e, sem):
                for t in range(NT):
                    dve.tensor_scalar(dst[:, t, :], iota[:, :], rank[:, t, bass.ds(e, 1)], weight[:, t, bass.ds(e, 1)],
                                      ALU.is_equal, MUL).then_inc(sg(sem), 1)

            selection(sel, chosen, 0, "sel_ready")
            dve.wait_ge(sg("counts_ready"), 1)

            def gathered(e):
                for b in (1, 3):
                    dve.wait_ge(sg("gather_mm"), 4 * e + b + 1)
                    dve.tensor_copy(xg[:, 2 * b:2 * b + 2, :], ps[:, b, :].rearrange("p (k n) -> p k n", k=2)).then_inc(sg("xg_ready"), 1)

            def add_scattered(e):
                for q in range(4):
                    dve.wait_ge(sg("scatter_mm"), 4 * e + q + 1)
                    if q == 0:
                        dve.wait_ge(sg("acc_done"), 4 * e + 1)
                    av = acc[:, :, q * SEQ:(q + 1) * SEQ]
                    dve.tensor_tensor(av, av, ps[:, 4 + q, :].rearrange("p (t n) -> p t n", t=NT), ADD).then_inc(sg("acc_done"), 1)

            def expert_narrow(e, T):
                M = P // T
                gathered(e)
                for s in range(EX_STEPS):
                    dve.wait_ge(sg("moe_sil"), CHUNKS * e + 2 * s + 2)
                    if s >= 2:
                        dve.wait_ge(sg("moe_down"), CHUNKS * e + 2 * (s - 1))
                    dve.tensor_tensor(m_hid[s % 2], m_sil[s % 2], ps[:, s % 2, SEQ:2 * SEQ], MUL).then_inc(sg("moe_hid"), 2)
                    if s == 0:
                        dve.wait_ge(sg("acc_done"), 4 * e + 1)
                        for t in range(NT):
                            dve.tensor_scalar(sel_g[:, t, 0:P].rearrange("p (r m) -> p r m", r=T),
                                              iota[:, 0:M].unsqueeze(1).to_broadcast([P, T, M]),
                                              rank[:, t, bass.ds(e, 1)], gate[:, t, bass.ds(e, 1)], ALU.is_equal, MUL).then_inc(sg("selg_ready"), 1)
                        selection(sel, chosen, e + 1, "sel_ready")
                dve.wait_ge(sg("moe_down"), CHUNKS * (e + 1))
                dve.tensor_copy(y_lo[:, 512:1024], ps[:, 3, :]).then_inc(sg("y_ready"), 2)
                add_scattered(e)

            def expert_wide(e):
                gathered(e)
                for c in range(CHUNKS):
                    dve.wait_ge(sg("moe_sil"), CHUNKS * e + c + 1)
                    if c >= 2:
                        dve.wait_ge(sg("moe_down"), CHUNKS * e + c - 1)
                    dve.tensor_tensor(m_hid[c % 2], m_sil[c % 2], ps[:, c % 2, SEQ:2 * SEQ], MUL).then_inc(sg("moe_hid"), 1)
                    if c == SEL_AT:
                        dve.wait_ge(sg("acc_done"), 4 * e + 1)
                        selection(sel_g, gate, e, "selg_ready")
                        selection(sel, chosen, e + 1, "sel_ready")
                dve.wait_ge(sg("moe_down"), CHUNKS * (e + 1))
                for b in (1, 3):
                    dve.tensor_copy(yT[:, 2 * b:2 * b + 2, :], ps[:, 2 + b, :].rearrange("p (k n) -> p k n", k=2)).then_inc(sg("yT_ready"), 1)
                dve.wait_ge(sg("y_tr"), 2 * e + 1)
                dve.tensor_copy(y_lo[:, 512:1024], ps[:, 7, :]).then_inc(sg("y_ready"), 1)
                dve.wait_ge(sg("y_tr"), 2 * e + 2)
                dve.tensor_copy(y_hi[:, 512:1024], ps[:, 1, :]).then_inc(sg("y_ready"), 1)
                add_scattered(e)

            with dve.Fori(0, EXP) as e:
                n = dve.value_load(cnt_i[0:1, bass.ds(e, 1)], min_val=0, max_val=SEQ)
                with dve.If(n > P // 2):
                    with dve.If(n > P):
                        expert_wide(e)
                    with dve.Else():
                        expert_narrow(e, 1)
                with dve.Else():
                    with dve.If(n > P // 4):
                        expert_narrow(e, 2)
                    with dve.Else():
                        expert_narrow(e, 4)
            dve.wait_ge(sg("last_gain_in"), 16)
            dve.wait_ge(sg("x_back"), 32)
            dve.wait_ge(sg("acc_done"), 4 * EXP + 1)
            for t in range(NT):
                mean_square(NT + 2 * NT * 3 + t, t)
                link(dve.scalar_tensor_tensor(acc[:, t, :], acc[:, t, :], rstd[:, t:t + 1], last_gain[:, :], MUL, MUL))
                dve.tensor_tensor(acc[:, t, :], acc[:, t, :], nat[:, t, :], ADD).then_inc(sg("y_final"), 1)

        @block.tensor
        def _(pe):
            def transposed_nat(n):
                for t in range(NT):
                    pe.wait_ge(sg("nat_ready"), NT * n + t + 1)
                    for k in range(KD):
                        m = pe.transpose(ps[:, TR_BANKS[n][k // 2], (k % 2) * SEQ + t * P:(k % 2) * SEQ + (t + 1) * P],
                                         nat[:, t, k * P:(k + 1) * P], ident[:, :])
                        if t == NT - 1 and k % 2 == 1:
                            m.then_inc(sg("tr_ready"), 1)

            id64 = ident[0:64, 0:64]
            pe.wait_ge(sg("ident_ready"), 1)
            pe.wait_ge(sg("lam_in"), 48)
            pe.wait_ge(sg("lstep_spread"), 1)
            for i in range(3):
                m = pe.transpose(ps[:, 4, 64 * i:64 * i + 64], raw_l[0:DG, i, :], id64)
            m.then_inc(sg("lam_tr"), 1)
            pe.wait_ge(sg("b_in"), 32)
            pe.wait_ge(sg("c_in"), 64)
            for r in range(4):
                if r >= 1:
                    pe.wait_ge(sg("bc_out"), 2 * r)
                for h in range(2):
                    for s in range(8):
                        src = raw_b[0:DG, r, :, 8 * h + s] if r < 2 else raw_c[0:DG, r - 2, 8 * h + s, :]
                        m = pe.transpose(ps[:, 5 + h, 64 * s:64 * s + 64], src, id64)
                    m.then_inc(sg("bc_tr"), 1)
            pe.wait_ge(sg("gain_in"), 32)
            pe.transpose(ps[:, 7, 0:64], raw_g[0:64, :], id64).then_inc(sg("gain_tr"), 1)
            pe.wait_ge(sg("d_spread"), 1)
            pe.wait_ge(sg("gcol_ready"), 1)
            pe.transpose(ps[:, 7, 64:128], raw_dx[0:GROUPS, :, :].rearrange("g t o -> g (t o)"), id64).then_inc(sg("d_tr"), 1)
            transposed_nat(0)
            pe.wait_ge(sg("hT_ready"), 4)
            for t in range(NT):
                for i in range(4):
                    if t == 0:
                        pe.wait_ge(sg(f"mix_w{i}"), 16)
                    for k in range(KD):
                        m = pe.matmul(ps[:, 2 * t + i // 2, (i % 2) * IW:(i % 2 + 1) * IW], hT[:, k, t * P:(t + 1) * P],
                                      w_in[:, i, k, :], start=k == 0, stop=k == KD - 1)
                m.then_inc(sg("u_mm"), 1)
            pe.wait_ge(sg("u_grp_ready"), 2)
            pe.wait_ge(sg("u_act"), 2)
            pe.wait_ge(sg("u_dve"), 2)
            for b in range(4):
                for g in range(16 * b, 16 * b + 16):
                    m = pe.transpose(ps[:, b, (g % 16) * NC:(g % 16 + 1) * NC],
                                     u_grp[0:NC, g, :, :].rearrange("c s i -> c (s i)"), ident[0:NC, 0:NC])
                m.then_inc(sg("uc_tr"), 1)

            def w_transposes(b):
                pe.wait_ge(sg("wt_ready"), b + 1)
                if b >= 2:
                    pe.wait_ge(sg("w_out_act"), 2 * (b - 1))
                if b == 0:
                    pe.wait_ge(sg("uc_ready"), 4)
                for g in range(SB):
                    for r in range(2):
                        n = 2 * g + r
                        m = pe.transpose(ps[:, 2 * (b % 2) + n // 4, (n % 4) * P:(n % 4 + 1) * P], wt[b % 2][:, r, g, :], ident[:, :])
                    if g % 2 == 1:
                        m.then_inc(sg("w_tr"), 1)

            def s_matmuls(b):
                pe.wait_ge(sg("w_out_act"), 2 * (b + 1))
                if b >= 2:
                    pe.wait_ge(sg("s_out"), b - 1)
                d = b // (NB // 2)
                for g in range(SB):
                    gp = (SB * b + g) % GP
                    for a in range(2):
                        rhs = uc[:, 2 * gp + a, :] if d == 0 else uc[:, 2 * gp + a, ::-1]
                        for r in range(2):
                            m = pe.matmul(ps[64 * a:64 * a + 64, 4 + b % 2, r * P + g * NC:r * P + (g + 1) * NC],
                                          wm[b % 2][:, g, r, 64 * a:64 * a + 64], rhs, start=True, stop=True)
                m.then_inc(sg("s_mm"), 1)

            for b in range(NB):
                w_transposes(b)
                if b >= 1:
                    s_matmuls(b - 1)
            s_matmuls(NB - 1)
            pe.wait_ge(sg("s_out"), NB)
            for b in range(NB):
                d = b // (NB // 2)
                pe.wait_ge(sg("v_ready"), b + 1)
                v = vv[b % 2]
                if b >= 2:
                    pe.wait_ge(sg("k_out"), b - 1)
                k0 = 0 if d == 0 else 1
                for r in range(2):
                    for g in range(SB):
                        dg = SB * b + g
                        for a in range(2):
                            m = pe.matmul(ps[32 * g:32 * g + 32, 4 + 2 * (b % 2) + a, 0:P],
                                          bbar[64 * a:64 * a + 64, r, dg:dg + 2, :].rearrange("p g i -> p (g i)"),
                                          v[64 * a:64 * a + 64, r, g, k0:k0 + CH, :].rearrange("p t o -> p (t o)"),
                                          start=r == 0, stop=r == 1)
                m.then_inc(sg("k_mm"), 1)
                y0 = 1 if d == 0 else 0
                pe.wait_ge(sg("x_ready"), 4 * (d + 1))
                for g in range(SB):
                    dg = SB * b + g
                    gp = dg % GP
                    for r in range(2):
                        rhs = xbd[:, r, dg, :, :] if d == 0 else xbd[:, r, dg, :, ::-1]
                        m = pe.matmul(ps[:, gp // 8, (gp % 8) * 64:(gp % 8 + 1) * 64],
                                      v[:, r, g, y0:y0 + CH, :].rearrange("p t o -> p (t o)"), rhs,
                                      start=(d == 0 and gp % 8 == 0 and r == 0), stop=False, skip_group_check=True)
                m.then_inc(sg("y_state"), 1)
            for b in range(5):
                if b < 4:
                    if b % 2 == 0:
                        pe.wait_ge(sg(f"toe_in{b // 2}"), 16 * CH)
                    for g in range(16 * b, 16 * b + 16):
                        m = pe.matmul(ps[:, b, (g % 16) * NC:(g % 16 + 1) * NC], toe[g // 32][:, g % 32, :], uc[:, g, :],
                                      start=False, stop=True, skip_group_check=True)
                    m.then_inc(sg("y_mm"), 1)
                if b >= 1:
                    pe.wait_ge(sg("gelu"), b)
                    for r in range(4 * (b - 1), 4 * b):
                        if r >= 4:
                            pe.wait_ge(sg("g_tok_act" if r % 2 == 0 else "g_tok_dve"), (r - 4) // 2 + 1)
                        for g in range(4 * r, 4 * r + 4):
                            m = pe.transpose(ps[0:NC, 4 + r % 4, (g % 4) * P:(g % 4 + 1) * P], yg[:, g, :], ident[:, :])
                        m.then_inc(sg("g_tr"), 1)
            pe.wait_ge(sg("g_tok_act"), 8)
            pe.wait_ge(sg("g_tok_dve"), 8)
            for b in range(4):
                for k in (2 * b, 2 * b + 1):
                    for t in range(CH):
                        m = pe.transpose(ps[:, b, (k % 2) * SEQ + t * NC:(k % 2) * SEQ + (t + 1) * NC],
                                         g_tok[0:NC, t, k * P:(k + 1) * P], ident[0:NC, 0:NC])
                m.then_inc(sg("gT_tr"), 1)
            pe.wait_ge(sg("gT_ready"), 4)
            for m_ in range(KD):
                if m_ % 2 == 0:
                    pe.wait_ge(*((sg(f"mix_w{m_ // 2}"), 32) if m_ < 6 else (sg("glu_w3"), 16)))
                if m_ >= 4:
                    pe.wait_ge(sg("m_ready"), m_ - 3)
                for k in range(KD):
                    m = pe.matmul(ps[:, 4 + m_ % 4, 0:SEQ], w_glu[:, m_ // 2, k, (m_ % 2) * P:(m_ % 2 + 1) * P],
                                  gT[:, k, :], start=k == 0, stop=k == KD - 1)
                m.then_inc(sg("glu_mm"), 1)
            pe.wait_ge(sg("m_ready"), 8)
            for t in range(NT):
                for i in range(4):
                    if t == 0:
                        pe.wait_ge(sg(f"mix_w{i}"), 48 if i < 3 else 32)
                    for k in range(KD):
                        m = pe.matmul(ps[:, 2 * t + i // 2, (i % 2) * IW:(i % 2 + 1) * IW], mT[:, k, t * P:(t + 1) * P],
                                      w_out0[:, i, k, :], start=k == 0, stop=k == KD - 1)
                m.then_inc(sg("mix_done"), 1)
            transposed_nat(1)
            pe.wait_ge(sg("hT_ready"), 8)

            def ffn_down(c):
                n = 3 * (c // 2) + 2
                pe.wait_ge(*item_full(n))
                pe.wait_ge(sg("hid_ready"), c + 1)
                for t in range(NT):
                    for h in range(2):
                        m = pe.matmul(ps[:, 2 + 2 * t + h, :], hid[c % 2][:, t * P:(t + 1) * P],
                                      slot_down(n)[:, c % 2, h * 512:(h + 1) * 512], start=c == 0, stop=c == 2 * FF_STEPS - 1)
                    if c == 2 * FF_STEPS - 1:
                        m.then_inc(sg("mix_done"), 1)
                if c < 2 * FF_STEPS - 1:
                    m.then_inc(sg("down_done"), 1)

            for c in range(2 * FF_STEPS):
                if c >= 2:
                    pe.wait_ge(sg("hid_ready"), c - 1)
                for i in range(2):
                    n = 3 * (c // 2) + i
                    pe.wait_ge(*item_full(n))
                    for k in range(KD):
                        m = pe.matmul(ps[:, c % 2, i * SEQ:(i + 1) * SEQ], slot(n)[:, k, (c % 2) * P:(c % 2 + 1) * P],
                                      hT[:, k, :], start=k == 0, stop=k == KD - 1)
                m.then_inc(sg("gu_done"), 1)
                if c >= 1:
                    ffn_down(c - 1)
            ffn_down(2 * FF_STEPS - 1)
            transposed_nat(2)
            pe.wait_ge(sg("hT_ready"), 12)
            for i in range(QKV // IW):
                pe.wait_ge(*item_full(ITEM_QKV + i))
                for t in range(NT):
                    for k in range(KD):
                        m = pe.matmul(ps[:, 3 * t + i // 2, (i % 2) * IW:(i % 2 + 1) * IW], hT[:, k, t * P:(t + 1) * P],
                                      slot(ITEM_QKV + i)[:, k, :], start=k == 0, stop=k == KD - 1)
                m.then_inc(sg("proj_done"), 1)
            pe.wait_ge(sg("rope_done"), NT)
            for b in range(4):
                for k in (2 * b, 2 * b + 1):
                    for t in range(NT):
                        m = pe.transpose(ps[:, b, (k % 2) * SEQ + t * P:(k % 2) * SEQ + (t + 1) * P],
                                         qkv[:, t, k * P:(k + 1) * P], ident[:, :])
                m.then_inc(sg("q_tr"), 1)
            for b in range(2):
                for k in (2 * b, 2 * b + 1):
                    for t in range(NT):
                        m = pe.transpose(ps[:, 4 + b, (k % 2) * SEQ + t * P:(k % 2) * SEQ + (t + 1) * P],
                                         k_dup[:, t, k].rearrange("p c d -> p (c d)"), ident[:, :])
                m.then_inc(sg("k_tr"), 1)
            pe.wait_ge(sg("qT_ready"), 6)

            def scores(u):
                t, hp = divmod(u, NH // 2)
                if u >= 2:
                    pe.wait_ge(sg("probs_ready"), 2 * (u - 1))
                for h in range(2):
                    m = pe.matmul(ps[:, 2 * (u % 2) + h, 0:SEQ], qT[64 * h:64 * h + 64, hp, t * P:(t + 1) * P],
                                  kT[64 * h:64 * h + 64, 2 * hp // HPK, :], start=True, stop=True)
                m.then_inc(sg("scores_ready"), 1)

            def prob_transposes(u):
                pe.wait_ge(sg("probs_ready"), 2 * (u + 1))
                if u >= 2:
                    pe.wait_ge(sg("probT_ready"), u - 1)
                for h in range(2):
                    for c in range(NT):
                        m = pe.transpose(ps[:, 4 + u % 2, (2 * h + c) * P:(2 * h + c + 1) * P], prob[u % 2][:, h, c * P:(c + 1) * P], ident[:, :])
                m.then_inc(sg("p_tr"), 1)

            def prob_values(u):
                t, hp = divmod(u, NH // 2)
                pe.wait_ge(sg("probT_ready"), u + 1)
                if u % 4 == 0 and u >= 8:
                    pe.wait_ge(sg("o_ready"), u // 4 - 1)
                kv = 2 * hp // HPK
                for h in range(2):
                    for c in range(NT):
                        m = pe.matmul(ps[:, 6 + (u // 4) % 2, (2 * (u % 4) + h) * HD:(2 * (u % 4) + h + 1) * HD], probT[u % 2][:, h, c, :],
                                      qkv[:, c, (QK + kv) * HD:(QK + kv + 1) * HD], start=c == 0, stop=c == NT - 1)
                m.then_inc(sg("pv_done"), 1)

            for u in range(UNITS + 2):
                if u < UNITS:
                    scores(u)
                if 1 <= u <= UNITS:
                    prob_transposes(u - 1)
                if u >= 2:
                    prob_values(u - 2)
            pe.wait_ge(sg("o_ready"), 4)
            for b in range(4):
                for k in (2 * b, 2 * b + 1):
                    for t in range(NT):
                        m = pe.transpose(ps[:, b, (k % 2) * SEQ + t * P:(k % 2) * SEQ + (t + 1) * P],
                                         o_nat[:, t, k * P:(k + 1) * P], ident[:, :])
                m.then_inc(sg("oT_tr"), 1)
            pe.wait_ge(sg("hT_ready"), 16)
            for t in range(NT):
                for i in range(D // IW):
                    pe.wait_ge(*item_full(ITEM_WO + i))
                    for k in range(KD):
                        m = pe.matmul(ps[:, 4 + 2 * t + i // 2, (i % 2) * IW:(i % 2 + 1) * IW], hT[:, k, t * P:(t + 1) * P],
                                      slot(ITEM_WO + i)[:, k, :], start=k == 0, stop=k == KD - 1)
                m.then_inc(sg("mix_done"), 1)
            transposed_nat(3)
            pe.wait_ge(sg("hT_ready"), 20)
            pe.wait_ge(sg("router_in"), 16)
            for t in range(NT):
                for k in range(KD):
                    m = pe.matmul(ps[:, 4, t * EXP:(t + 1) * EXP], hT[:, k, t * P:(t + 1) * P], w_router[:, k, :],
                                  start=k == 0, stop=k == KD - 1)
            m.then_inc(sg("logits_mm"), 1)
            pe.wait_ge(sg("chosen_ready"), 1)
            pe.matmul(ps[:, 5, 0:EXP], upper[:, :], chosen[:, 0, 0:EXP], start=True, stop=True)
            pe.matmul(ps[:, 5, EXP:2 * EXP], ones[:, :], chosen[:, 0, 0:EXP], start=True, stop=False)
            pe.matmul(ps[:, 5, EXP:2 * EXP], upper[:, :], chosen[:, 1, 0:EXP], start=False, stop=True)
            for t in range(NT):
                m = pe.matmul(ps[0:1, 6, 0:EXP], ones[:, 0:1], chosen[:, t, 0:EXP], start=t == 0, stop=t == NT - 1)
            m.then_inc(sg("rank_mm"), 1)
            pe.wait_ge(sg("counts_ready"), 1)

            def gather(e, V):
                pe.wait_ge(sg("sel_ready"), NT * (e + 1))
                for b in range(4):
                    for k in (2 * b, 2 * b + 1):
                        for t in range(NT):
                            m = pe.matmul(ps[:, b, (k % 2) * SEQ:(k % 2) * SEQ + V], h_moe[:, t, k * P:(k + 1) * P],
                                          sel[:, t, 0:V], start=t == 0, stop=t == NT - 1)
                    m.then_inc(sg("gather_mm"), 1)
                pe.wait_ge(sg("xg_ready"), 4 * (e + 1))

            def expert_narrow(e, T):
                M, w = P // T, IW // T
                part = [0, 2, 1, 3] if T == 4 else list(range(T))
                gather(e, M)

                def transposes(s):
                    pe.wait_ge(sg("moe_hid"), CHUNKS * e + 2 * s + 2)
                    if s == 0:
                        pe.wait_ge(sg("acc_done"), 4 * e + 1)
                    if T == 1:
                        for f in range(2):
                            m = pe.transpose(ps[:, 4 + s % 2, f * P:(f + 1) * P], m_hid[s % 2][:, f * P:(f + 1) * P], ident[:, :])
                    elif T == 2:
                        m = pe.transpose(ps[:, 4 + s % 2, 0:P], m_hid[s % 2][:, 0:P], ident[:, :])
                    else:
                        for a in range(2):
                            m = pe.matmul(ps[64 * a:64 * a + 64, 4 + s % 2, 0:64], m_hid[s % 2][:, 0:64], ident[:, 64 * a:64 * a + 64],
                                          start=True, stop=True)
                    m.then_inc(sg("hid_tr"), 1)

                def down(s):
                    pe.wait_ge(*moe_item_full(e, 3 * s + 2))
                    pe.wait_ge(sg("hidT_ready"), EX_STEPS * e + s + 1)
                    dn = slot_down(ITEM_MOE + 3 * s + 2)
                    n = min(D // T, 512)
                    for f in range(2):
                        for j in range(max(T, 2)):
                            o = ps[M * j:M * j + M, 2, 0:n] if T > 1 else ps[:, 2 + j, :]
                            m = pe.matmul(o, m_hidT[s % 2][:, f * M:(f + 1) * M], dn[:, f, j * n:(j + 1) * n],
                                          start=s == 0 and f == 0, stop=s == EX_STEPS - 1 and f == 1)
                    m.then_inc(sg("moe_down"), 2)

                for s in range(EX_STEPS):
                    if s >= 2:
                        pe.wait_ge(sg("moe_hid"), CHUNKS * e + 2 * (s - 1))
                    for i in range(2):
                        pe.wait_ge(*moe_item_full(e, 3 * s + i))
                    gu = at(((ITEM_MOE + 3 * s) % SLOTS) * ITEM, 2, KD, IW)
                    for k in range(KD):
                        for j in range(T):
                            o = ps[M * j:M * j + M, s % 2, :].rearrange("p (i n) -> p i n", i=2)[:, :, 0:w]
                            m = pe.matmul(o, xg[:, k, 0:M], gu[:, :, k, part[j] * w:(part[j] + 1) * w], start=k == 0, stop=k == KD - 1)
                    m.then_inc(sg("moe_gu"), 2)
                    if s >= 1:
                        transposes(s - 1)
                    if s >= 2:
                        down(s - 2)
                    if s == SEL_AT:
                        pe.wait_ge(sg("selg_ready"), NT * (e + 1))
                        for t in range(NT):
                            m = pe.transpose(ps[:, 6, t * P:(t + 1) * P], sel_g[:, t, 0:P], ident[:, :])
                            if t == 0:
                                m.then_inc(sg("y_tr"), 2)
                        m.then_inc(sg("selg_tr"), 1)
                transposes(EX_STEPS - 1)
                down(EX_STEPS - 2)
                down(EX_STEPS - 1)
                pe.wait_ge(sg("selgT_ready"), e + 1)
                pe.wait_ge(sg("y_ready"), 4 * (e + 1))
                for q in range(4):
                    j = q * T // 4
                    y0 = (q - j * 4 // T) * SEQ
                    for t in range(NT):
                        m = pe.matmul(ps[:, 4 + q, t * SEQ:(t + 1) * SEQ], sel_gT[M * j:M * j + M, 0, t, :],
                                      y_lo[M * j:M * j + M, y0:y0 + SEQ], start=True, stop=True)
                    m.then_inc(sg("scatter_mm"), 1)

            def expert_wide(e, V):
                gather(e, V)

                def down(c):
                    n = ITEM_MOE + 3 * (c // 2) + 2
                    pe.wait_ge(*moe_item_full(e, n - ITEM_MOE))
                    pe.wait_ge(sg("moe_hid"), CHUNKS * e + c + 1)
                    if c == 0:
                        pe.wait_ge(sg("acc_done"), 4 * e + 1)
                    for k in range(KD):
                        m = pe.matmul(ps[:, 2 + k // 2, (k % 2) * SEQ:(k % 2) * SEQ + V], slot_down(n)[:, c % 2, k * P:(k + 1) * P],
                                      m_hid[c % 2][:, 0:V], start=(c == 0 and k % 2 == 0), stop=c == CHUNKS - 1, skip_group_check=True)
                    m.then_inc(sg("moe_down"), 1)

                for c in range(CHUNKS):
                    if c >= 2:
                        pe.wait_ge(sg("moe_hid"), CHUNKS * e + c - 1)
                    for i in range(2):
                        n = ITEM_MOE + 3 * (c // 2) + i
                        pe.wait_ge(*moe_item_full(e, n - ITEM_MOE))
                        for k in range(KD):
                            m = pe.matmul(ps[:, c % 2, i * SEQ:i * SEQ + V], slot(n)[:, k, (c % 2) * P:(c % 2 + 1) * P],
                                          xg[:, k, 0:V], start=k == 0, stop=k == KD - 1)
                    m.then_inc(sg("moe_gu"), 1)
                    if c >= 1:
                        down(c - 1)
                    if c == SEL_AT + 3:
                        pe.wait_ge(sg("selg_ready"), NT * (e + 1))
                        for ct in range(NT):
                            for t in range(NT):
                                m = pe.transpose(ps[:, 6, (NT * ct + t) * P:(NT * ct + t + 1) * P], sel_g[:, t, ct * P:(ct + 1) * P], ident[:, :])
                                if ct == 0 and t == 0:
                                    m.then_inc(sg("hid_tr"), EX_STEPS)
                        m.then_inc(sg("selg_tr"), 1)
                down(CHUNKS - 1)
                pe.wait_ge(sg("yT_ready"), 4 * (e + 1))
                for ct in range(2):
                    for k in range(KD):
                        m = pe.transpose(ps[:, (6 if ct == 0 else 0) + k // 4, (k % 4) * P:(k % 4 + 1) * P],
                                         yT[:, k, ct * P:(ct + 1) * P], ident[:, :])
                    m.then_inc(sg("y_tr"), 1)
                pe.wait_ge(sg("selgT_ready"), e + 1)
                pe.wait_ge(sg("y_ready"), 4 * (e + 1))
                for q in range(4):
                    for t in range(NT):
                        for ct in range(2):
                            kk = min(V - ct * P, P)
                            m = pe.matmul(ps[:, 4 + q, t * SEQ:(t + 1) * SEQ], sel_gT[0:kk, ct, t, :],
                                          (y_lo if ct == 0 else y_hi)[0:kk, q * SEQ:(q + 1) * SEQ], start=ct == 0, stop=ct == 1)
                    m.then_inc(sg("scatter_mm"), 1)

            with pe.Fori(0, EXP) as e:
                n = pe.value_load(cnt_i[0:1, bass.ds(e, 1)], min_val=0, max_val=SEQ)
                with pe.If(n > P // 2):
                    with pe.If(n > P):
                        with pe.If(n > WIDE[0]):
                            expert_wide(e, WIDE[1])
                        with pe.Else():
                            expert_wide(e, WIDE[0])
                    with pe.Else():
                        expert_narrow(e, 1)
                with pe.Else():
                    with pe.If(n > P // 4):
                        expert_narrow(e, 2)
                    with pe.Else():
                        expert_narrow(e, 4)
            pe.wait_ge(sg("sel_ready"), NT * (EXP + 1))


_INS = ("x", "norm_gains", "ssm_w_in", "ssm_lambda_re", "ssm_lambda_im", "ssm_log_step", "ssm_b_re", "ssm_b_im",
        "ssm_c_re", "ssm_c_im", "ssm_d", "ssm_w_glu", "ssm_w_out", "ffn_w_gate", "ffn_w_up", "ffn_w_down",
        "attn_w_qkv", "attn_q_gain", "attn_k_gain", "attn_w_out", "moe_w_router", "moe_w_gate", "moe_w_up",
        "moe_w_down")


def rope_tables(seq, axis_dim, grid_w=64, theta=10000.0):
    import numpy as np
    freqs = np.float32(theta) ** (-np.arange(0, axis_dim, 2, dtype=np.float32) / np.float32(axis_dim))
    token = np.arange(seq)
    ang = np.concatenate([(token // grid_w).astype(np.float32)[:, None] * freqs,
                          (token % grid_w).astype(np.float32)[:, None] * freqs], axis=1).astype(np.float32)
    return np.cos(ang).astype(np.float32), np.sin(ang).astype(np.float32)


def build(nc, inputs):
    import numpy as np
    arrays = {f"in_{n}": np.ascontiguousarray(inputs[n]) for n in _INS}
    seq, head = arrays["in_x"].shape[1], arrays["in_attn_q_gain"].shape[1]
    arrays["rope_cos"], arrays["rope_sin"] = rope_tables(seq, head // 2)
    args = [nc.dram_tensor(n, a.shape, mybir.dt.from_np(a.dtype), kind="ExternalInput").ap() for n, a in arrays.items()]
    out = nc.dram_tensor("out", arrays["in_x"].shape, mybir.dt.float32, kind="ExternalOutput").ap()
    hybrid_trunk(nc, *args, out)
    return arrays, out


def kernel(**inputs):
    import concourse.bacc as bacc
    from concourse.bass_utils import run_bass_kernel_spmd
    nc = bacc.Bacc("TRN2", target_bir_lowering=False, num_devices=1)
    arrays, _ = build(nc, inputs)
    return run_bass_kernel_spmd(nc, [arrays], core_ids=[0]).results[0]["out"]
```

```python
import concourse.bass as bass
from concourse import mybir
from contextlib import ExitStack

WIDE = (136, 160, 256)


def hybrid_trunk(nc, x_in, norm_gains, ssm_w_in, ssm_lambda_re, ssm_lambda_im, ssm_log_step,
                 ssm_b_re, ssm_b_im, ssm_c_re, ssm_c_im, ssm_d, ssm_w_glu, ssm_w_out,
                 ffn_w_gate, ffn_w_up, ffn_w_down, attn_w_qkv, attn_q_gain, attn_k_gain,
                 attn_w_out, moe_w_router, moe_w_gate, moe_w_up, moe_w_down,
                 rope_cos, rope_sin, out):
    f32, i32 = mybir.dt.float32, mybir.dt.int32
    ALU, ACT, AX = mybir.AluOpType, mybir.ActivationFunctionType, mybir.AxisListType
    MUL, ADD, SUB = ALU.mult, ALU.add, ALU.subtract

    P = 128
    SEQ, D = x_in.shape[1], x_in.shape[2]
    NT, KD = SEQ // P, D // P
    DIRS, GROUPS, ST = ssm_lambda_re.shape[1:]
    GC = D // GROUPS
    CH = P // GC
    NC = SEQ // CH
    GP = GROUPS // 2
    DG = DIRS * GP
    NPOW = CH + 1
    SB = 4
    NB = DG // SB
    EPS = 1e-6
    IW = 256
    ITEM = KD * IW
    SLOTS = 21
    FF_STEPS = ffn_w_gate.shape[2] // IW
    EXP, EFF = moe_w_gate.shape[1], moe_w_gate.shape[3]
    EX_STEPS = EFF // IW
    HALF = EX_STEPS // 2
    QKV = attn_w_qkv.shape[2]
    NH, HD = D // attn_q_gain.shape[1], attn_q_gain.shape[1]
    NKV = (QKV // HD - NH) // 2
    HPK = NH // NKV
    QK = NH + NKV
    assert HALF * 3 == SLOTS and EX_STEPS == 2 * HALF and CH * GC == P and NC * CH == SEQ

    ctx = ExitStack()
    with ctx:
        def sb(name, shape, dt=f32):
            return ctx.enter_context(nc.sbuf_tensor(name, shape, dt))

        sems = {}

        def sg(name):
            if name not in sems:
                sems[name] = ctx.enter_context(nc.semaphore(name))
            return sems[name]

        BIGW = 53056
        FIXED = 448
        fixed = sb("fixed", [P, FIXED])
        cnt_i = sb("cnt_i", [1, EXP], i32)
        BIGW_ = BIGW - FIXED
        with nc.sbuf_tensor("big", [P, BIGW_], f32) as big:
            pass
        with ExitStack() as reuse:
            slot_f = [reuse.enter_context(nc.sbuf_tensor(f"slot{i}", [P, ITEM], f32)) for i in range(SLOTS)]
            ff_f = reuse.enter_context(nc.sbuf_tensor("ff_f", [P, 2048], f32))
        r32 = mybir.dt.float32r
        slot_r = [sb(f"slot_r{i}", [P, ITEM], r32) for i in range(SLOTS)]
        ff_r = sb("ff_r", [P, 2048], r32)
        sb("x_place", [P, 2048])
        hT_r_ = sb("hT_r", [P, 2048], r32)
        nat_r = sb("nat_r", [P, 2048], r32)
        sb("rest", [P, BIGW_ - ITEM * SLOTS - 4 * 2048])

        ps = ctx.enter_context(nc.psum_tensor("ps", [P, 8, 512], f32))
        x_scr = nc.dram_tensor("x_scr", (P, NT * D), f32, kind="Internal").ap()
        k_scr = nc.dram_tensor("k_scr", (GROUPS, GC, 15 * GC), f32, kind="Internal").ap()

        def shaped(v, *shape):
            names = "abcd"[:len(shape)]
            return v.rearrange(f"p ({' '.join(names)}) -> p {' '.join(names)}",
                               **{names[i]: shape[i] for i in range(len(shape) - 1)})

        def at(off, *shape):
            n = 1
            for s in shape:
                n *= s
            assert off + n <= BIGW
            v = fixed[:, off - BIGW_:off - BIGW_ + n] if off >= BIGW_ else big[:, off:off + n]
            return v if len(shape) == 1 else shaped(v, *shape)

        TOP = BIGW - 448
        ident = at(TOP, P)
        gcol = at(TOP + 128, 64)
        ssq = at(TOP + 192, 2)
        msq = at(TOP + 194, 2)
        rstd = at(TOP + 196, 2)
        nhalf = at(TOP + 198, 48)
        hms = at(TOP + 246, 48)
        hrs = at(TOP + 294, 48)
        small = at(TOP + 342, 106)

        def slot(n):
            return at((n % SLOTS) * ITEM, KD, IW)

        def slot_down(n):
            return at((n % SLOTS) * ITEM, 2, D)

        RA, RDS, RC, REZ, RB = 0, 8192, 20480, 28672, 36864
        X_, HT, N1, R8_ = 45056, 47104, 49152, 51200
        x = at(X_, NT, D)
        hT = at(HT, KD, SEQ)
        nat = at(N1, NT, D)
        nat_flat = at(N1, NT * D)
        post_gain = at(R8_, D)
        w_in = at(RA, 4, KD, IW)
        xbd = at(RA, 2, DG, 2, NC)
        u_grp = at(RB, GROUPS, CH, GC)
        u_tok = at(RA, CH, D)
        w_glu = at(RB, 4, KD, IW)
        w_out0 = at(REZ, 4, KD, IW)
        bbar = at(RDS, 2, DG + 1, GC)
        cP = at(RDS + 2080, 2, DG, GC)
        S_ = at(RDS + 4128, 2, DG, NC)
        bP = at(RDS + 4128, 2, DG, GC)
        pw = at(RDS + 8224, 2, NPOW, DG)
        pd = at(RDS + 9376, 2, NPOW, DG)
        def tmp(n):
            assert n < 27
            return at(RDS + 10528 + 64 * n, DG)
        yg = at(RDS + 4128, GROUPS, NC)
        gT = at(RDS + 4128 + 2048, KD, SEQ)
        mT = hT
        wt = [at(RC + 1024 * i, 2, SB, P) for i in range(2)]
        wm = [at(RC + 2048 + 1024 * i, SB, 2, P) for i in range(2)]
        kall = at(RC, 2, 8, 15, GC)
        kzero = at(RC + 3840, 2, 8, GC)
        mtmp = [at(RC + 5800 + 576 * i, SB * NPOW * GC) for i in range(4)]
        ptmp = [mtmp[2:4], [at(RC + 4100 + 576 * i, SB * NPOW * GC) for i in range(2)]]
        GA = 38
        toe = [at(REZ, GROUPS // 2, P), at(RC + 4096, GROUPS // 2, P)]
        g_tok = at(RA, CH, D)
        ec = at(REZ, 2, DG, NC)
        zz = at(REZ + 4096, 2, DG, NC)
        vv = [at(i, 2, SB, NPOW, GC) for i in (N1 + 1024, RB + 3 * ITEM)]
        raw_b = at(RB, 2, P, GC)
        raw_c = at(RB + 4096, 2, GC, P)
        raw_l = at(REZ, 4, P)
        raw_g = at(REZ + 512, P)
        raw_s = at(REZ + 640, 2)
        raw_d = at(REZ + 704, GC)
        raw_dx = at(REZ + 768, CH, GC)
        uc = at(HT, GROUPS, NC)
        ud = at(N1, GROUPS, NC)
        tmp8 = at(N1, GP, NC)
        r8t = at(N1 + 1024 + 1152, GP, NC)
        sig = at(N1, KD, SEQ)
        dcol = at(52352, GROUPS)

        sil = [ff_f[:, 256 * i:256 * i + 256] for i in range(2)]
        hid_lo = [ff_r[:, 1024 + 256 * i:1280 + 256 * i] for i in range(2)]
        hid_f = ff_f[:, 1536:1792]
        hid_hi_r = [ff_r[:, 512 + 256 * i:768 + 256 * i] for i in range(2)]
        hT_r = shaped(hT_r_[:, :], KD, SEQ)
        qkv = at(43008, NT, QKV)
        kT = at(R8_, NKV, SEQ)
        qT = hT
        k_dup = at(46080, NT, NKV, 2, HD)
        rope_m = [at(R8_ + 256 * i, NH // 2, HD // 2) for i in range(4)]
        head_sq = at(N1, QK, HD)
        o_nat = qkv
        prob = [at(N1 + 512 * i, 2, SEQ) for i in range(2)]
        probT = [at(N1 + 1024 + 512 * i, 2, NT, P) for i in range(2)]
        rope_raw = at(52224, 2, NT, HD // 2)
        qk_gain = at(52352, 2, HD)
        rope_t = at(N1 + 1280, 2, 4, NT, HD // 2)
        nmax, psum_, prcp = (small[:, 32 * i:32 * i + 32] for i in range(3))
        UNITS = NT * NH // 2
        h_moe = nat
        acc = x
        xg = hT
        yT = hT
        moe_gain = at(44032, D)
        y_lo = at(43008, D)
        y_hi = at(HT, D)
        sel_g = at(43008, NT, SEQ)
        sel = at(44032, NT, SEQ)
        sel_gT = at(44544, NT, NT, P)
        m_hidT = [at(43520 + 256 * i, SEQ) for i in range(2)]
        m_sil = [at(51200 + 256 * i, SEQ) for i in range(2)]
        m_hid = [at(51712 + 256 * i, SEQ) for i in range(2)]
        iota = at(52224, SEQ)
        iota_i = at(43700, SEQ).bitcast(i32)
        rank = at(52480, NT, EXP + 1)
        chosen = at(52498, NT, EXP + 1)
        gate = at(52516, NT, EXP + 1)
        w_router = gcol.rearrange("p (k e) -> p k e", k=KD)
        upper = at(43008, P)
        ones = at(43136, P)
        lower_e = at(43264, EXP, EXP)
        gt_ = at(43328, NT, EXP, EXP)
        eq_ = at(43456, NT, EXP, EXP)
        logit = at(43584, NT, EXP)
        lshift = at(43600, NT, EXP)
        wexp = at(43616, NT, EXP)
        beats = at(43632, NT, EXP)
        lmax = at(43648, NT)
        wsum = at(43650, NT)
        last_gain = at(((EXP * 3 * EX_STEPS) % SLOTS) * ITEM, D)
        SEL_AT = 3
        CHUNKS = EFF // P
        EI = 3 * EX_STEPS

        block = ctx.enter_context(nc.Block())
        w_in_v = [w[0].rearrange("(k p) n -> p k n", p=P) for w in (ssm_w_in, ssm_w_glu, ssm_w_out)]

        def cols(w, j):
            return w.rearrange("(k p) n -> p k n", p=P)[:, :, j * IW:(j + 1) * IW]

        def rows(w, j):
            return w[j * IW:(j + 1) * IW, :].rearrange("(f p) n -> p f n", p=P)

        items = []
        for j in range(FF_STEPS):
            items += [cols(ffn_w_gate[0], j), cols(ffn_w_up[0], j), rows(ffn_w_down[0], j)]
        ITEM_QKV = len(items)
        items += [cols(attn_w_qkv[0], j) for j in range(QKV // IW)]
        ITEM_WO = len(items)
        items += [cols(attn_w_out[0], j) for j in range(D // IW)]
        ITEM_MOE = len(items)
        full = [f"item_in_slot{n}" for n in range(SLOTS)]
        FF_SLOTS = 10
        QKV_HI = (17, 18, 19, 20, 0, 1)

        def raw_slot(n):
            return n % FF_SLOTS if n < ITEM_QKV else (n - ITEM_QKV + 3 if n < ITEM_WO else n - ITEM_WO + 13)

        def hi_slot(n):
            return FF_SLOTS + n % FF_SLOTS if n < ITEM_QKV else (QKV_HI[n - ITEM_QKV] if n < ITEM_WO else n - ITEM_WO + 9)

        def before_hi(n):
            if n < ITEM_QKV:
                return n - FF_SLOTS if n >= FF_SLOTS else None
            return (27, 28, 29, None, 30, 31, 29, 30, 31, 32)[n - ITEM_QKV]

        def down_view(n):
            return n < ITEM_QKV and n % 3 == 2

        def hi_lo(n):
            shape = (2, D) if down_view(n) else (KD, IW)
            return shaped(slot_r[hi_slot(n)][:, :], *shape), shaped(slot_r[raw_slot(n)][:, :], *shape)

        def raw(n):
            return shaped(slot_f[raw_slot(n)][:, :], *((2, D) if down_view(n) else (KD, IW)))

        HT_LO = (None,) + tuple(shaped(v[:, :], KD, SEQ) for v in (nat_r, slot_r[2], slot_r[17]))

        def item_full(n):
            return sg(full[raw_slot(n)]), 16 * sum(raw_slot(k) == raw_slot(n) for k in range(n + 1))

        TR_BANKS = ((0, 1, 2, 3), (4, 5, 6, 7), (0, 1, 6, 7), (0, 1, 2, 3))

        Q_BANKS, K_BANKS = (0, 1, 2, 6), (7, 3)

        def item_read(n):
            if n == ITEM_QKV - 1:
                return sg("mix_done"), 2 * NT
            if n >= ITEM_WO:
                return sg("mix_done"), 3 * NT
            if n < ITEM_QKV:
                return sg("gu_done" if n % 3 < 2 else "down_done"), 2 * (n // 3) + 2
            return sg("proj_done"), NT

        def moe_item_full(e, m):
            earlier = sum(raw_slot(k) == m % SLOTS for k in range(ITEM_MOE))
            return sg(full[m % SLOTS]), 16 * (earlier + m // SLOTS + 1) + 32 * e

        @block.sync
        def _(sp):
            for t in range(NT):
                sp.dma_start(x[:, t, :], x_in[0, t * P:(t + 1) * P, :]).then_inc(sg(f"x_in{t}"), 16)
            lam_v = [w[0].rearrange("d (g a) p -> (d g) (a p)", a=2) for w in (ssm_lambda_re, ssm_lambda_im)]
            for i in range(2):
                sp.dma_start(raw_l[0:DG, i, :], lam_v[i]).then_inc(sg("lam_in"), 16)
            sp.dma_start(raw_s[0:DG, :], ssm_log_step[0].rearrange("d (g a) -> (d g) a", a=2)).then_inc(sg("lam_in"), 16)
            sp.dma_start(raw_g[0:64, :], norm_gains.rearrange("l n (k p) -> (l n k) p", p=P)).then_inc(sg("gain_in"), 16)
            sp.dma_start(raw_d[0:GROUPS, :], ssm_d[0].rearrange("(g s) -> g s", s=GC)).then_inc(sg("gain_in"), 16)
            for i in range(4):
                sp.dma_start(w_in[:, i, :, :], w_in_v[0][:, :, i * IW:(i + 1) * IW]).then_inc(sg(f"mix_w{i}"), 16)
            for i, w in enumerate((ssm_b_re, ssm_b_im)):
                sp.dma_start(raw_b[0:DG, i, :, :], w[0].rearrange("d (g a) p s -> (d g) (a p) s", a=2)).then_inc(sg("b_in"), 16)
            for i, w in enumerate((ssm_c_re, ssm_c_im)):
                for a in range(2):
                    sp.dma_start(raw_c[0:DG, i, :, a * ST:(a + 1) * ST],
                                 w[0].rearrange("d (g a) s p -> a (d g) s p", a=2)[a]).then_inc(sg("c_in"), 16)
            sp.wait_ge(sg("u_mm"), NT)
            for t in range(NT):
                sp.wait_ge(sg("u_act"), t + 1)
                for s in range(CH):
                    sp.dma_start(u_tok[16 * t:16 * t + 16, s, :], nat[s:P:CH, t, :]).then_inc(sg("u_tok_in"), 16)
            sp.wait_ge(sg("uc_tr"), 4)
            for i in range(3):
                sp.dma_start(w_glu[:, i, :, :], w_in_v[1][:, :, i * IW:(i + 1) * IW]).then_inc(sg(f"mix_w{i}"), 16)
            k_w = k_scr.rearrange("(q j a) s x -> j a s q x", j=SB, a=2)
            for hf in range(2):
                qs = slice(4 * hf, 4 * hf + 4)
                sp.wait_ge(sg("k_final"), hf + 1)
                for j in range(SB):
                    for a in range(2):
                        sp.dma_start(k_w[j, a, :, qs], kall[32 * j:32 * j + GC, a, qs, :, :].rearrange("p q t o -> p q (t o)")).then_inc(sg("k_stored"), 16)
                sp.wait_ge(sg("k_stored"), 16 * 2 * SB * (hf + 1))
                if hf == 0:
                    sp.wait_ge(sg("x_ready"), 8)
                else:
                    sp.wait_ge(sg("y_state"), NB)
                for s in range(CH):
                    sp.dma_start(toe[hf][GC * s:GC * (s + 1), :, :],
                                 k_scr[32 * hf:32 * hf + 32].rearrange("g s x -> s g x")[:, :, (CH - 1 - s) * GC:(CH - 1 - s) * GC + P]).then_inc(sg(f"toe_in{hf}"), 16)
            sp.dma_start(w_glu[:, 3, :, :], w_in_v[1][:, :, 3 * IW:4 * IW]).then_inc(sg("glu_w3"), 16)
            for i in (2, 3, 0, 1):
                if i == 0:
                    sp.wait_ge(sg("y_mm"), 2)
                sp.dma_start(w_out0[:, i, :, :], w_in_v[2][:, :, i * IW:(i + 1) * IW]).then_inc(sg(f"mix_w{i}"), 16)
            sp.dma_start(post_gain[:, :], norm_gains[0, 1:2, :].to_broadcast([P, D])).then_inc(sg("post_gain_in"), 16)
            for n, src in enumerate(items):
                if n == 0:
                    sp.wait_ge(sg("gT_tr"), 4)
                if n == 4:
                    sp.wait_ge(sg("m_ready"), 8)
                if n >= FF_SLOTS:
                    sp.wait_ge(*item_read(n - FF_SLOTS if n < ITEM_WO else n - 16))
                sp.dma_start(raw(n), src).then_inc(sg(full[raw_slot(n)]), 16)
                if n == FF_SLOTS:
                    sp.wait_ge(sg("x_done"), 2)
                    sp.dma_start(post_gain[:, :], norm_gains[0, 3:4, :].to_broadcast([P, D])).then_inc(sg("post_gain_in"), 16)
                    for i, w in enumerate((rope_cos, rope_sin)):
                        sp.dma_start(rope_raw[:, i], w.rearrange("(t p) f -> p t f", p=P)).then_inc(sg("rope_in"), 16)
                    for i, w in enumerate((attn_q_gain, attn_k_gain)):
                        sp.dma_start(qk_gain[:, i], w[0:1, :].to_broadcast([P, HD])).then_inc(sg("rope_in"), 16)
            def moe_item(e, m):
                j, kind = divmod(m, 3)
                js = slice(j * IW, (j + 1) * IW)
                if kind < 2:
                    w = (moe_w_gate, moe_w_up)[kind][0, bass.ds(e, 1), :, js].rearrange("e (k p) n -> p (e k) n", p=P)
                    dst = slot(m)
                else:
                    w = moe_w_down[0, bass.ds(e, 1), js, :].rearrange("e (f p) n -> p (e f) n", p=P)
                    dst = slot_down(m)
                sp.dma_start(dst, w).then_inc(sg(full[m % SLOTS]), 16)

            def moe_wait_read(e, m):
                prev = m - SLOTS + (EI if m < SLOTS else 0)
                expert = e - 1 if m < SLOTS else e
                sp.wait_ge(sg("moe_gu" if prev % 3 < 2 else "moe_down"), CHUNKS * expert + 2 * (prev // 3) + 2)

            sp.wait_ge(sg("x_done"), 4)
            sp.dma_start(x_scr[:, :], x.rearrange("p t d -> p (t d)")).then_inc(sg("x_stored"), 16)
            LATE = range(9, 18)
            sp.wait_ge(sg("proj_done"), NT)
            for m in range(SLOTS):
                if m not in LATE:
                    moe_item(0, m)
            sp.wait_ge(sg("scores_ready"), UNITS)
            sp.dma_start(post_gain[:, :], norm_gains[1, 1:2, :].to_broadcast([P, D])).then_inc(sg("post_gain_in"), 16)
            sp.wait_ge(sg("oT_tr"), 4)
            sp.wait_ge(sg("x_stored"), 16)
            sp.dma_start(x.rearrange("p t d -> p (t d)"), x_scr[:, :]).then_inc(sg("x_back"), 16)
            sp.dma_start(moe_gain[:, :], norm_gains[1, 2:3, :].to_broadcast([P, D])).then_inc(sg("moe_gain_in"), 16)
            sp.dma_start(w_router, moe_w_router[0].rearrange("(k p) e -> p k e", p=P)).then_inc(sg("router_in"), 16)
            sp.wait_ge(sg("mix_done"), 3 * NT)
            for m in LATE:
                moe_item(0, m)
            sp.wait_ge(sg("x_done"), 6)
            sp.dma_start(x_scr[:, :], x.rearrange("p t d -> p (t d)")).then_inc(sg("x_stored"), 16)
            for m in range(SLOTS, EI):
                moe_wait_read(0, m)
                moe_item(0, m)
            with sp.Fori(1, EXP) as e:
                for m in range(EI):
                    moe_wait_read(e, m)
                    moe_item(e, m)
            sp.wait_ge(sg("moe_gu"), CHUNKS * (EXP - 1) + 2 * HALF + 2)
            sp.dma_start(last_gain[:, :], norm_gains[1, 3:4, :].to_broadcast([P, D])).then_inc(sg("last_gain_in"), 16)
            sp.wait_ge(sg("gather_mm"), 4 * EXP)
            sp.wait_ge(sg("x_stored"), 32)
            sp.dma_start(nat.rearrange("p t d -> p (t d)"), x_scr[:, :]).then_inc(sg("x_back"), 16)
            for t in range(NT):
                sp.wait_ge(sg("y_final"), t + 1)
                sp.dma_start(out[0, t * P:(t + 1) * P, :], acc[:, t, :]).then_inc(sg("out_stored"), 16)
            sp.wait_ge(sg("out_stored"), 16 * NT)

        @block.gpsimd
        def _(pool):
            step = [0]

            def link(ins):
                step[0] += 1
                ins.then_inc(sg("pool_step"), 1)
                pool.wait_ge(sg("pool_step"), step[0])

            link(pool.memset(ident[:, :], 0.0))
            pool.affine_select(out=ident[:, :], in_=ident[:, :], compare_op=ALU.not_equal, fill=1.0,
                               base=0, pattern=[[-1, P]], channel_multiplier=1).then_inc(sg("ident_ready"), 1)
            pool.memset(bbar[:, :, DG, :], 0.0).then_inc(sg("bbar_pad"), 1)
            link(pool.memset(nhalf[:, :], -0.5))

            def rstd_of(n):
                for t in range(NT):
                    pool.wait_ge(sg("ms_ready"), NT * n + t + 1)
                    pool.tensor_tensor(rstd[:, t:t + 1], msq[:, t:t + 1], nhalf[:, 0:1], ALU.pow).then_inc(sg("rstd_ready"), 1)

            def rstd_pair(n):
                for t in range(NT):
                    for i in range(2):
                        pool.wait_ge(sg("ms_ready"), NT * n + 2 * t + i + 1)
                        pool.tensor_tensor(rstd[:, t:t + 1], msq[:, t:t + 1], nhalf[:, 0:1], ALU.pow).then_inc(sg("rstd_ready"), 1)

            rstd_of(0)
            pool.wait_ge(sg("bbar_ready"), 1)
            for b in range(NB):
                d, q = divmod(b, NB // 2)
                s = slice(SB * b, SB * (b + 1))
                pt = pd[:, :, 1:NPOW, s] if d == 0 else pw[:, :, 0:CH, s]
                if b >= 2:
                    pool.wait_ge(sg("wt_ready"), b - 1)
                for i, (bi, ti) in enumerate(((0, 1), (1, 0))):
                    pool.tensor_tensor(ptmp[b % 2][i][:, 0:SB * P].rearrange("p (g s i) -> p g s i", g=SB, s=CH),
                                       bbar[:, bi, s, :].unsqueeze(2).to_broadcast([P, SB, CH, GC]),
                                       pt[:, ti].rearrange("p s g -> p g s").unsqueeze(3).to_broadcast([P, SB, CH, GC]),
                                       MUL).then_inc(sg("wt_pool"), 1)
                if b >= NB - 8:
                    if b == NB - 8:
                        pool.wait_ge(sg("uc_tr"), 4)
                    z = b - (NB - 8)
                    pool.memset(xbd.rearrange("p r g a c -> p (r g a c)")[:, z * 1024:(z + 1) * 1024], 0.0).then_inc(sg("xbd_zero"), 1)
            for b in range(NB):
                d, q = divmod(b, NB // 2)
                s = slice(SB * b, SB * (b + 1))
                pt = pw[:, :, :, s] if d == 0 else pd[:, :, :, s]
                pool.wait_ge(sg("wt_ready"), NB - 1 + b) if b < 2 else pool.wait_ge(sg("v_ready"), b - 1)
                for i, (ci, ti) in enumerate(((0, 1), (1, 0))):
                    pool.tensor_tensor(ptmp[b % 2][i].rearrange("p (g s i) -> p g s i", g=SB, s=NPOW),
                                       cP[:, ci, s, :].unsqueeze(2).to_broadcast([P, SB, NPOW, GC]),
                                       pt[:, ti].rearrange("p s g -> p g s").unsqueeze(3).to_broadcast([P, SB, NPOW, GC]),
                                       MUL).then_inc(sg("v_pool"), 1)
            rstd_pair(1)
            rstd_pair(3)
            for t in range(NT):
                pool.wait_ge(sg("head_ms"), t + 1)
                hs = slice(t * QK, (t + 1) * QK)
                pool.tensor_tensor(hrs[:, hs], hms[:, hs], nhalf[:, hs], ALU.pow).then_inc(sg("head_rstd"), 1)
            pool.wait_ge(sg("oT_tr"), 4)
            link(pool.memset(upper[:, :], 1.0))
            link(pool.affine_select(out=upper[:, :], in_=upper[:, :], compare_op=ALU.is_gt, fill=0.0,
                                    base=0, pattern=[[1, P]], channel_multiplier=-1))
            link(pool.memset(ones[:, :], 1.0))
            link(pool.memset(lower_e[:, :, :], 1.0))
            link(pool.affine_select(out=lower_e[:, :, :], in_=lower_e[:, :, :], compare_op=ALU.is_gt, fill=0.0,
                                    base=0, pattern=[[1, EXP], [-1, EXP]], channel_multiplier=0))
            for v in (rank, chosen, gate):
                link(pool.memset(v[:, :, EXP:EXP + 1], 0.0))
            link(pool.iota(iota_i, pattern=[[1, SEQ]], base=0, channel_multiplier=0))
            pool.tensor_copy(iota[:, :], iota_i).then_inc(sg("route_consts"), 1)
            rstd_pair(5)
            pool.wait_ge(sg("x_stored"), 32)
            pool.wait_ge(sg("nat_ready"), 8)
            pool.wait_ge(sg("ssq_ready"), 14)
            pool.memset(acc[:, :, :], 0.0).then_inc(sg("acc_done"), 1)
            rstd_of(7)

        @block.scalar
        def _(act):
            step = [0]

            def link(ins):
                step[0] += 1
                ins.then_inc(sg("act_step"), 1)
                act.wait_ge(sg("act_step"), step[0])

            def nat_sq(t, src):
                return nat[:, t, :] if len(src.shape) == 2 else nat[:, t, :].rearrange("p (a b) -> p a b", a=2)

            def sum_squares(t, src):
                act.activation(nat_sq(t, src), src, ACT.Square, accum_out=ssq[:, t:t + 1]).then_inc(sg("ssq_ready"), 1)

            def norm_sums(n, bank):
                for t in range(NT):
                    act.wait_ge(sg("mix_done"), NT * n + t + 1)
                    sum_squares(t, ps[:, bank + 2 * t:bank + 2 * t + 2, :])
                    act.wait_ge(sg("x_done"), NT * n + t + 1)
                    sum_squares(t, x[:, t, :])

            def split(n):
                act.wait_ge(*item_full(n))
                if before_hi(n) is not None:
                    act.wait_ge(*item_read(before_hi(n)))
                act.activation(hi_lo(n)[0], raw(n), ACT.Copy).then_inc(sg("w_hi"), 1)

            def hT_hi(n, banks, gain):
                for b in (0, 2):
                    act.wait_ge(sg("tr_ready" if n < 3 else "oT_tr"), (4 * n if n < 3 else 0) + b + 1)
                    for k in (2 * b, 2 * b + 1):
                        ins = act.activation(hT_r[:, k, :], ps[:, banks[b], (k % 2) * SEQ:(k % 2 + 1) * SEQ], ACT.Copy,
                                             scale=1.0 if gain is None else gcol[:, gain * 8 + k:gain * 8 + k + 1])
                    ins.then_inc(sg("hT_hi"), 1)

            def hT_half(n, gain):
                for b in (0, 2):
                    act.wait_ge(sg("tr_ready"), 4 * n + b + 1)
                    for k in (2 * b, 2 * b + 1):
                        ins = act.activation(hT[:, k, :], ps[:, TR_BANKS[n][b], (k % 2) * SEQ:(k % 2 + 1) * SEQ], ACT.Copy,
                                             scale=1.0 if gain is None else gcol[:, gain * 8 + k:gain * 8 + k + 1])
                    ins.then_inc(sg("hT_ready"), 1)

            for t in range(NT):
                act.wait_ge(sg(f"x_in{t}"), 16)
                sum_squares(t, x[:, t, :])
            act.wait_ge(sg("gain_tr"), 1)
            act.activation(gcol[:, :], ps[:, 7, 0:64], ACT.Copy).then_inc(sg("gcol_ready"), 1)
            act.wait_ge(sg("lam_copied"), 1)
            act.activation(tmp(2), ps[:, 4, 128:192], ACT.Exp).then_inc(sg("step_ready"), 1)
            act.wait_ge(sg("ang_ready"), 1)
            act.activation(tmp(4), tmp(3), ACT.Exp).then_inc(sg("mag_ready"), 1)
            act.activation(tmp(7), tmp(5), ACT.Sin).then_inc(sg("mag_ready"), 1)
            act.activation(tmp(8), tmp(6), ACT.Sin).then_inc(sg("mag_ready"), 1)
            act.wait_ge(sg("gcol_ready"), 1)
            hT_half(0, 0)
            act.wait_ge(sg("pw_ready"), 1)
            for k in range(NPOW):
                ins = act.activation(pd[:, :, k, :], pw[:, :, CH - k, :], ACT.Copy)
            ins.then_inc(sg("pd_ready"), 1)
            for t in range(NT):
                act.wait_ge(sg("u_mm"), t + 1)
                act.activation(nat_sq(t, ps[:, 2 * t:2 * t + 2, :]), ps[:, 2 * t:2 * t + 2, :], ACT.Copy).then_inc(sg("u_act"), 1)
            for i in range(2):
                act.wait_ge(sg("bc_tr"), 2 * i + 2)
                for h in range(2):
                    act.activation(bP[:, i, :, 8 * h:8 * h + 8].rearrange("p g s -> p s g"),
                                   ps[:, 5 + h, :].rearrange("p (s g) -> p s g", g=DG), ACT.Copy).then_inc(sg("bc_out"), 1)
            for i in range(2):
                act.wait_ge(sg("bc_tr"), 4 + 2 * i + 2)
                for h in range(2):
                    act.activation(cP[:, i, :, 8 * h:8 * h + 8].rearrange("p g s -> p s g"),
                                   ps[:, 5 + h, :].rearrange("p (s g) -> p s g", g=DG), ACT.Copy).then_inc(sg("bc_out"), 1)
            act.wait_ge(sg("u_tok_in"), 16 * NT * CH)
            act.wait_ge(sg("bc_tr"), 8)
            act.activation(u_grp[0:NC, 0:GA].rearrange("p g s i -> p s g i"),
                           u_tok[0:NC, :, 0:GA * GC].rearrange("p s (g i) -> p s g i", i=GC), ACT.Copy).then_inc(sg("u_grp_ready"), 1)
            for b in range(4):
                act.wait_ge(sg("uc_tr"), b + 1)
                act.activation(uc[:, 16 * b:16 * b + 16, :].rearrange("p g c -> p (g c)"), ps[:, b, :], ACT.Copy).then_inc(sg("uc_ready"), 1)
            for b in range(NB):
                if b >= 2:
                    act.wait_ge(sg("s_mm"), b - 1)
                for h in range(2):
                    act.wait_ge(sg("w_tr"), 2 * b + h + 1)
                    act.activation(wm[b % 2][:, 2 * h:2 * h + 2, :, :].rearrange("p g r q -> p (g r q)"),
                                   ps[:, 2 * (b % 2) + h, :], ACT.Copy).then_inc(sg("w_out_act"), 1)
                if b >= 1:
                    act.wait_ge(sg("s_mm"), b)
                    act.activation(S_[:, :, SB * (b - 1):SB * b, :].rearrange("p r g c -> p r (g c)"),
                                   ps[:, 4 + (b - 1) % 2, 0:256].rearrange("p (r x) -> p r x", r=2), ACT.Copy).then_inc(sg("s_out"), 1)
            act.wait_ge(sg("s_mm"), NB)
            act.activation(S_[:, :, SB * (NB - 1):SB * NB, :].rearrange("p r g c -> p r (g c)"),
                           ps[:, 4 + (NB - 1) % 2, 0:256].rearrange("p (r x) -> p r x", r=2), ACT.Copy).then_inc(sg("s_out"), 1)
            def states_placed(d):
                g = slice(GP * d, GP * (d + 1))
                for r in range(2):
                    act.wait_ge(sg("x_nat"), 2 * d + r + 1)
                    for a in range(2):
                        h = slice(64 * a, 64 * a + 64)
                        act.activation(xbd[h, r, g, a, 1:NC], zz[h, r, g, 0:NC - 1], ACT.Copy).then_inc(sg("x_ready"), 1)

            act.wait_ge(sg("xbd_zero"), 8)
            states_placed(0)
            for b in range(NB):
                d, q = divmod(b, NB // 2)
                act.wait_ge(sg("k_mm"), b + 1)
                if d == 0:
                    ins = act.activation(kall[:, :, q, CH - 1:15, :],
                                         ps[:, 4 + 2 * (b % 2):6 + 2 * (b % 2), 0:P].rearrange("p a (t o) -> p a t o", o=GC), ACT.Copy)
                else:
                    ins = act.activation(kall[:, :, q, 0:CH - 1, :],
                                         ps[:, 4 + 2 * (b % 2):6 + 2 * (b % 2), 0:(CH - 1) * GC].rearrange("p a (t o) -> p a t o", o=GC), ACT.Copy)
                if d == 1:
                    ins = act.activation(kzero[:, :, q, :],
                                         ps[:, 4 + 2 * (b % 2):6 + 2 * (b % 2), (CH - 1) * GC:CH * GC], ACT.Copy)
                ins.then_inc(sg("k_out"), 1)
                if b == NB // 2 - 1:
                    states_placed(1)
            for b in range(5):
                if b < 4:
                    act.wait_ge(sg("y_sum"), b + 1)
                    act.activation(yg[:, 16 * b:16 * b + 16, :], yg[:, 16 * b:16 * b + 16, :], ACT.Gelu_apprx_tanh).then_inc(sg("gelu"), 1)
                if b >= 1:
                    for r in range(4 * (b - 1), 4 * b, 2):
                        act.wait_ge(sg("g_tr"), r + 1)
                        act.activation(g_tok[0:NC, :, 64 * r:64 * r + 64].rearrange("c t (g o) -> c g t o", o=GC),
                                       ps[0:NC, 4 + r % 4, :].rearrange("c (g t o) -> c g t o", g=4, t=CH), ACT.Copy).then_inc(sg("g_tok_act"), 1)
            for b in (0, 2):
                act.wait_ge(sg("gT_tr"), b + 1)
                act.activation(gT[:, 2 * b:2 * b + 2, :].rearrange("p k (c t) -> p k t c", t=CH),
                               ps[:, b, :].rearrange("p (k t c) -> p k t c", k=2, t=CH), ACT.Copy).then_inc(sg("gT_ready"), 1)
            for m in range(KD):
                act.wait_ge(sg("glu_mm"), m + 1)
                act.activation(sig[:, m, :], ps[:, 4 + m % 4, 0:SEQ], ACT.Sigmoid).then_inc(sg("sig_ready"), 1)
            for n in range(3):
                split(n)
            norm_sums(0, 0)
            hT_hi(1, TR_BANKS[1], 2)
            for c in range(2 * FF_STEPS):
                n = 3 * (c // 2 + 1)
                if c % 2 == 0 and n < ITEM_QKV:
                    split(n)
                act.wait_ge(sg("gu_done"), c + 1)
                if c >= 2:
                    act.wait_ge(sg("hid_ready"), c - 1)
                act.activation(sil[c % 2], ps[:, c % 2, 0:SEQ], ACT.Silu).then_inc(sg("sil_ready"), 1)
                if n < ITEM_QKV:
                    split(n + 1 + c % 2)
                elif c % 2 == 0:
                    split(ITEM_QKV)
                else:
                    for i in range(1, 4):
                        split(ITEM_QKV + i)
            norm_sums(1, 2)
            hT_hi(2, TR_BANKS[2], 4)
            for n in range(ITEM_QKV + 4, ITEM_MOE):
                split(n)
            act.wait_ge(sg("x_stored"), 16)
            for t in range(NT):
                act.wait_ge(sg("proj_done"), t + 1)
                if t == 1:
                    act.wait_ge(sg("head_sum"), 1)
                act.activation(head_sq, ps[:, 3 * t:3 * t + 3, :].rearrange("p b n -> p (b n)")[:, 0:QK * HD].rearrange("p (h d) -> p h d", d=HD),
                               ACT.Square).then_inc(sg("head_sq"), 1)
                act.activation(qkv[:, t, QK * HD:QKV], ps[:, 3 * t + 2, IW:2 * IW], ACT.Copy).then_inc(sg("v_ready_t"), 1)
            for b in (0, 2):
                act.wait_ge(sg("q_tr"), b + 1)
                act.activation(qT[:, 2 * b:2 * b + 2, :], ps[:, Q_BANKS[b], :].rearrange("p (k n) -> p k n", k=2), ACT.Copy).then_inc(sg("qT_ready"), 1)
            act.wait_ge(sg("k_tr"), 1)
            act.activation(kT[:, 0:2, :], ps[:, K_BANKS[0], :].rearrange("p (k n) -> p k n", k=2), ACT.Copy).then_inc(sg("qT_ready"), 1)
            for u in range(UNITS):
                act.wait_ge(sg("smax_ready"), u + 1)
                if u >= 2:
                    act.wait_ge(sg("p_tr"), u - 1)
                for h in range(2):
                    act.activation(prob[u % 2][:, h, :], ps[:, 2 * (u % 2) + h, 0:SEQ], ACT.Exp, bias=nmax[:, 2 * u + h:2 * u + h + 1],
                                   scale=HD ** -0.5, accum_out=psum_[:, 2 * u + h:2 * u + h + 1]).then_inc(sg("probs_ready"), 1)
            hT_hi(3, range(4), None)
            norm_sums(2, 4)
            hT_half(3, None)
            act.wait_ge(sg("logits_shifted"), 1)
            act.activation(wexp, lshift, ACT.Exp).then_inc(sg("logits_exp"), 1)
            act.wait_ge(sg("counts_ready"), 1)

            def gathered(e, other, count):
                for b in (0, 2):
                    act.wait_ge(sg("gather_mm"), 4 * e + b + 1)
                    ins = act.activation(xg[:, 2 * b:2 * b + 2, :], ps[:, b, :].rearrange("p (k n) -> p k n", k=2), ACT.Copy)
                    if b == 2:
                        ins.then_inc(sg("xg_ready"), 2)
                    else:
                        ins.then_inc(sg(other), count)

            def selection_transposed(e):
                act.wait_ge(sg("selg_tr"), e + 1)
                act.activation(sel_gT.rearrange("p a b n -> p (a b n)"), ps[:, 6, :], ACT.Copy).then_inc(sg("selgT_ready"), 1)

            def expert_narrow(e):
                gathered(e, "yT_ready", 4)
                for s in range(EX_STEPS + 1):
                    if s < EX_STEPS:
                        act.wait_ge(sg("moe_gu"), CHUNKS * e + 2 * s + 2)
                        if s >= 2:
                            act.wait_ge(sg("moe_hid"), CHUNKS * e + 2 * (s - 1))
                        act.activation(m_sil[s % 2], ps[:, s % 2, 0:SEQ], ACT.Silu).then_inc(sg("moe_sil"), 2)
                    if s >= 1:
                        act.wait_ge(sg("hid_tr"), EX_STEPS * e + s)
                        if s >= 3:
                            act.wait_ge(sg("moe_down"), CHUNKS * e + 2 * (s - 2))
                        act.activation(m_hidT[(s - 1) % 2], ps[:, 4 + (s - 1) % 2, 0:SEQ], ACT.Copy).then_inc(sg("hidT_ready"), 1)
                    if s == SEL_AT + 1:
                        selection_transposed(e)
                act.wait_ge(sg("moe_down"), CHUNKS * (e + 1))
                act.activation(y_lo[:, 0:512], ps[:, 2, :], ACT.Copy).then_inc(sg("y_ready"), 2)

            def expert_wide(e):
                gathered(e, "hidT_ready", EX_STEPS)
                for c in range(CHUNKS):
                    act.wait_ge(sg("moe_gu"), CHUNKS * e + c + 1)
                    if c >= 2:
                        act.wait_ge(sg("moe_hid"), CHUNKS * e + c - 1)
                    act.activation(m_sil[c % 2], ps[:, c % 2, 0:SEQ], ACT.Silu).then_inc(sg("moe_sil"), 1)
                    if c == SEL_AT + 4:
                        selection_transposed(e)
                act.wait_ge(sg("moe_down"), CHUNKS * (e + 1))
                for b in (0, 2):
                    act.activation(yT[:, 2 * b:2 * b + 2, :], ps[:, 2 + b, :].rearrange("p (k n) -> p k n", k=2), ACT.Copy).then_inc(sg("yT_ready"), 1)
                act.wait_ge(sg("y_tr"), 2 * e + 1)
                act.activation(y_lo[:, 0:512], ps[:, 6, :], ACT.Copy).then_inc(sg("y_ready"), 1)
                act.wait_ge(sg("y_tr"), 2 * e + 2)
                act.activation(y_hi[:, 0:512], ps[:, 0, :], ACT.Copy).then_inc(sg("y_ready"), 1)

            with act.Fori(0, EXP) as e:
                n = act.value_load(cnt_i[0:1, bass.ds(e, 1)], min_val=0, max_val=SEQ)
                with act.If(n > P):
                    expert_wide(e)
                with act.Else():
                    expert_narrow(e)
            act.wait_ge(sg("scatter_mm"), 4 * EXP)
            for t in range(NT):
                act.wait_ge(sg("acc_done"), 4 * EXP + 1)
                act.activation(hT.rearrange("p k n -> p (k n)")[:, t * D:(t + 1) * D], acc[:, t, :], ACT.Square,
                               accum_out=ssq[:, t:t + 1]).then_inc(sg("ssq_ready"), 1)

        @block.vector
        def _(dve):
            step = [0]

            def link(ins):
                step[0] += 1
                ins.then_inc(sg("dve_step"), 1)
                dve.wait_ge(sg("dve_step"), step[0])

            def tt(o, a, b, op):
                link(dve.tensor_tensor(o, a, b, op))

            def mean_square(n, t):
                dve.wait_ge(sg("ssq_ready"), n + 1)
                dve.tensor_scalar(msq[:, t:t + 1], ssq[:, t:t + 1], 1.0 / D, EPS, MUL, ADD).then_inc(sg("ms_ready"), 1)
                dve.wait_ge(sg("rstd_ready"), n + 1)

            def pre_norm(n, t, gain_row=None):
                mean_square(n, t)
                if gain_row is None:
                    dve.tensor_scalar(nat[:, t, :], x[:, t, :], rstd[:, t:t + 1], None, MUL).then_inc(sg("nat_ready"), 1)
                else:
                    dve.scalar_tensor_tensor(nat[:, t, :], x[:, t, :], rstd[:, t:t + 1], gain_row, MUL, MUL).then_inc(sg("nat_ready"), 1)

            def norms(n, bank, gain_row=None):
                for t in range(NT):
                    mean_square(NT + 2 * NT * n + 2 * t, t)
                    dve.wait_ge(sg("post_gain_in"), 16 * (n + 1))
                    link(dve.scalar_tensor_tensor(nat[:, t, :], ps[:, bank + 2 * t:bank + 2 * t + 2, :].rearrange("p a b -> p (a b)"),
                                                  rstd[:, t:t + 1], post_gain[:, :], MUL, MUL))
                    dve.tensor_tensor(x[:, t, :], x[:, t, :], nat[:, t, :], ADD).then_inc(sg("x_done"), 1)
                    dve.wait_ge(sg("x_done"), NT * n + t + 1)
                    pre_norm(NT + 2 * NT * n + 2 * t + 1, t, gain_row)

            def split(n):
                dve.wait_ge(sg("w_hi"), n + 1)
                dve.tensor_tensor(hi_lo(n)[1], raw(n), hi_lo(n)[0], SUB).then_inc(sg("w_lo"), 1)

            def hT_split(n, banks, gain):
                for b in (1, 3):
                    dve.wait_ge(sg("tr_ready" if n < 3 else "oT_tr"), (4 * n if n < 3 else 0) + b + 1)
                    for k in (2 * b, 2 * b + 1):
                        ins = dve.tensor_scalar(hT_r[:, k, :], ps[:, banks[b], (k % 2) * SEQ:(k % 2 + 1) * SEQ],
                                                1.0 if gain is None else gcol[:, gain * 8 + k:gain * 8 + k + 1], None, MUL)
                link(ins)
                for b in (0, 1, 2, 3):
                    if b % 2 == 0:
                        dve.wait_ge(sg("hT_hi"), 2 * (n - 1) + b // 2 + 1)
                    for k in (2 * b, 2 * b + 1):
                        ins = dve.scalar_tensor_tensor(HT_LO[n][:, k, :], ps[:, banks[b], (k % 2) * SEQ:(k % 2 + 1) * SEQ],
                                                       1.0 if gain is None else gcol[:, gain * 8 + k:gain * 8 + k + 1], hT_r[:, k, :], MUL, SUB)
                    ins.then_inc(sg("hT_ready"), 1)

            def hT_half(n, gain):
                for b in (1, 3):
                    dve.wait_ge(sg("tr_ready"), 4 * n + b + 1)
                    for k in (2 * b, 2 * b + 1):
                        ins = dve.tensor_scalar(hT[:, k, :], ps[:, TR_BANKS[n][b], (k % 2) * SEQ:(k % 2 + 1) * SEQ],
                                                1.0 if gain is None else gcol[:, gain * 8 + k:gain * 8 + k + 1], None, MUL)
                    ins.then_inc(sg("hT_ready"), 1)

            dve.wait_ge(sg("lam_in"), 48)
            dve.tensor_copy(raw_l[0:DG, 2, :].rearrange("g (a p) -> g a p", a=2),
                            raw_s[0:DG, :].unsqueeze(2).to_broadcast([DG, 2, ST])).then_inc(sg("lstep_spread"), 1)
            for t in range(NT):
                pre_norm(t, t)
            dve.wait_ge(sg("gain_in"), 32)
            dve.tensor_copy(raw_dx[0:GROUPS, :, :], raw_d[0:GROUPS, :].unsqueeze(1).to_broadcast([GROUPS, CH, GC])).then_inc(sg("d_spread"), 1)
            lr, li, st, ea, mag, rs, rc_, sn, cs = (tmp(i) for i in range(9))
            dve.wait_ge(sg("lam_tr"), 1)
            dve.tensor_copy(lr, ps[:, 4, 0:64])
            dve.tensor_copy(li, ps[:, 4, 64:128]).then_inc(sg("lam_copied"), 1)
            dve.wait_ge(sg("step_ready"), 1)
            tt(ea, lr, st, MUL)
            tt(rs, li, st, MUL)
            n_, t_ = tmp(9), tmp(10)
            MAGIC = 12582912.0
            link(dve.tensor_scalar(n_, rs, 0.15915494309189535, MAGIC, MUL, ADD))
            link(dve.tensor_scalar(n_, n_, -MAGIC, None, ADD))
            for c in (6.28125, 1.9350051879882812e-3, 3.019915981956753e-7):
                link(dve.scalar_tensor_tensor(rs, n_, -c, rs, MUL, ADD))
            PI = 3.1415925
            link(dve.tensor_scalar(rs, rs, PI, -PI, ALU.min, ALU.max))
            link(dve.tensor_scalar(t_, rs, -1.0, None, MUL))
            tt(t_, t_, rs, ALU.max)
            dve.tensor_scalar(rc_, t_, -1.0, 1.5707963267948966, MUL, ADD).then_inc(sg("ang_ready"), 1)
            dve.wait_ge(sg("gcol_ready"), 1)
            hT_half(0, 0)
            dve.wait_ge(sg("mag_ready"), 3)
            dve.memset(pw[:, 0, 0, :], 1.0)
            dve.memset(pw[:, 1, 0, :], 0.0)
            tt(pw[:, 0, 1, :], mag, cs, MUL)
            tt(pw[:, 1, 1, :], mag, sn, MUL)

            def cmul(o_re, o_im, a, b, t):
                dve.tensor_tensor(t[0], a[0], b[0], MUL)
                dve.tensor_tensor(t[1], a[1], b[1], MUL)
                dve.tensor_tensor(t[2], a[0], b[1], MUL)
                tt(t[3], a[1], b[0], MUL)
                dve.tensor_tensor(o_re, t[0], t[1], SUB)
                tt(o_im, t[2], t[3], ADD)

            q = tuple(tmp(n) for n in (11, 12, 9, 10))
            q1, q2 = q[0:2]
            cmul(pw[:, 0, 2, :], pw[:, 1, 2, :], (pw[:, 0, 1, :],) + (pw[:, 1, 1, :],), (pw[:, 0, 1, :], pw[:, 1, 1, :]), q)
            w = [m[:, 0:2 * DG].rearrange("p (k g) -> p k g", k=2) for m in mtmp]
            b2 = [pw[:, r, 2:3, :].to_broadcast([P, 2, DG]) for r in range(2)]
            cmul(pw[:, 0, 3:5, :], pw[:, 1, 3:5, :], (pw[:, 0, 1:3, :], pw[:, 1, 1:3, :]), b2, w)
            w = [m[:, 0:4 * DG].rearrange("p (k g) -> p k g", k=4) for m in mtmp]
            b4 = [pw[:, r, 4:5, :].to_broadcast([P, 4, DG]) for r in range(2)]
            cmul(pw[:, 0, 5:9, :], pw[:, 1, 5:9, :], (pw[:, 0, 1:5, :], pw[:, 1, 1:5, :]), b4, w)
            dve.memset(tmp(26), 0.0).then_inc(sg("pw_ready"), 1)
            den, nr, qr, qi = tmp(13), tmp(14), tmp(15), tmp(16)
            tt(q1, lr, lr, MUL)
            tt(q2, li, li, MUL)
            tt(den, q1, q2, ADD)
            link(dve.reciprocal(den, den))
            link(dve.tensor_scalar(nr, pw[:, 0, 1, :], -1.0, None, ADD))
            dve.tensor_tensor(q[0], nr, lr, MUL)
            dve.tensor_tensor(q[1], pw[:, 1, 1, :], li, MUL)
            dve.tensor_tensor(q[2], pw[:, 1, 1, :], lr, MUL)
            tt(q[3], nr, li, MUL)
            dve.tensor_tensor(q[0], q[0], q[1], ADD)
            tt(q[2], q[2], q[3], SUB)
            dve.tensor_tensor(qr, q[0], den, MUL)
            tt(qi, q[2], den, MUL)
            e1 = (tmp(17), tmp(18))
            cur = (cs, sn)
            for i in range(3):
                nxt = e1 if i % 2 == 0 else (tmp(19), tmp(20))
                cmul(nxt[0], nxt[1], cur, cur, q)
                tt(q1, nxt[0], nxt[0], MUL)
                tt(q2, nxt[1], nxt[1], MUL)
                tt(q1, q1, q2, ADD)
                link(dve.tensor_scalar(q1, q1, -0.5, 1.5, MUL, ADD))
                tt(nxt[0], nxt[0], q1, MUL)
                tt(nxt[1], nxt[1], q1, MUL)
                cur = nxt
            dve.wait_ge(sg("d_tr"), 1)
            link(dve.tensor_copy(dcol[:, :], ps[:, 7, 64:128]))
            link(dve.memset(ec[:, 0, :, 0:1], 1.0))
            link(dve.memset(ec[:, 1, :, 0:1], 0.0))
            n = 1
            while n < NC:
                bb = [v.unsqueeze(2).to_broadcast([P, DG, n]) for v in cur]
                t = [at(REZ + 4096 + 1024 * i, DG, n) for i in range(4)]
                cmul(ec[:, 0, :, n:2 * n], ec[:, 1, :, n:2 * n], (ec[:, 0, :, 0:n], ec[:, 1, :, 0:n]), bb, t)
                if 2 * n < NC:
                    nxt = (tmp(21), tmp(22)) if cur[0] is not None and n in (1, 4, 16) else (tmp(23), tmp(24))
                    cmul(nxt[0], nxt[1], cur, cur, q)
                    cur = nxt
                n *= 2
            dve.wait_ge(sg("u_tok_in"), 16 * NT * CH)
            dve.wait_ge(sg("bc_tr"), 8)
            for k in range(CH):
                ins = dve.tensor_copy(u_grp[0:NC, GA:, k, :], u_tok[0:NC, k, GA * GC:].rearrange("p (g i) -> p g i", i=GC))
            ins.then_inc(sg("u_grp_ready"), 1)
            dve.wait_ge(sg("bc_out"), 4)
            m1 = at(REZ + 4096, DG, GC)
            m2 = at(REZ + 4096 + 1024, DG, GC)
            qb = [v.unsqueeze(2).to_broadcast([P, DG, GC]) for v in (qr, qi)]
            tt(m1, bP[:, 0], qb[0], MUL)
            tt(m2, bP[:, 1], qb[1], MUL)
            tt(bbar[:, 0, 0:DG, :], m1, m2, SUB)
            tt(m1, bP[:, 1], qb[0], MUL)
            tt(m2, bP[:, 0], qb[1], MUL)
            dve.wait_ge(sg("bbar_pad"), 1)
            dve.wait_ge(sg("pd_ready"), 1)
            dve.tensor_tensor(bbar[:, 1, 0:DG, :], m1, m2, ADD).then_inc(sg("bbar_ready"), 1)
            dve.wait_ge(sg("bbar_ready"), 1)

            def build_wt(b):
                d = b // (NB // 2)
                s = slice(SB * b, SB * (b + 1))
                pt = pd[:, :, 1:NPOW, s] if d == 0 else pw[:, :, 0:CH, s]
                v4 = [m[:, 0:SB * P].rearrange("p (g s i) -> p g s i", g=SB, s=CH) for m in mtmp]
                for i in range(2):
                    ins = dve.tensor_tensor(v4[i], bbar[:, i, s, :].unsqueeze(2).to_broadcast([P, SB, CH, GC]),
                                            pt[:, i].rearrange("p s g -> p g s").unsqueeze(3).to_broadcast([P, SB, CH, GC]), MUL)
                link(ins)
                if b >= 2:
                    dve.wait_ge(sg("w_tr"), 2 * (b - 1))
                link(dve.tensor_tensor(wt[b % 2][:, 0].rearrange("p g x -> p (g x)"), mtmp[0][:, 0:SB * P], mtmp[1][:, 0:SB * P], SUB))
                dve.wait_ge(sg("wt_pool"), 2 * (b + 1))
                dve.tensor_tensor(wt[b % 2][:, 1].rearrange("p g x -> p (g x)"), ptmp[b % 2][0][:, 0:SB * P], ptmp[b % 2][1][:, 0:SB * P], ADD).then_inc(sg("wt_ready"), 1)

            for b in range(NB):
                build_wt(b)
            m2_, m4_, m8_ = tmp(21), tmp(22), tmp(25)
            tt(m2_, mag, mag, MUL)
            tt(m4_, m2_, m2_, MUL)
            tt(m8_, m4_, m4_, MUL)

            def chunk_scan(d, step):
                g = slice(GP * d, GP * (d + 1))
                z0, z1, t8 = zz[:, 0, g], zz[:, 1, g], tmp8[:, :]
                s0, s1, c0, c1 = S_[:, 0, g], S_[:, 1, g], ec[:, 0, g], ec[:, 1, g]
                if step == 0:
                    dve.wait_ge(sg("s_out"), NB // 2 * (d + 1))
                    dve.tensor_tensor(z0, s0, c0, MUL)
                    tt(t8, s1, c1, MUL)
                    tt(z0, z0, t8, ADD)
                elif step == 1:
                    dve.tensor_tensor(z1, s1, c0, MUL)
                    tt(t8, s0, c1, MUL)
                    tt(z1, z1, t8, SUB)
                elif step == 2:
                    link(dve.tensor_copy(r8t[:, :, :], m8_[:, g].unsqueeze(2).to_broadcast([P, GP, NC])))
                    link(dve.memset(r8t[:, :, 0:1], 0.0))
                elif step < 5:
                    r = step - 3
                    link(dve.tensor_tensor_scan(S_[:, r, g, :].rearrange("p g c -> p (g c)"), r8t[:, :, :].rearrange("p g c -> p (g c)"),
                                                zz[:, r, g, :].rearrange("p g c -> p (g c)"), 0.0, MUL, ADD))
                elif step == 5:
                    dve.tensor_tensor(z0, s0, c0, MUL)
                    tt(t8, s1, c1, MUL)
                elif step == 6:
                    dve.tensor_tensor(z0, z0, t8, SUB).then_inc(sg("x_nat"), 1)
                    dve.wait_ge(sg("x_nat"), 2 * d + 1)
                    dve.tensor_tensor(z1, s1, c0, MUL)
                    tt(t8, s0, c1, MUL)
                else:
                    dve.tensor_tensor(z1, z1, t8, ADD).then_inc(sg("x_nat"), 1)

            for step_ in range(8):
                chunk_scan(0, step_)
            def k_zero(hf):
                dve.wait_ge(sg("k_out"), NB // 2 + 4 * (hf + 1))
                v = kall[:, :, 4 * hf:4 * hf + 4, CH - 1, :]
                dve.tensor_tensor(v, v, kzero[:, :, 4 * hf:4 * hf + 4, :], ADD).then_inc(sg("k_final"), 1)

            for b in range(NB):
                d = b // (NB // 2)
                s = slice(SB * b, SB * (b + 1))
                pt = pw[:, :, :, s] if d == 0 else pd[:, :, :, s]
                v4 = [m.rearrange("p (g s i) -> p g s i", g=SB, s=NPOW) for m in mtmp]
                for i in range(2):
                    ins = dve.tensor_tensor(v4[i], cP[:, i, s, :].unsqueeze(2).to_broadcast([P, SB, NPOW, GC]),
                                            pt[:, i].rearrange("p s g -> p g s").unsqueeze(3).to_broadcast([P, SB, NPOW, GC]), MUL)
                link(ins)
                if b >= 2:
                    dve.wait_ge(sg("y_state"), b - 1)
                v = vv[b % 2]
                link(dve.tensor_tensor(v[:, 0].rearrange("p g s i -> p (g s i)"), mtmp[0], mtmp[1], SUB))
                dve.wait_ge(sg("v_pool"), 2 * (b + 1))
                dve.scalar_tensor_tensor(v[:, 1].rearrange("p g s i -> p (g s i)"), ptmp[b % 2][0], -1.0, ptmp[b % 2][1], MUL, SUB).then_inc(sg("v_ready"), 1)
                if b < 8:
                    chunk_scan(1, b)
                if b == 13:
                    k_zero(0)
            k_zero(1)
            dve.wait_ge(sg("y_state"), NB)
            tt(ud[:, :, :], uc[:, :, :], dcol[:, :].unsqueeze(2).to_broadcast([P, GROUPS, NC]), MUL)
            for b in range(5):
                if b < 4:
                    dve.wait_ge(sg("y_mm"), b + 1)
                    dve.tensor_tensor(yg[:, 16 * b:16 * b + 16, :].rearrange("p g c -> p (g c)"), ps[:, b, :],
                                      ud[:, 16 * b:16 * b + 16, :].rearrange("p g c -> p (g c)"), ADD).then_inc(sg("y_sum"), 1)
                if b >= 1:
                    for r in range(4 * (b - 1) + 1, 4 * b, 2):
                        dve.wait_ge(sg("g_tr"), r + 1)
                        dve.tensor_copy(g_tok[0:NC, :, 64 * r:64 * r + 64].rearrange("c t (g o) -> c g t o", o=GC),
                                        ps[0:NC, 4 + r % 4, :].rearrange("c (g t o) -> c g t o", g=4, t=CH)).then_inc(sg("g_tok_dve"), 1)
            for b in (1, 3):
                dve.wait_ge(sg("gT_tr"), b + 1)
                dve.tensor_copy(gT[:, 2 * b:2 * b + 2, :].rearrange("p k (c t) -> p k t c", t=CH),
                                ps[:, b, :].rearrange("p (k t c) -> p k t c", k=2, t=CH)).then_inc(sg("gT_ready"), 1)
            for m in range(KD):
                dve.wait_ge(sg("sig_ready"), m + 1)
                dve.tensor_tensor(mT[:, m, :], sig[:, m, :], gT[:, m, :], MUL).then_inc(sg("m_ready"), 1)
            for n in range(3):
                split(n)
            norms(0, 0)
            hT_split(1, TR_BANKS[1], 2)
            for c in range(2 * FF_STEPS):
                n = 3 * (c // 2 + 1)
                if c % 2 == 0 and n < ITEM_QKV:
                    split(n)
                dve.wait_ge(sg("sil_ready"), c + 1)
                if c >= 1:
                    dve.wait_ge(sg("hid_ready"), c)
                link(dve.tensor_tensor(hid_f, sil[c % 2], ps[:, c % 2, SEQ:2 * SEQ], MUL))
                if c >= 2:
                    dve.wait_ge(sg("down_done"), c - 1)
                link(dve.tensor_copy(hid_hi_r[c % 2], hid_f))
                dve.tensor_tensor(hid_lo[c % 2], hid_f, hid_hi_r[c % 2], SUB).then_inc(sg("hid_ready"), 1)
                if n < ITEM_QKV:
                    split(n + 1 + c % 2)
                elif c % 2 == 0:
                    split(ITEM_QKV)
                else:
                    for i in range(1, 4):
                        split(ITEM_QKV + i)
            norms(1, 2)
            hT_split(2, TR_BANKS[2], 4)
            for n in range(ITEM_QKV + 4, ITEM_MOE):
                split(n)
            dve.wait_ge(sg("rope_in"), 64)
            for w in range(2):
                for i, (cs_, par) in enumerate(((0, 0), (1, 1), (1, 0), (0, 1))):
                    ins = dve.tensor_tensor(rope_t[:, w, i], rope_raw[:, cs_],
                                            qk_gain[:, w, par::2].unsqueeze(1).to_broadcast([P, NT, HD // 2]), MUL)
            link(ins)
            def finish_heads(q):
                t, h0 = divmod(q, 2)
                dve.wait_ge(sg("probs_ready"), 8 * (q + 1))
                dve.wait_ge(sg("pv_done"), 4 * (q + 1))
                link(dve.reciprocal(prcp[:, 8 * q:8 * q + 8], psum_[:, 8 * q:8 * q + 8]))
                dve.tensor_tensor(o_nat[:, t, h0 * 512:(h0 + 1) * 512].rearrange("p (h d) -> p h d", d=HD),
                                  ps[:, 6 + q % 2, :].rearrange("p (h d) -> p h d", d=HD),
                                  prcp[:, 8 * q:8 * q + 8].unsqueeze(2).to_broadcast([P, 8, HD]), MUL).then_inc(sg("o_ready"), 1)

            dve.wait_ge(sg("x_stored"), 16)
            for t in range(NT):
                hs_ = slice(t * QK, (t + 1) * QK)
                dve.wait_ge(sg("head_sq"), t + 1)
                dve.tensor_reduce(hms[:, hs_], head_sq, AX.X, ADD).then_inc(sg("head_sum"), 1)
                dve.wait_ge(sg("head_sum"), t + 1)
                dve.tensor_scalar(hms[:, hs_], hms[:, hs_], 1.0 / HD, EPS, MUL, ADD).then_inc(sg("head_ms"), 1)
                dve.wait_ge(sg("head_rstd"), t + 1)
                dve.wait_ge(sg("v_ready_t"), t + 1)
                v = qkv[:, t, 0:QK * HD].rearrange("p (h d) -> p h d", d=HD)
                tt(v, ps[:, 3 * t:3 * t + 3, :].rearrange("p b n -> p (b n)")[:, 0:QK * HD].rearrange("p (h d) -> p h d", d=HD),
                   hrs[:, hs_].unsqueeze(2).to_broadcast([P, QK, HD]), MUL)
                for h0, nh in ((0, 8), (8, 8), (NH, NKV)):
                    hs = slice(h0, h0 + nh)
                    for i in range(4):
                        ins = dve.tensor_tensor(rope_m[i][:, 0:nh], v[:, hs, (i % 2)::2],
                                                rope_t[:, h0 // NH, i, t].unsqueeze(1).to_broadcast([P, nh, HD // 2]), MUL)
                    link(ins)
                    if h0 < NH:
                        dve.tensor_tensor(v[:, hs, 0::2], rope_m[0], rope_m[1], SUB)
                        link(dve.tensor_tensor(v[:, hs, 1::2], rope_m[2], rope_m[3], ADD))
                    else:
                        for c in range(2):
                            dve.tensor_tensor(k_dup[:, t, :, c, 0::2], rope_m[0][:, 0:nh], rope_m[1][:, 0:nh], SUB)
                            ins = dve.tensor_tensor(k_dup[:, t, :, c, 1::2], rope_m[2][:, 0:nh], rope_m[3][:, 0:nh], ADD)
                        ins.then_inc(sg("rope_done"), 1)
                        dve.wait_ge(sg("rope_done"), t + 1)
            for b in (1, 3):
                dve.wait_ge(sg("q_tr"), b + 1)
                dve.tensor_copy(qT[:, 2 * b:2 * b + 2, :], ps[:, Q_BANKS[b], :].rearrange("p (k n) -> p k n", k=2)).then_inc(sg("qT_ready"), 1)
            dve.wait_ge(sg("k_tr"), 2)
            dve.tensor_copy(kT[:, 2:4, :], ps[:, K_BANKS[1], :].rearrange("p (k n) -> p k n", k=2)).then_inc(sg("qT_ready"), 1)

            def score_max(u):
                dve.wait_ge(sg("scores_ready"), u + 1)
                link(dve.tensor_reduce(nmax[:, 2 * u:2 * u + 2], ps[:, 2 * (u % 2):2 * (u % 2) + 2, 0:SEQ], AX.X, ALU.max))
                dve.tensor_scalar(nmax[:, 2 * u:2 * u + 2], nmax[:, 2 * u:2 * u + 2], -HD ** -0.5, None, MUL).then_inc(sg("smax_ready"), 1)

            score_max(0)
            for u in range(UNITS):
                if u + 1 < UNITS:
                    score_max(u + 1)
                dve.wait_ge(sg("p_tr"), u + 1)
                if u >= 2:
                    dve.wait_ge(sg("pv_done"), u - 1)
                dve.tensor_copy(probT[u % 2], ps[:, 4 + u % 2, :].rearrange("p (a b n) -> p a b n", a=2, b=NT)).then_inc(sg("probT_ready"), 1)
                if u % 4 == 0 and u >= 4:
                    finish_heads(u // 4 - 1)
            finish_heads(UNITS // 4 - 1)
            hT_split(3, range(4), None)
            dve.wait_ge(sg("x_back"), 16)
            dve.wait_ge(sg("moe_gain_in"), 16)
            norms(2, 4, moe_gain)
            hT_half(3, None)
            dve.wait_ge(sg("route_consts"), 1)
            dve.wait_ge(sg("logits_mm"), 1)
            link(dve.tensor_copy(logit[:, :, :], ps[:, 4, 0:NT * EXP].rearrange("p (t e) -> p t e", t=NT)))
            link(dve.tensor_reduce(lmax, logit, AX.X, ALU.max))
            dve.tensor_tensor(lshift, logit, lmax.unsqueeze(2).to_broadcast([P, NT, EXP]), SUB).then_inc(sg("logits_shifted"), 1)
            lj = logit.unsqueeze(2).to_broadcast([P, NT, EXP, EXP])
            li_ = logit.unsqueeze(3).to_broadcast([P, NT, EXP, EXP])
            dve.tensor_tensor(gt_, lj, li_, ALU.is_gt)
            tt(eq_, lj, li_, ALU.is_equal)
            tt(eq_, eq_, lower_e.unsqueeze(1).to_broadcast([P, NT, EXP, EXP]), MUL)
            tt(gt_, gt_, eq_, ADD)
            link(dve.tensor_reduce(beats, gt_, AX.X, ADD))
            dve.tensor_scalar(chosen[:, :, 0:EXP], beats, 1.5, None, ALU.is_lt).then_inc(sg("chosen_ready"), 1)
            dve.wait_ge(sg("chosen_ready"), 1)
            dve.wait_ge(sg("logits_exp"), 1)
            tt(wexp, wexp, chosen[:, :, 0:EXP], MUL)
            link(dve.tensor_reduce(wsum, wexp, AX.X, ADD))
            link(dve.reciprocal(wsum, wsum))
            tt(gate[:, :, 0:EXP], wexp, wsum.unsqueeze(2).to_broadcast([P, NT, EXP]), MUL)
            dve.wait_ge(sg("rank_mm"), 1)
            link(dve.tensor_copy(rank[:, :, 0:EXP], ps[:, 5, 0:NT * EXP].rearrange("p (t e) -> p t e", t=NT)))
            dve.tensor_copy(cnt_i[0:1, :], ps[0:1, 6, 0:EXP]).then_inc(sg("counts_ready"), 1)

            def selection(dst, weight, e, sem):
                for t in range(NT):
                    dve.tensor_scalar(dst[:, t, :], iota[:, :], rank[:, t, bass.ds(e, 1)], weight[:, t, bass.ds(e, 1)],
                                      ALU.is_equal, MUL).then_inc(sg(sem), 1)

            selection(sel, chosen, 0, "sel_ready")
            dve.wait_ge(sg("counts_ready"), 1)

            def gathered(e):
                for b in (1, 3):
                    dve.wait_ge(sg("gather_mm"), 4 * e + b + 1)
                    dve.tensor_copy(xg[:, 2 * b:2 * b + 2, :], ps[:, b, :].rearrange("p (k n) -> p k n", k=2)).then_inc(sg("xg_ready"), 1)

            def add_scattered(e):
                for q in range(4):
                    dve.wait_ge(sg("scatter_mm"), 4 * e + q + 1)
                    if q == 0:
                        dve.wait_ge(sg("acc_done"), 4 * e + 1)
                    av = acc[:, :, q * SEQ:(q + 1) * SEQ]
                    dve.tensor_tensor(av, av, ps[:, 4 + q, :].rearrange("p (t n) -> p t n", t=NT), ADD).then_inc(sg("acc_done"), 1)

            def expert_narrow(e, T):
                M = P // T
                gathered(e)
                for s in range(EX_STEPS):
                    dve.wait_ge(sg("moe_sil"), CHUNKS * e + 2 * s + 2)
                    if s >= 2:
                        dve.wait_ge(sg("moe_down"), CHUNKS * e + 2 * (s - 1))
                    dve.tensor_tensor(m_hid[s % 2], m_sil[s % 2], ps[:, s % 2, SEQ:2 * SEQ], MUL).then_inc(sg("moe_hid"), 2)
                    if s == 0:
                        dve.wait_ge(sg("acc_done"), 4 * e + 1)
                        for t in range(NT):
                            dve.tensor_scalar(sel_g[:, t, 0:P].rearrange("p (r m) -> p r m", r=T),
                                              iota[:, 0:M].unsqueeze(1).to_broadcast([P, T, M]),
                                              rank[:, t, bass.ds(e, 1)], gate[:, t, bass.ds(e, 1)], ALU.is_equal, MUL).then_inc(sg("selg_ready"), 1)
                        selection(sel, chosen, e + 1, "sel_ready")
                dve.wait_ge(sg("moe_down"), CHUNKS * (e + 1))
                dve.tensor_copy(y_lo[:, 512:1024], ps[:, 3, :]).then_inc(sg("y_ready"), 2)
                add_scattered(e)

            def expert_wide(e):
                gathered(e)
                for c in range(CHUNKS):
                    dve.wait_ge(sg("moe_sil"), CHUNKS * e + c + 1)
                    if c >= 2:
                        dve.wait_ge(sg("moe_down"), CHUNKS * e + c - 1)
                    dve.tensor_tensor(m_hid[c % 2], m_sil[c % 2], ps[:, c % 2, SEQ:2 * SEQ], MUL).then_inc(sg("moe_hid"), 1)
                    if c == SEL_AT:
                        dve.wait_ge(sg("acc_done"), 4 * e + 1)
                        selection(sel_g, gate, e, "selg_ready")
                        selection(sel, chosen, e + 1, "sel_ready")
                dve.wait_ge(sg("moe_down"), CHUNKS * (e + 1))
                for b in (1, 3):
                    dve.tensor_copy(yT[:, 2 * b:2 * b + 2, :], ps[:, 2 + b, :].rearrange("p (k n) -> p k n", k=2)).then_inc(sg("yT_ready"), 1)
                dve.wait_ge(sg("y_tr"), 2 * e + 1)
                dve.tensor_copy(y_lo[:, 512:1024], ps[:, 7, :]).then_inc(sg("y_ready"), 1)
                dve.wait_ge(sg("y_tr"), 2 * e + 2)
                dve.tensor_copy(y_hi[:, 512:1024], ps[:, 1, :]).then_inc(sg("y_ready"), 1)
                add_scattered(e)

            with dve.Fori(0, EXP) as e:
                n = dve.value_load(cnt_i[0:1, bass.ds(e, 1)], min_val=0, max_val=SEQ)
                with dve.If(n > P // 2):
                    with dve.If(n > P):
                        expert_wide(e)
                    with dve.Else():
                        expert_narrow(e, 1)
                with dve.Else():
                    with dve.If(n > P // 4):
                        expert_narrow(e, 2)
                    with dve.Else():
                        expert_narrow(e, 4)
            dve.wait_ge(sg("last_gain_in"), 16)
            dve.wait_ge(sg("x_back"), 32)
            dve.wait_ge(sg("acc_done"), 4 * EXP + 1)
            for t in range(NT):
                mean_square(NT + 2 * NT * 3 + t, t)
                link(dve.scalar_tensor_tensor(acc[:, t, :], acc[:, t, :], rstd[:, t:t + 1], last_gain[:, :], MUL, MUL))
                dve.tensor_tensor(acc[:, t, :], acc[:, t, :], nat[:, t, :], ADD).then_inc(sg("y_final"), 1)

        @block.tensor
        def _(pe):
            def keep_warm(n, bank=7):
                for _ in range(n):
                    pe.matmul(ps[:, bank, :], ident[:, :], ident[:, :].unsqueeze(1).to_broadcast([P, 4, P]), start=True, stop=True)

            def matmul3(o, stationary, moving, start, stop):
                (ah, al), (bh, bl) = stationary, moving
                pe.matmul(o, ah, bh, start=start, stop=False)
                pe.matmul(o, ah, bl, start=False, stop=False)
                return pe.matmul(o, al, bh, start=False, stop=stop)

            def transposed_nat(n):
                for t in range(NT):
                    pe.wait_ge(sg("nat_ready"), NT * n + t + 1)
                    for k in range(KD):
                        m = pe.transpose(ps[:, TR_BANKS[n][k // 2], (k % 2) * SEQ + t * P:(k % 2) * SEQ + (t + 1) * P],
                                         nat[:, t, k * P:(k + 1) * P], ident[:, :])
                        if t == NT - 1 and k % 2 == 1:
                            m.then_inc(sg("tr_ready"), 1)

            id64 = ident[0:64, 0:64]
            pe.wait_ge(sg("ident_ready"), 1)
            pe.wait_ge(sg("lam_in"), 48)
            pe.wait_ge(sg("lstep_spread"), 1)
            for i in range(3):
                m = pe.transpose(ps[:, 4, 64 * i:64 * i + 64], raw_l[0:DG, i, :], id64)
            m.then_inc(sg("lam_tr"), 1)
            pe.wait_ge(sg("gain_in"), 32)
            pe.transpose(ps[:, 7, 0:64], raw_g[0:64, :], id64).then_inc(sg("gain_tr"), 1)
            pe.wait_ge(sg("d_spread"), 1)
            pe.wait_ge(sg("gcol_ready"), 1)
            pe.transpose(ps[:, 7, 64:128], raw_dx[0:GROUPS, :, :].rearrange("g t o -> g (t o)"), id64).then_inc(sg("d_tr"), 1)
            transposed_nat(0)
            pe.wait_ge(sg("hT_ready"), 4)
            for t in range(NT):
                for i in range(4):
                    if t == 0:
                        pe.wait_ge(sg(f"mix_w{i}"), 16)
                    for k in range(KD):
                        m = pe.matmul(ps[:, 2 * t + i // 2, (i % 2) * IW:(i % 2 + 1) * IW], hT[:, k, t * P:(t + 1) * P],
                                      w_in[:, i, k, :], start=k == 0, stop=k == KD - 1)
                m.then_inc(sg("u_mm"), 1)
            pe.wait_ge(sg("b_in"), 32)
            pe.wait_ge(sg("c_in"), 64)
            for r in range(4):
                if r >= 1:
                    pe.wait_ge(sg("bc_out"), 2 * r)
                for h in range(2):
                    for s in range(8):
                        src = raw_b[0:DG, r, :, 8 * h + s] if r < 2 else raw_c[0:DG, r - 2, 8 * h + s, :]
                        m = pe.transpose(ps[:, 5 + h, 64 * s:64 * s + 64], src, id64)
                    m.then_inc(sg("bc_tr"), 1)
            pe.wait_ge(sg("u_grp_ready"), 2)
            pe.wait_ge(sg("u_act"), 2)
            for b in range(4):
                for g in range(16 * b, 16 * b + 16):
                    m = pe.transpose(ps[:, b, (g % 16) * NC:(g % 16 + 1) * NC],
                                     u_grp[0:NC, g, :, :].rearrange("c s i -> c (s i)"), ident[0:NC, 0:NC])
                m.then_inc(sg("uc_tr"), 1)

            def w_transposes(b):
                pe.wait_ge(sg("wt_ready"), b + 1)
                if b >= 2:
                    pe.wait_ge(sg("w_out_act"), 2 * (b - 1))
                if b == 0:
                    pe.wait_ge(sg("uc_ready"), 4)
                for g in range(SB):
                    for r in range(2):
                        n = 2 * g + r
                        m = pe.transpose(ps[:, 2 * (b % 2) + n // 4, (n % 4) * P:(n % 4 + 1) * P], wt[b % 2][:, r, g, :], ident[:, :])
                    if g % 2 == 1:
                        m.then_inc(sg("w_tr"), 1)

            def s_matmuls(b):
                pe.wait_ge(sg("w_out_act"), 2 * (b + 1))
                if b >= 2:
                    pe.wait_ge(sg("s_out"), b - 1)
                d = b // (NB // 2)
                for g in range(SB):
                    gp = (SB * b + g) % GP
                    for a in range(2):
                        rhs = uc[:, 2 * gp + a, :] if d == 0 else uc[:, 2 * gp + a, ::-1]
                        for r in range(2):
                            m = pe.matmul(ps[64 * a:64 * a + 64, 4 + b % 2, r * P + g * NC:r * P + (g + 1) * NC],
                                          wm[b % 2][:, g, r, 64 * a:64 * a + 64], rhs, start=True, stop=True)
                m.then_inc(sg("s_mm"), 1)

            pe.wait_ge(sg("bc_out"), 8)
            keep_warm(5, 6)
            for b in range(NB):
                w_transposes(b)
                if b >= 1:
                    s_matmuls(b - 1)
            s_matmuls(NB - 1)
            pe.wait_ge(sg("s_out"), NB)
            for b in range(NB):
                d = b // (NB // 2)
                pe.wait_ge(sg("v_ready"), b + 1)
                v = vv[b % 2]
                if b >= 2:
                    pe.wait_ge(sg("k_out"), b - 1)
                k0 = 0 if d == 0 else 1
                if b == 8:
                    keep_warm(5, 4 + 2 * (b % 2))
                for r in range(2):
                    for g in range(SB):
                        dg = SB * b + g
                        for a in range(2):
                            m = pe.matmul(ps[32 * g:32 * g + 32, 4 + 2 * (b % 2) + a, 0:P],
                                          bbar[64 * a:64 * a + 64, r, dg:dg + 2, :].rearrange("p g i -> p (g i)"),
                                          v[64 * a:64 * a + 64, r, g, k0:k0 + CH, :].rearrange("p t o -> p (t o)"),
                                          start=r == 0, stop=r == 1)
                m.then_inc(sg("k_mm"), 1)
                y0 = 1 if d == 0 else 0
                pe.wait_ge(sg("x_ready"), 4 * (d + 1))
                for g in range(SB):
                    dg = SB * b + g
                    gp = dg % GP
                    for r in range(2):
                        rhs = xbd[:, r, dg, :, :] if d == 0 else xbd[:, r, dg, :, ::-1]
                        m = pe.matmul(ps[:, gp // 8, (gp % 8) * 64:(gp % 8 + 1) * 64],
                                      v[:, r, g, y0:y0 + CH, :].rearrange("p t o -> p (t o)"), rhs,
                                      start=(d == 0 and gp % 8 == 0 and r == 0), stop=False, skip_group_check=True)
                m.then_inc(sg("y_state"), 1)
            for b in range(5):
                if b < 4:
                    if b % 2 == 0:
                        if b == 0:
                            pe.wait_ge(sg("k_out"), NB - 1)
                            keep_warm(3, 4)
                        pe.wait_ge(sg(f"toe_in{b // 2}"), 16 * CH)
                    for g in range(16 * b, 16 * b + 16):
                        m = pe.matmul(ps[:, b, (g % 16) * NC:(g % 16 + 1) * NC], toe[g // 32][:, g % 32, :], uc[:, g, :],
                                      start=False, stop=True, skip_group_check=True)
                    m.then_inc(sg("y_mm"), 1)
                if b >= 1:
                    pe.wait_ge(sg("gelu"), b)
                    for r in range(4 * (b - 1), 4 * b):
                        if r >= 4:
                            pe.wait_ge(sg("g_tok_act" if r % 2 == 0 else "g_tok_dve"), (r - 4) // 2 + 1)
                        for g in range(4 * r, 4 * r + 4):
                            m = pe.transpose(ps[0:NC, 4 + r % 4, (g % 4) * P:(g % 4 + 1) * P], yg[:, g, :], ident[:, :])
                        m.then_inc(sg("g_tr"), 1)
            pe.wait_ge(sg("g_tok_act"), 8)
            pe.wait_ge(sg("g_tok_dve"), 8)
            for b in range(4):
                for k in (2 * b, 2 * b + 1):
                    for t in range(CH):
                        m = pe.transpose(ps[:, b, (k % 2) * SEQ + t * NC:(k % 2) * SEQ + (t + 1) * NC],
                                         g_tok[0:NC, t, k * P:(k + 1) * P], ident[0:NC, 0:NC])
                m.then_inc(sg("gT_tr"), 1)
            pe.wait_ge(sg("gT_ready"), 4)
            for m_ in range(KD):
                if m_ % 2 == 0:
                    pe.wait_ge(*((sg(f"mix_w{m_ // 2}"), 32) if m_ < 6 else (sg("glu_w3"), 16)))
                if m_ >= 4:
                    pe.wait_ge(sg("m_ready"), m_ - 3)
                for k in range(KD):
                    m = pe.matmul(ps[:, 4 + m_ % 4, 0:SEQ], w_glu[:, m_ // 2, k, (m_ % 2) * P:(m_ % 2 + 1) * P],
                                  gT[:, k, :], start=k == 0, stop=k == KD - 1)
                m.then_inc(sg("glu_mm"), 1)
            pe.wait_ge(sg("m_ready"), 8)
            for t in range(NT):
                for i in range(4):
                    if t == 0:
                        pe.wait_ge(sg(f"mix_w{i}"), 48 if i < 3 else 32)
                    for k in range(KD):
                        m = pe.matmul(ps[:, 2 * t + i // 2, (i % 2) * IW:(i % 2 + 1) * IW], mT[:, k, t * P:(t + 1) * P],
                                      w_out0[:, i, k, :], start=k == 0, stop=k == KD - 1)
                m.then_inc(sg("mix_done"), 1)
            transposed_nat(1)
            pe.wait_ge(sg("hT_ready"), 8)

            def ffn_down(c):
                n = 3 * (c // 2) + 2
                pe.wait_ge(sg("w_lo"), n + 1)
                pe.wait_ge(sg("hid_ready"), c + 1)
                for t in range(NT):
                    for h in range(2):
                        m = matmul3(ps[:, 2 + 2 * t + h, :], [v[:, t * P:(t + 1) * P] for v in (hid_hi_r[c % 2], hid_lo[c % 2])],
                                    [v[:, c % 2, h * 512:(h + 1) * 512] for v in hi_lo(n)], c == 0, c == 2 * FF_STEPS - 1)
                    if c == 2 * FF_STEPS - 1:
                        m.then_inc(sg("mix_done"), 1)
                if c < 2 * FF_STEPS - 1:
                    m.then_inc(sg("down_done"), 1)

            for c in range(2 * FF_STEPS):
                if c >= 2:
                    pe.wait_ge(sg("hid_ready"), c - 1)
                for i in range(2):
                    n = 3 * (c // 2) + i
                    pe.wait_ge(sg("w_lo"), n + 1)
                    for k in range(KD):
                        m = matmul3(ps[:, c % 2, i * SEQ:(i + 1) * SEQ], [v[:, k, (c % 2) * P:(c % 2 + 1) * P] for v in hi_lo(n)],
                                    [v[:, k, :] for v in (hT_r, HT_LO[1])], k == 0, k == KD - 1)
                m.then_inc(sg("gu_done"), 1)
                if c >= 1:
                    ffn_down(c - 1)
            ffn_down(2 * FF_STEPS - 1)
            transposed_nat(2)
            pe.wait_ge(sg("hT_ready"), 12)
            for t in range(NT):
                for i in range(QKV // IW):
                    pe.wait_ge(sg("w_lo"), ITEM_QKV + i + 1)
                    for k in range(KD):
                        m = matmul3(ps[:, 3 * t + i // 2, (i % 2) * IW:(i % 2 + 1) * IW],
                                    [v[:, k, t * P:(t + 1) * P] for v in (hT_r, HT_LO[2])],
                                    [v[:, k, :] for v in hi_lo(ITEM_QKV + i)], k == 0, k == KD - 1)
                m.then_inc(sg("proj_done"), 1)
            for t in range(NT):
                if t == NT - 1:
                    keep_warm(15)
                pe.wait_ge(sg("rope_done"), t + 1)
                for k in range(KD):
                    m = pe.transpose(ps[:, Q_BANKS[k // 2], (k % 2) * SEQ + t * P:(k % 2) * SEQ + (t + 1) * P],
                                     qkv[:, t, k * P:(k + 1) * P], ident[:, :])
                    if t == NT - 1 and k % 2 == 1:
                        m.then_inc(sg("q_tr"), 1)
            for b in range(2):
                for k in (2 * b, 2 * b + 1):
                    for t in range(NT):
                        m = pe.transpose(ps[:, K_BANKS[b], (k % 2) * SEQ + t * P:(k % 2) * SEQ + (t + 1) * P],
                                         k_dup[:, t, k].rearrange("p c d -> p (c d)"), ident[:, :])
                m.then_inc(sg("k_tr"), 1)
            pe.wait_ge(sg("qT_ready"), 6)

            def scores(u):
                t, hp = divmod(u, NH // 2)
                if u >= 2:
                    pe.wait_ge(sg("probs_ready"), 2 * (u - 1))
                for h in range(2):
                    m = pe.matmul(ps[:, 2 * (u % 2) + h, 0:SEQ], qT[64 * h:64 * h + 64, hp, t * P:(t + 1) * P],
                                  kT[64 * h:64 * h + 64, 2 * hp // HPK, :], start=True, stop=True)
                m.then_inc(sg("scores_ready"), 1)

            def prob_transposes(u):
                pe.wait_ge(sg("probs_ready"), 2 * (u + 1))
                if u >= 2:
                    pe.wait_ge(sg("probT_ready"), u - 1)
                for h in range(2):
                    for c in range(NT):
                        m = pe.transpose(ps[:, 4 + u % 2, (2 * h + c) * P:(2 * h + c + 1) * P], prob[u % 2][:, h, c * P:(c + 1) * P], ident[:, :])
                m.then_inc(sg("p_tr"), 1)

            def prob_values(u):
                t, hp = divmod(u, NH // 2)
                pe.wait_ge(sg("probT_ready"), u + 1)
                if u % 4 == 0 and u >= 8:
                    pe.wait_ge(sg("o_ready"), u // 4 - 1)
                kv = 2 * hp // HPK
                for h in range(2):
                    for c in range(NT):
                        m = pe.matmul(ps[:, 6 + (u // 4) % 2, (2 * (u % 4) + h) * HD:(2 * (u % 4) + h + 1) * HD], probT[u % 2][:, h, c, :],
                                      qkv[:, c, (QK + kv) * HD:(QK + kv + 1) * HD], start=c == 0, stop=c == NT - 1)
                m.then_inc(sg("pv_done"), 1)

            for u in range(UNITS + 2):
                if u < UNITS:
                    scores(u)
                if 1 <= u <= UNITS:
                    prob_transposes(u - 1)
                if u >= 2:
                    prob_values(u - 2)
            pe.wait_ge(sg("o_ready"), 4)
            for b in range(4):
                for k in (2 * b, 2 * b + 1):
                    for t in range(NT):
                        m = pe.transpose(ps[:, b, (k % 2) * SEQ + t * P:(k % 2) * SEQ + (t + 1) * P],
                                         o_nat[:, t, k * P:(k + 1) * P], ident[:, :])
                m.then_inc(sg("oT_tr"), 1)
            pe.wait_ge(sg("hT_ready"), 16)
            for t in range(NT):
                for i in range(D // IW):
                    pe.wait_ge(sg("w_lo"), ITEM_WO + i + 1)
                    for k in range(KD):
                        m = matmul3(ps[:, 4 + 2 * t + i // 2, (i % 2) * IW:(i % 2 + 1) * IW],
                                    [v[:, k, t * P:(t + 1) * P] for v in (hT_r, HT_LO[3])],
                                    [v[:, k, :] for v in hi_lo(ITEM_WO + i)], k == 0, k == KD - 1)
                m.then_inc(sg("mix_done"), 1)
            transposed_nat(3)
            pe.wait_ge(sg("hT_ready"), 20)
            pe.wait_ge(sg("router_in"), 16)
            for t in range(NT):
                for k in range(KD):
                    m = pe.matmul(ps[:, 4, t * EXP:(t + 1) * EXP], hT[:, k, t * P:(t + 1) * P], w_router[:, k, :],
                                  start=k == 0, stop=k == KD - 1)
            m.then_inc(sg("logits_mm"), 1)
            pe.wait_ge(sg("chosen_ready"), 1)
            pe.matmul(ps[:, 5, 0:EXP], upper[:, :], chosen[:, 0, 0:EXP], start=True, stop=True)
            pe.matmul(ps[:, 5, EXP:2 * EXP], ones[:, :], chosen[:, 0, 0:EXP], start=True, stop=False)
            pe.matmul(ps[:, 5, EXP:2 * EXP], upper[:, :], chosen[:, 1, 0:EXP], start=False, stop=True)
            for t in range(NT):
                m = pe.matmul(ps[0:1, 6, 0:EXP], ones[:, 0:1], chosen[:, t, 0:EXP], start=t == 0, stop=t == NT - 1)
            m.then_inc(sg("rank_mm"), 1)
            pe.wait_ge(sg("counts_ready"), 1)

            def gather(e, V):
                pe.wait_ge(sg("sel_ready"), NT * (e + 1))
                for b in range(4):
                    for k in (2 * b, 2 * b + 1):
                        for t in range(NT):
                            m = pe.matmul(ps[:, b, (k % 2) * SEQ:(k % 2) * SEQ + V], h_moe[:, t, k * P:(k + 1) * P],
                                          sel[:, t, 0:V], start=t == 0, stop=t == NT - 1)
                    m.then_inc(sg("gather_mm"), 1)
                pe.wait_ge(sg("xg_ready"), 4 * (e + 1))

            def expert_narrow(e, T):
                M, w = P // T, IW // T
                part = [0, 2, 1, 3] if T == 4 else list(range(T))
                gather(e, M)

                def transposes(s):
                    pe.wait_ge(sg("moe_hid"), CHUNKS * e + 2 * s + 2)
                    if s == 0:
                        pe.wait_ge(sg("acc_done"), 4 * e + 1)
                    if T == 1:
                        for f in range(2):
                            m = pe.transpose(ps[:, 4 + s % 2, f * P:(f + 1) * P], m_hid[s % 2][:, f * P:(f + 1) * P], ident[:, :])
                    elif T == 2:
                        m = pe.transpose(ps[:, 4 + s % 2, 0:P], m_hid[s % 2][:, 0:P], ident[:, :])
                    else:
                        for a in range(2):
                            m = pe.matmul(ps[64 * a:64 * a + 64, 4 + s % 2, 0:64], m_hid[s % 2][:, 0:64], ident[:, 64 * a:64 * a + 64],
                                          start=True, stop=True)
                    m.then_inc(sg("hid_tr"), 1)

                def down(s):
                    pe.wait_ge(*moe_item_full(e, 3 * s + 2))
                    pe.wait_ge(sg("hidT_ready"), EX_STEPS * e + s + 1)
                    dn = slot_down(3 * s + 2)
                    n = min(D // T, 512)
                    for f in range(2):
                        for j in range(max(T, 2)):
                            o = ps[M * j:M * j + M, 2, 0:n] if T > 1 else ps[:, 2 + j, :]
                            m = pe.matmul(o, m_hidT[s % 2][:, f * M:(f + 1) * M], dn[:, f, j * n:(j + 1) * n],
                                          start=s == 0 and f == 0, stop=s == EX_STEPS - 1 and f == 1)
                    m.then_inc(sg("moe_down"), 2)

                for s in range(EX_STEPS):
                    if s >= 2:
                        pe.wait_ge(sg("moe_hid"), CHUNKS * e + 2 * (s - 1))
                    for i in range(2):
                        pe.wait_ge(*moe_item_full(e, 3 * s + i))
                    gu = at(((3 * s) % SLOTS) * ITEM, 2, KD, IW)
                    for k in range(KD):
                        for j in range(T):
                            o = ps[M * j:M * j + M, s % 2, :].rearrange("p (i n) -> p i n", i=2)[:, :, 0:w]
                            m = pe.matmul(o, xg[:, k, 0:M], gu[:, :, k, part[j] * w:(part[j] + 1) * w], start=k == 0, stop=k == KD - 1)
                    m.then_inc(sg("moe_gu"), 2)
                    if s >= 1:
                        transposes(s - 1)
                    if s >= 2:
                        down(s - 2)
                    if s == SEL_AT:
                        pe.wait_ge(sg("selg_ready"), NT * (e + 1))
                        for t in range(NT):
                            m = pe.transpose(ps[:, 6, t * P:(t + 1) * P], sel_g[:, t, 0:P], ident[:, :])
                            if t == 0:
                                m.then_inc(sg("y_tr"), 2)
                        m.then_inc(sg("selg_tr"), 1)
                transposes(EX_STEPS - 1)
                down(EX_STEPS - 2)
                down(EX_STEPS - 1)
                pe.wait_ge(sg("selgT_ready"), e + 1)
                pe.wait_ge(sg("y_ready"), 4 * (e + 1))
                for q in range(4):
                    j = q * T // 4
                    y0 = (q - j * 4 // T) * SEQ
                    for t in range(NT):
                        m = pe.matmul(ps[:, 4 + q, t * SEQ:(t + 1) * SEQ], sel_gT[M * j:M * j + M, 0, t, :],
                                      y_lo[M * j:M * j + M, y0:y0 + SEQ], start=True, stop=True)
                    m.then_inc(sg("scatter_mm"), 1)

            def expert_wide(e, V):
                gather(e, V)

                def down(c):
                    n = 3 * (c // 2) + 2
                    pe.wait_ge(*moe_item_full(e, n))
                    pe.wait_ge(sg("moe_hid"), CHUNKS * e + c + 1)
                    if c == 0:
                        pe.wait_ge(sg("acc_done"), 4 * e + 1)
                    for k in range(KD):
                        m = pe.matmul(ps[:, 2 + k // 2, (k % 2) * SEQ:(k % 2) * SEQ + V], slot_down(n)[:, c % 2, k * P:(k + 1) * P],
                                      m_hid[c % 2][:, 0:V], start=(c == 0 and k % 2 == 0), stop=c == CHUNKS - 1, skip_group_check=True)
                    m.then_inc(sg("moe_down"), 1)

                for c in range(CHUNKS):
                    if c >= 2:
                        pe.wait_ge(sg("moe_hid"), CHUNKS * e + c - 1)
                    for i in range(2):
                        n = 3 * (c // 2) + i
                        pe.wait_ge(*moe_item_full(e, n))
                        for k in range(KD):
                            m = pe.matmul(ps[:, c % 2, i * SEQ:i * SEQ + V], slot(n)[:, k, (c % 2) * P:(c % 2 + 1) * P],
                                          xg[:, k, 0:V], start=k == 0, stop=k == KD - 1)
                    m.then_inc(sg("moe_gu"), 1)
                    if c >= 1:
                        down(c - 1)
                    if c == SEL_AT + 3:
                        pe.wait_ge(sg("selg_ready"), NT * (e + 1))
                        for ct in range(NT):
                            for t in range(NT):
                                m = pe.transpose(ps[:, 6, (NT * ct + t) * P:(NT * ct + t + 1) * P], sel_g[:, t, ct * P:(ct + 1) * P], ident[:, :])
                                if ct == 0 and t == 0:
                                    m.then_inc(sg("hid_tr"), EX_STEPS)
                        m.then_inc(sg("selg_tr"), 1)
                down(CHUNKS - 1)
                pe.wait_ge(sg("yT_ready"), 4 * (e + 1))
                for ct in range(2):
                    for k in range(KD):
                        m = pe.transpose(ps[:, (6 if ct == 0 else 0) + k // 4, (k % 4) * P:(k % 4 + 1) * P],
                                         yT[:, k, ct * P:(ct + 1) * P], ident[:, :])
                    m.then_inc(sg("y_tr"), 1)
                pe.wait_ge(sg("selgT_ready"), e + 1)
                pe.wait_ge(sg("y_ready"), 4 * (e + 1))
                for q in range(4):
                    for t in range(NT):
                        for ct in range(2):
                            kk = min(V - ct * P, P)
                            m = pe.matmul(ps[:, 4 + q, t * SEQ:(t + 1) * SEQ], sel_gT[0:kk, ct, t, :],
                                          (y_lo if ct == 0 else y_hi)[0:kk, q * SEQ:(q + 1) * SEQ], start=ct == 0, stop=ct == 1)
                    m.then_inc(sg("scatter_mm"), 1)

            with pe.Fori(0, EXP) as e:
                n = pe.value_load(cnt_i[0:1, bass.ds(e, 1)], min_val=0, max_val=SEQ)
                with pe.If(n > P // 2):
                    with pe.If(n > P):
                        with pe.If(n > WIDE[0]):
                            with pe.If(n > WIDE[1]):
                                expert_wide(e, WIDE[2])
                            with pe.Else():
                                expert_wide(e, WIDE[1])
                        with pe.Else():
                            expert_wide(e, WIDE[0])
                    with pe.Else():
                        expert_narrow(e, 1)
                with pe.Else():
                    with pe.If(n > P // 4):
                        expert_narrow(e, 2)
                    with pe.Else():
                        expert_narrow(e, 4)
            pe.wait_ge(sg("sel_ready"), NT * (EXP + 1))


_INS = ("x", "norm_gains", "ssm_w_in", "ssm_lambda_re", "ssm_lambda_im", "ssm_log_step", "ssm_b_re", "ssm_b_im",
        "ssm_c_re", "ssm_c_im", "ssm_d", "ssm_w_glu", "ssm_w_out", "ffn_w_gate", "ffn_w_up", "ffn_w_down",
        "attn_w_qkv", "attn_q_gain", "attn_k_gain", "attn_w_out", "moe_w_router", "moe_w_gate", "moe_w_up",
        "moe_w_down")


def rope_tables(seq, axis_dim, grid_w=64, theta=10000.0):
    import numpy as np
    freqs = np.float32(theta) ** (-np.arange(0, axis_dim, 2, dtype=np.float32) / np.float32(axis_dim))
    token = np.arange(seq)
    ang = np.concatenate([(token // grid_w).astype(np.float32)[:, None] * freqs,
                          (token % grid_w).astype(np.float32)[:, None] * freqs], axis=1).astype(np.float32)
    return np.cos(ang).astype(np.float32), np.sin(ang).astype(np.float32)


def build(nc, inputs):
    import numpy as np
    arrays = {f"in_{n}": np.ascontiguousarray(inputs[n]) for n in _INS}
    seq, head = arrays["in_x"].shape[1], arrays["in_attn_q_gain"].shape[1]
    arrays["rope_cos"], arrays["rope_sin"] = rope_tables(seq, head // 2)
    args = [nc.dram_tensor(n, a.shape, mybir.dt.from_np(a.dtype), kind="ExternalInput").ap() for n, a in arrays.items()]
    out = nc.dram_tensor("out", arrays["in_x"].shape, mybir.dt.float32, kind="ExternalOutput").ap()
    hybrid_trunk(nc, *args, out)
    return arrays, out


def kernel(**inputs):
    import concourse.bacc as bacc
    from concourse.bass_utils import run_bass_kernel_spmd
    nc = bacc.Bacc("TRN2", target_bir_lowering=False, num_devices=1)
    arrays, _ = build(nc, inputs)
    return run_bass_kernel_spmd(nc, [arrays], core_ids=[0]).results[0]["out"]
```
